# Optimizing a Trainium2 kernel written in Bass

```python
import jax, jax.numpy as jnp
from jax import lax
import numpy as np

D_MODEL = 1024
BATCH = 1
SEQ = 512
DEPTH = 1

CHUNK = 64
A_HEADS = D_MODEL // 128
A_HEAD_DIM = 64
A_LEFT_CHUNKS = 8
A_BAND = A_LEFT_CHUNKS + 1
A_MAX_REL = 128
B_HEADS = D_MODEL // 128
B_Q_LORA = D_MODEL // 4
B_KV_LORA = D_MODEL // 8
B_NOPE = 64
B_ROPE = 32
B_V_DIM = 64
B_QK_DIM = B_NOPE + B_ROPE
ROPE_THETA = 10000.0
Q_BLOCK = 128
A_WIDTH = A_HEADS * A_HEAD_DIM
B_WIDTH = B_HEADS * B_V_DIM
D_MIX = A_WIDTH + B_WIDTH
IN_COLS = 3 * A_WIDTH + B_Q_LORA + B_KV_LORA + B_ROPE
D_FF = ((8 * D_MODEL // 3 + 127) // 128) * 128
EPS = 1e-6
NEG_INF = -1e30


def rmsnorm(x, g):
    xf = x.astype(jnp.float32)
    y = xf * lax.rsqrt(jnp.mean(xf * xf, axis=-1, keepdims=True) + EPS)
    return (y * g.astype(jnp.float32)).astype(x.dtype)

def swiglu(h, w_gate, w_up, w_down):
    return (jax.nn.silu(h @ w_gate) * (h @ w_up)) @ w_down

def rope_tables(seq, dim):
    inv = 1.0 / (ROPE_THETA ** (jnp.arange(0, dim, 2, dtype=jnp.float32) / dim))
    ang = jnp.arange(seq, dtype=jnp.float32)[:, None] * inv[None, :]
    return jnp.cos(ang), jnp.sin(ang)

def apply_rope(x, cos, sin):
    x1, x2 = jnp.split(x, 2, axis=-1)
    c = cos[None, :, None, :].astype(x.dtype)
    s = sin[None, :, None, :].astype(x.dtype)
    return jnp.concatenate([x1 * c - x2 * s, x1 * s + x2 * c], axis=-1)

def chunked_relbias_attention(q, k, v, rel_bias):
    b, s, h, dh = q.shape
    nc = s // CHUNK
    band_len = A_BAND * CHUNK
    pad = ((0, 0), (A_LEFT_CHUNKS * CHUNK, 0), (0, 0), (0, 0))
    kp = jnp.pad(k, pad)
    vp = jnp.pad(v, pad)
    qc = q.reshape(b, nc, CHUNK, h, dh).transpose(1, 0, 2, 3, 4)
    qi = jnp.arange(CHUNK)
    kj = jnp.arange(band_len) - A_LEFT_CHUNKS * CHUNK
    rel = jnp.clip(qi[:, None] - kj[None, :], -A_MAX_REL, A_MAX_REL) + A_MAX_REL
    bias = rel_bias.astype(jnp.float32)[:, rel]
    scale = dh ** -0.5

    def one_chunk(args):
        q_blk, c = args
        kb = lax.dynamic_slice_in_dim(kp, c * CHUNK, band_len, axis=1)
        vb = lax.dynamic_slice_in_dim(vp, c * CHUNK, band_len, axis=1)
        sc = jnp.einsum('bihd,bjhd->bhij', q_blk, kb).astype(jnp.float32) * scale
        sc = sc + bias[None]
        valid = jnp.arange(band_len) >= (A_LEFT_CHUNKS - c) * CHUNK
        sc = jnp.where(valid[None, None, None, :], sc, NEG_INF)
        p = jax.nn.softmax(sc, axis=-1).astype(vb.dtype)
        return jnp.einsum('bhij,bjhd->bihd', p, vb)

    o = lax.map(one_chunk, (qc, jnp.arange(nc, dtype=jnp.int32)))
    return o.transpose(1, 0, 2, 3, 4).reshape(b, s, h * dh)

def block_causal_attention(q, k, v):
    b, s, h, dq = q.shape
    dv = v.shape[-1]
    nb = s // Q_BLOCK
    qb = q.reshape(b, nb, Q_BLOCK, h, dq).transpose(1, 0, 2, 3, 4)
    k_chunk = jnp.arange(s) // CHUNK
    scale = dq ** -0.5

    def one_block(args):
        q_blk, i = args
        q_chunk = (i * Q_BLOCK + jnp.arange(Q_BLOCK)) // CHUNK
        sc = jnp.einsum('bqhd,bkhd->bhqk', q_blk, k).astype(jnp.float32) * scale
        mask = k_chunk[None, :] <= q_chunk[:, None]
        sc = jnp.where(mask[None, None], sc, NEG_INF)
        p = jax.nn.softmax(sc, axis=-1).astype(v.dtype)
        return jnp.einsum('bhqk,bkhd->bqhd', p, v)

    o = lax.map(one_block, (qb, jnp.arange(nb, dtype=jnp.int32)))
    return o.transpose(1, 0, 2, 3, 4).reshape(b, s, h * dv)

def mla_attention(c_q, c_kv, k_rope, q_lat_norm, w_uq, kv_lat_norm, w_ukv,
                  q_nope_norm, q_rope_norm, k_nope_norm, k_rope_norm, cos, sin):
    b, s, _ = c_q.shape
    q = (rmsnorm(c_q, q_lat_norm) @ w_uq).reshape(b, s, B_HEADS, B_QK_DIM)
    kv = (rmsnorm(c_kv, kv_lat_norm) @ w_ukv).reshape(b, s, B_HEADS, B_NOPE + B_V_DIM)
    q_nope = rmsnorm(q[..., :B_NOPE], q_nope_norm)
    q_pe = apply_rope(rmsnorm(q[..., B_NOPE:], q_rope_norm), cos, sin)
    k_nope = rmsnorm(kv[..., :B_NOPE], k_nope_norm)
    v = kv[..., B_NOPE:]
    k_pe = apply_rope(rmsnorm(k_rope, k_rope_norm)[:, :, None, :], cos, sin)
    q_full = jnp.concatenate([q_nope, q_pe], axis=-1)
    k_full = jnp.concatenate([k_nope, jnp.broadcast_to(k_pe, (b, s, B_HEADS, B_ROPE))], axis=-1)
    return block_causal_attention(q_full, k_full, v)

def first_inputs(seed: int = 0) -> dict:
    key = jax.random.key(seed)
    ks = iter(jax.random.split(key, 32))
    f32 = jnp.float32

    def w(shape, fan_in):
        return jax.random.normal(next(ks), (DEPTH,) + shape, f32) * fan_in ** -0.5

    def gain(n):
        return 1.0 + 0.05 * jax.random.normal(next(ks), (DEPTH, n), f32)

    x = jax.random.normal(next(ks), (BATCH, SEQ, D_MODEL), f32)
    return {
        "x": x,
        "ffn1_norm": gain(D_MODEL),
        "ffn1_w_gate": w((D_MODEL, D_FF), D_MODEL),
        "ffn1_w_up": w((D_MODEL, D_FF), D_MODEL),
        "ffn1_w_down": w((D_FF, D_MODEL), D_FF),
        "mix_norm": gain(D_MODEL),
        "w_in": w((D_MODEL, IN_COLS), D_MODEL),
        "a_q_norm": gain(A_HEAD_DIM),
        "a_k_norm": gain(A_HEAD_DIM),
        "a_rel_bias": 0.5 * jax.random.normal(next(ks), (DEPTH, A_HEADS, 2 * A_MAX_REL + 1), f32),
        "b_q_lat_norm": gain(B_Q_LORA),
        "b_w_uq": w((B_Q_LORA, B_HEADS * B_QK_DIM), B_Q_LORA),
        "b_kv_lat_norm": gain(B_KV_LORA),
        "b_w_ukv": w((B_KV_LORA, B_HEADS * (B_NOPE + B_V_DIM)), B_KV_LORA),
        "b_q_nope_norm": gain(B_NOPE),
        "b_q_rope_norm": gain(B_ROPE),
        "b_k_nope_norm": gain(B_NOPE),
        "b_k_rope_norm": gain(B_ROPE),
        "w_out": w((D_MIX, D_MODEL), D_MIX),
        "ffn2_norm": gain(D_MODEL),
        "ffn2_w_gate": w((D_MODEL, D_FF), D_MODEL),
        "ffn2_w_up": w((D_MODEL, D_FF), D_MODEL),
        "ffn2_w_down": w((D_FF, D_MODEL), D_FF),
        "final_norm": gain(D_MODEL),
    }

def first_block(x, ffn1_norm, ffn1_w_gate, ffn1_w_up, ffn1_w_down, mix_norm, w_in,
              a_q_norm, a_k_norm, a_rel_bias, b_q_lat_norm, b_w_uq, b_kv_lat_norm,
              b_w_ukv, b_q_nope_norm, b_q_rope_norm, b_k_nope_norm, b_k_rope_norm,
              w_out, ffn2_norm, ffn2_w_gate, ffn2_w_up, ffn2_w_down, final_norm):
    b, s, _ = x.shape
    cos, sin = rope_tables(s, B_ROPE)
    o_qa, o_ka, o_va = 0, A_WIDTH, 2 * A_WIDTH
    o_cq = 3 * A_WIDTH
    o_ckv = o_cq + B_Q_LORA
    o_kr = o_ckv + B_KV_LORA
    for l in range(DEPTH):
        x = x + 0.5 * swiglu(rmsnorm(x, ffn1_norm[l]), ffn1_w_gate[l], ffn1_w_up[l], ffn1_w_down[l])
        proj = rmsnorm(x, mix_norm[l]) @ w_in[l]
        qa = rmsnorm(proj[..., o_qa:o_ka].reshape(b, s, A_HEADS, A_HEAD_DIM), a_q_norm[l])
        ka = rmsnorm(proj[..., o_ka:o_va].reshape(b, s, A_HEADS, A_HEAD_DIM), a_k_norm[l])
        va = proj[..., o_va:o_cq].reshape(b, s, A_HEADS, A_HEAD_DIM)
        out_a = chunked_relbias_attention(qa, ka, va, a_rel_bias[l])
        out_b = mla_attention(proj[..., o_cq:o_ckv], proj[..., o_ckv:o_kr], proj[..., o_kr:],
                              b_q_lat_norm[l], b_w_uq[l], b_kv_lat_norm[l], b_w_ukv[l],
                              b_q_nope_norm[l], b_q_rope_norm[l], b_k_nope_norm[l],
                              b_k_rope_norm[l], cos, sin)
        x = x + jnp.concatenate([out_a, out_b], axis=-1) @ w_out[l]
        x = x + 0.5 * swiglu(rmsnorm(x, ffn2_norm[l]), ffn2_w_gate[l], ffn2_w_up[l], ffn2_w_down[l])
        x = rmsnorm(x, final_norm[l])
    return x


CONV_WIDTH = D_MODEL // 2
RWKV_WIDTH = D_MODEL - CONV_WIDTH
RWKV_HEAD = 64
RWKV_HEADS = RWKV_WIDTH // RWKV_HEAD
CONV_K = 31
DECAY_LORA = 64
A_LORA = 64
GATE_LORA = 160
D_FF_2 = 2816
FFN_CONV_K = 3
N_RWKV_IN = 3 * RWKV_WIDTH + DECAY_LORA + A_LORA + GATE_LORA
N_IN = 2 * CONV_WIDTH + N_RWKV_IN
RWKV_SPLITS = (RWKV_WIDTH, 2 * RWKV_WIDTH, 3 * RWKV_WIDTH,
               3 * RWKV_WIDTH + DECAY_LORA, 3 * RWKV_WIDTH + DECAY_LORA + A_LORA)
RMS_EPS = 1e-6
LN_EPS = 1e-5
LNX_EPS = 64e-5


def rms_norm(x, g):
    xf = x.astype(jnp.float32)
    y = xf * lax.rsqrt(jnp.mean(xf * xf, axis=-1, keepdims=True) + RMS_EPS)
    return (y * g.astype(jnp.float32)).astype(x.dtype)

def layer_norm(x, eps):
    xf = x.astype(jnp.float32)
    mu = jnp.mean(xf, axis=-1, keepdims=True)
    d = xf - mu
    return d * lax.rsqrt(jnp.mean(d * d, axis=-1, keepdims=True) + eps)

def causal_dwconv(x, w, b):
    K, C = w.shape
    y = lax.conv_general_dilated(x, w[:, None, :].astype(x.dtype), window_strides=(1,),
                                 padding=[(K - 1, 0)],
                                 dimension_numbers=('NWC', 'WIO', 'NWC'),
                                 feature_group_count=C)
    return y + b

def wkv7_scan(r, decay, k, v, kk, a):
    B, T, H, N = r.shape

    def step(S, inp):
        r_t, w_t, k_t, v_t, kk_t, a_t = inp
        s_kk = jnp.einsum('bhij,bhj->bhi', S, kk_t)
        S = (S * w_t[:, :, None, :] - s_kk[..., None] * (a_t * kk_t)[:, :, None, :]
             + v_t[..., None] * k_t[:, :, None, :])
        return S, jnp.einsum('bhij,bhj->bhi', S, r_t)

    xs = tuple(jnp.moveaxis(z.astype(jnp.float32), 1, 0) for z in (r, decay, k, v, kk, a))
    S0 = jnp.zeros((B, H, N, N), jnp.float32)
    _, ys = lax.scan(step, S0, xs)
    return jnp.moveaxis(ys, 0, 1)

def token_mix(h, w_in, conv_dw_w, conv_dw_b, conv_ln_g, conv_ln_b, rwkv_mu, w0, w2,
              a0, a2, g2, k_k, k_a, r_k, lnx_g, lnx_b, w_out):
    B, T, _ = h.shape
    f32 = jnp.float32
    p = h @ w_in
    p_conv, p_rw = p[..., :2 * CONV_WIDTH], p[..., 2 * CONV_WIDTH:]

    u, u_gate = jnp.split(p_conv, 2, axis=-1)
    u = u * jax.nn.sigmoid(u_gate)
    u = causal_dwconv(u, conv_dw_w, conv_dw_b)
    u = jax.nn.silu((layer_norm(u, LN_EPS) * conv_ln_g + conv_ln_b).astype(h.dtype))

    prev = jnp.pad(p_rw, ((0, 0), (1, 0), (0, 0)))[:, :-1]
    p_rw = p_rw + (prev - p_rw) * rwkv_mu
    r, k, v, wd, ad, gd = jnp.split(p_rw, RWKV_SPLITS, axis=-1)
    w_log = -jax.nn.softplus(-(w0 + jnp.tanh(wd) @ w2).astype(f32)) - 0.5
    decay = jnp.exp(-jnp.exp(w_log))
    a = jax.nn.sigmoid(a0 + ad @ a2)
    g = jax.nn.sigmoid(gd) @ g2
    heads = lambda z: z.reshape(B, T, RWKV_HEADS, RWKV_HEAD)
    kk = heads(k * k_k).astype(f32)
    kk = kk / jnp.maximum(jnp.sqrt(jnp.sum(kk * kk, axis=-1, keepdims=True)), 1e-12)
    k = k * (1.0 + (a - 1.0) * k_a)
    rh, kh, vh = heads(r), heads(k), heads(v)
    y = wkv7_scan(rh, heads(decay), kh, vh, kk, heads(a))
    y = layer_norm(y, LNX_EPS).reshape(B, T, RWKV_WIDTH) * lnx_g + lnx_b
    bonus = jnp.sum((rh * kh * r_k).astype(f32), axis=-1, keepdims=True) * vh.astype(f32)
    y = ((y + bonus.reshape(B, T, RWKV_WIDTH)) * g).astype(h.dtype)

    return jnp.concatenate([u, y], axis=-1) @ w_out

def channel_mix(h, w_up, ffn_dw_w, ffn_dw_b, w_down):
    z = causal_dwconv(h @ w_up, ffn_dw_w, ffn_dw_b)
    z_gate, z_val = jnp.split(z, 2, axis=-1)
    return (jax.nn.silu(z_gate) * z_val) @ w_down

def second_inputs(seed: int = 0) -> dict:
    key = jax.random.key(seed)
    ks = jax.random.split(key, 32)
    L = DEPTH
    nrm = lambda k, shape, s: jax.random.normal(k, shape, jnp.float32) * s
    return {
        'x': nrm(ks[0], (BATCH, SEQ, D_MODEL), 1.0),
        'c': nrm(ks[1], (BATCH, D_MODEL), 1.0),
        'ada_w': nrm(ks[2], (L, D_MODEL, 6 * D_MODEL), 0.5 * D_MODEL ** -0.5),
        'ada_b': nrm(ks[3], (L, 6 * D_MODEL), 0.02),
        'mix_pre_g': 1.0 + nrm(ks[4], (L, D_MODEL), 0.05),
        'mix_post_g': 1.0 + nrm(ks[5], (L, D_MODEL), 0.05),
        'w_in': nrm(ks[6], (L, D_MODEL, N_IN), D_MODEL ** -0.5),
        'conv_dw_w': nrm(ks[7], (L, CONV_K, CONV_WIDTH), CONV_K ** -0.5),
        'conv_dw_b': nrm(ks[8], (L, CONV_WIDTH), 0.02),
        'conv_ln_g': 1.0 + nrm(ks[9], (L, CONV_WIDTH), 0.05),
        'conv_ln_b': nrm(ks[10], (L, CONV_WIDTH), 0.02),
        'rwkv_mu': jax.random.uniform(ks[11], (L, N_RWKV_IN), jnp.float32),
        'w0': jax.random.uniform(ks[12], (L, RWKV_WIDTH), jnp.float32, minval=-5.0, maxval=1.0),
        'w2': nrm(ks[13], (L, DECAY_LORA, RWKV_WIDTH), 0.5 * DECAY_LORA ** -0.5),
        'a0': nrm(ks[14], (L, RWKV_WIDTH), 0.5),
        'a2': nrm(ks[15], (L, A_LORA, RWKV_WIDTH), 0.5 * A_LORA ** -0.5),
        'g2': nrm(ks[16], (L, GATE_LORA, RWKV_WIDTH), GATE_LORA ** -0.5),
        'k_k': 0.85 + nrm(ks[17], (L, RWKV_WIDTH), 0.05),
        'k_a': 1.0 + nrm(ks[18], (L, RWKV_WIDTH), 0.05),
        'r_k': nrm(ks[19], (L, RWKV_HEADS, RWKV_HEAD), 0.1),
        'lnx_g': 1.0 + nrm(ks[20], (L, RWKV_WIDTH), 0.05),
        'lnx_b': nrm(ks[21], (L, RWKV_WIDTH), 0.02),
        'w_out': nrm(ks[22], (L, D_MODEL, D_MODEL), D_MODEL ** -0.5),
        'ffn_pre_g': 1.0 + nrm(ks[23], (L, D_MODEL), 0.05),
        'ffn_post_g': 1.0 + nrm(ks[24], (L, D_MODEL), 0.05),
        'w_up': nrm(ks[25], (L, D_MODEL, 2 * D_FF_2), D_MODEL ** -0.5),
        'ffn_dw_w': nrm(ks[26], (L, FFN_CONV_K, 2 * D_FF_2), FFN_CONV_K ** -0.5),
        'ffn_dw_b': nrm(ks[27], (L, 2 * D_FF_2), 0.02),
        'w_down': nrm(ks[28], (L, D_FF_2, D_MODEL), D_FF_2 ** -0.5),
    }

def second_block(x, c, ada_w, ada_b, mix_pre_g, mix_post_g, w_in, conv_dw_w, conv_dw_b,
              conv_ln_g, conv_ln_b, rwkv_mu, w0, w2, a0, a2, g2, k_k, k_a, r_k,
              lnx_g, lnx_b, w_out, ffn_pre_g, ffn_post_g, w_up, ffn_dw_w, ffn_dw_b,
              w_down):
    for l in range(DEPTH):
        mod = jax.nn.silu(c) @ ada_w[l] + ada_b[l]
        sh_m, sc_m, gt_m, sh_f, sc_f, gt_f = jnp.split(mod[:, None, :], 6, axis=-1)
        h = rms_norm(x, mix_pre_g[l]) * (1.0 + sc_m) + sh_m
        m = token_mix(h, w_in[l], conv_dw_w[l], conv_dw_b[l], conv_ln_g[l], conv_ln_b[l],
                      rwkv_mu[l], w0[l], w2[l], a0[l], a2[l], g2[l], k_k[l], k_a[l],
                      r_k[l], lnx_g[l], lnx_b[l], w_out[l])
        x = x + gt_m * rms_norm(m, mix_post_g[l])
        h = rms_norm(x, ffn_pre_g[l]) * (1.0 + sc_f) + sh_f
        f = channel_mix(h, w_up[l], ffn_dw_w[l], ffn_dw_b[l], w_down[l])
        x = x + gt_f * rms_norm(f, ffn_post_g[l])
    return x


def setup_inputs(seed=0):
    out = dict(first_inputs(seed))
    for name, value in second_inputs(seed + 1).items():
        if name != "x":
            out[name + "_2"] = value
    return out


def reference(
    x, ffn1_norm, ffn1_w_gate, ffn1_w_up, ffn1_w_down, mix_norm, w_in, a_q_norm, a_k_norm,
    a_rel_bias, b_q_lat_norm, b_w_uq, b_kv_lat_norm, b_w_ukv, b_q_nope_norm, b_q_rope_norm,
    b_k_nope_norm, b_k_rope_norm, w_out, ffn2_norm, ffn2_w_gate, ffn2_w_up, ffn2_w_down,
    final_norm, c_2, ada_w_2, ada_b_2, mix_pre_g_2, mix_post_g_2, w_in_2, conv_dw_w_2,
    conv_dw_b_2, conv_ln_g_2, conv_ln_b_2, rwkv_mu_2, w0_2, w2_2, a0_2, a2_2, g2_2, k_k_2,
    k_a_2, r_k_2, lnx_g_2, lnx_b_2, w_out_2, ffn_pre_g_2, ffn_post_g_2, w_up_2, ffn_dw_w_2,
    ffn_dw_b_2, w_down_2,
):
    x = first_block(
        x, ffn1_norm, ffn1_w_gate, ffn1_w_up, ffn1_w_down, mix_norm, w_in, a_q_norm, a_k_norm,
        a_rel_bias, b_q_lat_norm, b_w_uq, b_kv_lat_norm, b_w_ukv, b_q_nope_norm, b_q_rope_norm,
        b_k_nope_norm, b_k_rope_norm, w_out, ffn2_norm, ffn2_w_gate, ffn2_w_up, ffn2_w_down,
        final_norm,
    )
    return second_block(
        x, c_2, ada_w_2, ada_b_2, mix_pre_g_2, mix_post_g_2, w_in_2, conv_dw_w_2, conv_dw_b_2,
        conv_ln_g_2, conv_ln_b_2, rwkv_mu_2, w0_2, w2_2, a0_2, a2_2, g2_2, k_k_2, k_a_2, r_k_2,
        lnx_g_2, lnx_b_2, w_out_2, ffn_pre_g_2, ffn_post_g_2, w_up_2, ffn_dw_w_2, ffn_dw_b_2,
        w_down_2,
    )


_drawn_inputs = setup_inputs


def setup_inputs(seed=0):
    import zlib

    import numpy as np

    out = dict(_drawn_inputs(seed))
    spreads = {}
    factors = {'mix_norm': 4.59,
     'a_q_norm': 8.0,
     'a_k_norm': 8.0,
     'b_q_lat_norm': 8.0,
     'b_kv_lat_norm': 7.97,
     'b_q_nope_norm': 8.0,
     'b_q_rope_norm': 8.0,
     'b_k_nope_norm': 8.0,
     'b_k_rope_norm': 8.0,
     'ffn2_norm': 2.696,
     'mix_pre_g_2': 2.737,
     'mix_post_g_2': 3.769,
     'conv_dw_b_2': 7.093,
     'conv_ln_g_2': 15.96,
     'conv_ln_b_2': 37.096,
     'w2_2': 5.873,
     'k_k_2': 39.82,
     'k_a_2': 3.992,
     'lnx_g_2': 18.68,
     'lnx_b_2': 50.85,
     'ffn_pre_g_2': 2.869,
     'ffn_post_g_2': 4.144,
     'ffn_dw_b_2': 7.506}
    for name, (base, spread) in spreads.items():
        noise = np.random.default_rng([zlib.crc32(name.encode()), seed]).standard_normal(out[name].shape)
        drawn = base * np.exp(spread * noise) if base else spread * noise
        out[name] = __import__('jax').numpy.asarray(drawn.astype(out[name].dtype))
    for name, factor in factors.items():
        out[name] = (out[name] * factor).astype(out[name].dtype)
    return out
```

```python
from contextlib import ExitStack

import numpy as np

import concourse.bass as bass
from concourse import mybir

P = 128
T = 512
NT = T // P
D = 1024
KD = D // P
DFF = 2816
KF = DFF // P
CH = 64
NC = T // CH
RING = 4
SLAB = KD * P
DOWN_CUT = [(0, 8), (8, 16), (16, 22)]
CONV_K = 31
DECAY = float(np.exp(-0.5))
EPS = 1e-6
LOWEST = -3e38

F32 = mybir.dt.float32
F32R = mybir.dt.float32r
ALU = mybir.AluOpType
ACT = mybir.ActivationFunctionType
AXX = mybir.AxisListType.X

SLABS = [("gu1", 2 * KF), ("down1", 24), ("in1", 16), ("uq", 2), ("ukv", 1), ("out1", 8),
         ("gu2", 2 * KF), ("down2", 24), ("in2", 23), ("out2", 8), ("up", 2 * KF), ("down3", 24)]


def starts(items):
    at, n = {}, 0
    for name, count in items:
        at[name] = n
        n += count
    return at, n


SLAB_AT, N_SLABS = starts(SLABS)
N_LOADS = -(-N_SLABS // RING) * RING

VEC_COLS = [("ffn1_norm", 8), ("mix_norm", 8), ("a_q_norm", 1), ("a_k_norm", 1), ("b_q_lat_norm", 2),
            ("b_kv_lat_norm", 1), ("b_q_nope_norm", 1), ("b_q_rope_norm", 1), ("b_k_nope_norm", 1),
            ("b_k_rope_norm", 1), ("ffn2_norm", 8), ("final_norm", 8), ("c", 8), ("ada_b", 48),
            ("mix_pre_g", 8), ("mix_post_g", 8), ("conv_w", 4 * CONV_K), ("conv_b", 4),
            ("conv_ln_g", 4), ("conv_ln_b", 4), ("mu", 15), ("w0", 4), ("a0", 4), ("k_k", 4),
            ("k_a", 4), ("r_k", 4), ("lnx_g", 4), ("lnx_b", 4), ("ffn_pre_g", 8), ("ffn_post_g", 8),
            ("ffn_dw_w", 3 * 2 * KF), ("ffn_dw_b", 2 * KF)]
VEC_AT, N_VEC = starts(VEC_COLS)

BOTH_COLS = [("ident", 128), ("head2", 2), ("ones", 1)]
BLOCK1_COLS = [("head4", 4), ("quarter", 1), ("swap", 128), ("maskq", 128), ("maskk", 64)]
BLOCK2_COLS = [("eye64", 64), ("su", 64), ("iu", 64), ("niu", 64), ("np0", 64), ("nq0", 64),
               ("off32", 64), ("off64", 64), ("center", 128), ("block", 128), ("mean512", 128), ("keep", 512)]
BOTH_AT, N_BOTH = starts(BOTH_COLS)
BLOCK1_AT, N_BLOCK1 = starts(BLOCK1_COLS)
BLOCK2_AT, N_BLOCK2 = starts(BLOCK2_COLS)

MADE = 62

HI_AT = {"ffn1": 0, "mix": 1, "ffn2": 2, "mixpre": 3, "ffnpre": 4}
SCALED_AT = {"ffn1": 0, "mix": 1, "ffn2": 2, "mixpre": 3, "mixpost": 4, "ffnpre": 5, "ffnpost": 6}
NORMS = ["ffn1", "mix", "ffn2", "final", "mixpre", "mixpost", "ffnpre", "ffnpost"]

IN1_RAW = ["cq0", "cq1", "ckv0", "kr0"] + [f"qa{j}" for j in range(4)] + [f"ka{j}" for j in range(4)]
LATENT_RAW = ["qn0", "qn1", "qn2", "qn3", "qr0", "qr1", "kn0", "kn1", "kn2", "kn3"]


def constants():
    p = np.arange(P)
    t = np.arange(CH)
    s = p[:, None] % CH
    c = {
        "ident": np.eye(P), "swap": np.eye(P)[:, (p // 32) * 32 + (p + 16) % 32],
        "head2": p[:, None] // 64 == np.arange(2), "head4": p[:, None] // 32 == np.arange(4),
        "ones": np.ones((P, 1)), "quarter": p[:, None] < 32,
        "eye64": s == t, "su": s < t, "iu": s <= t, "niu": -1.0 * (s <= t),
        "np0": -1.0 * ((s < t) & (s // 16 == t // 16)), "nq0": -1.0 * ((s > t) & (s // 16 == t // 16)),
        "off32": (s // 32 == t // 32) & (s // 16 > t // 16),
        "off64": s // 32 > t // 32,
        "keep": np.broadcast_to(np.arange(T) % CH != 0, (P, T)),
        "block": p[:, None] // 64 == p[None, :] // 64,
        "center": np.eye(P) - (p[:, None] // 64 == p[None, :] // 64) / 64.0,
        "mean512": np.full((P, P), 1.0 / 512),
        "maskq": np.broadcast_to(p[None, :] < CH, (P, P)),
        "maskk": np.full((P, CH), -1e30),
    }
    tables = [np.ascontiguousarray(np.concatenate([np.asarray(c[k]).astype(np.float32) for k, _ in cols], 1))
              for cols in (BOTH_COLS, BLOCK1_COLS, BLOCK2_COLS)]
    inv = (1.0 / (np.float32(10000.0) ** (np.arange(0, 32, 2, dtype=np.float32) / np.float32(32)))).astype(np.float32)
    ang = (np.arange(T, dtype=np.float32)[:, None] * inv[None, :]).astype(np.float32)
    j = p % 16
    sign = np.where(p % 32 < 16, -1.0, 1.0)[:, None]
    rope = np.stack([np.cos(ang).T[j], np.sin(ang).T[j] * sign], 1).astype(np.float32)
    return (*tables, np.ascontiguousarray(rope))


def build(nc, x_in, slabs, ada_in, vec_in, both_in, block1_in, block2_in, rope_in, relb_in, lora_in, g2b_in,
          y_out):
    ctx = ExitStack()
    with ctx:
        base = -(-nc.sbuf_base // 64) * 64
        cursor = [base]

        def place(name, cols, dt=F32, offset=None):
            if offset is None:
                offset = cursor[0]
                cursor[0] += -(-4 * cols // 32) * 32
            return nc.alloc_sbuf_tensor_at(name, [P, cols], dt, offset=offset)

        def tiles(t, n, w=T):
            return t[:, 0:n * w].rearrange("p (n w) -> p n w", n=n)

        xT_t = place("xT", KD * T)
        h_at = cursor[0]
        hi_t, lo_t = place("h_hi", KD * T, F32R), place("h_lo", KD * T, F32R)
        wraw_t, whi_t, wlo_t = place("w_raw", RING * SLAB), place("w_hi", RING * SLAB, F32R), place("w_lo", RING * SLAB, F32R)
        tmp_t = place("tmp", 6 * T)
        vec_t, both_t = place("vec", N_VEC), place("both", N_BOTH)
        block_at = cursor[0]
        block2_t = place("block2", N_BLOCK2)
        block1_t = place("block1", N_BLOCK1, offset=block_at)
        mod_t, small_t = place("mod", 48 + 32), place("small", 256)
        g2b_t = place("g2b", T)
        arena = cursor[0]
        acth_t, actl_t = place("act_hi", KF * T, F32R), place("act_lo", KF * T, F32R)
        assert cursor[0] <= nc.sbuf_usable_end, (cursor[0], nc.sbuf_usable_end)
        xT, h_hi, h_lo = tiles(xT_t, KD), tiles(hi_t, KD), tiles(lo_t, KD)
        w_raw, w_hi, w_lo = (tiles(t, RING, SLAB) for t in (wraw_t, whi_t, wlo_t))
        tmp = tiles(tmp_t, 6)
        act_hi, act_lo = tiles(acth_t, KF), tiles(actl_t, KF)

        def slot(name, at, n, dt=F32, w=T):
            assert at * T + n * w <= 2 * KF * T, name
            return tiles(place(name, n * w, dt, offset=arena + 4 * T * at), n, w)

        qa, ka, qn, kn = slot("qa", 0, 4), slot("ka", 4, 4), slot("qn", 8, 4), slot("kn", 12, 4)
        qr, kr, va = slot("qr", 16, 2), slot("kr", 18, 1), slot("va", 19, 4)
        cq, ckv = slot("cq", 23, 2), slot("ckv", 25, 1)
        cq_hi, cq_lo = slot("cq_hi", 26, 2, F32R), slot("cq_lo", 28, 2, F32R)
        ckv_hi, ckv_lo = slot("ckv_hi", 30, 1, F32R), slot("ckv_lo", 31, 1, F32R)
        rope, vb, relb = slot("rope", 32, 2), slot("vb", 34, 4), slot("relb", 38, 2)
        adaw = slot("adaw", 40, 2, w=SLAB)
        probT = slot("probT", 23, 8)
        prob = slot("prob", 31, 3)
        rk_r, rk_k, rk_v, rk_w, rk_a, rk_g = (slot("rk_" + n, 2 * i, 2) for i, n in enumerate("rkvwag"))
        tokV, tokK, tokB, tokQ = (slot("tok_" + n, 12 + 2 * i, 2) for i, n in enumerate("vkbq"))
        mMT, mMR, mAR = (slot("m_" + n, 20 + 2 * i, 2) for i, n in enumerate(("mt", "mr", "ar")))
        mP, mQ, mR, mO1, mO2 = (slot("m_" + n, 26 + 2 * i, 2) for i, n in enumerate(("p", "q", "r", "o1", "o2")))
        rk_b, y_keep = slot("rk_b", 36, 2), slot("y_keep", 38, 2)
        lora, lora_act = slot("lora", 40, 2), slot("lora_act", 42, 2)
        mW, mX, mZ, mS = rk_k, rk_w, rk_a, rk_v
        mG, mHD = mO1, mO2
        g2b, lora_act2 = g2b_t, tmp[:, 5, :]
        shift = tmp_t[:, 2 * T:2 * T + 2 * 516].rearrange("p (n w) -> p n w", n=2)
        conv_in, conv_out, conv_gate = slot("conv_in", 0, 4, w=T + 32), slot("conv_out", 5, 4), slot("conv_gate", 9, 2)
        mid_a = slot("mid_a", 0, KD)
        mid_h = tiles(place("mid_h", KD * T, offset=h_at), KD)

        bank = [ctx.enter_context(nc.psum_tensor(f"bank{i}", [P, T], F32))[:, :] for i in range(8)]

        def vec(k, j=0, n=1):
            return vec_t[:, VEC_AT[k] + j:VEC_AT[k] + j + n]

        def const(k):
            for t, at, cols in ((both_t, BOTH_AT, BOTH_COLS), (block1_t, BLOCK1_AT, BLOCK1_COLS),
                                (block2_t, BLOCK2_AT, BLOCK2_COLS)):
                if k in at:
                    return t[:, at[k]:at[k] + dict(cols)[k]]

        ident = const("ident")
        mod = mod_t[:, 0:48]
        gs = {"mixpre": mod_t[:, 48:56], "ffnpre": mod_t[:, 56:64]}
        gp = {"mixpost": mod_t[:, 64:72], "ffnpost": mod_t[:, 72:80]}
        shf = {"mixpre": mod_t[:, 0:8], "ffnpre": mod_t[:, 24:32]}
        n_std, n_rs = small_t[:, 0:4], small_t[:, 4:8]
        silc = small_t[:, 8:16]
        hd_rs = {"lat": small_t[:, 16:28], "main": small_t[:, 28:92], "up": small_t[:, 92:188]}
        row_max, row_nmax, row_sum = small_t[:, 188:192], small_t[:, 192:196], small_t[:, 196:200]
        rk_rs, d_end, omka = small_t[:, 200:216], small_t[:, 216:232], small_t[:, 232:236]

        sems = {}

        def S(name):
            if name not in sems:
                sems[name] = ctx.enter_context(nc.semaphore(name))
            return sems[name]

        def chunk(m, e, g, c):
            return m[CH * e:CH * e + CH, g, CH * c:CH * c + CH]

        def rows(m, g=slice(None)):
            return m[:, g, :].rearrange("p (c t) -> p c t", c=NC)

        def every_chunk(t64):
            return t64.unsqueeze(1).to_broadcast([P, NC, CH])

        block = ctx.enter_context(nc.Block())

        @block.sync
        def _(sp):
            for dst, src in ((vec_t, vec_in), (both_t, both_in), (block1_t, block1_in)):
                sp.dma_start(dst[:, :], src).then_inc(S("tables_in"), 16)
            sp.dma_start(xT, x_in).then_inc(S("x_in"), 16)
            for r in range(RING):
                sp.dma_start(w_raw[:, r, :], slabs[r]).then_inc(S(f"w_raw_in{r}"), 16)
            with sp.Fori(1, N_LOADS // RING) as i:
                for r in range(RING):
                    sp.wait_ge(S("w_split"), i * RING + (r + 1 - RING))
                    sp.dma_start(w_raw[:, r, :], slabs[i * RING + r]).then_inc(S(f"w_raw_in{r}"), 16)
            for j in range(KD):
                sp.wait_ge(S("norm_lo"), 8 * NORMS.index("ffnpost") + j + 1)
                sp.dma_start(y_out[:, j, :], xT[:, j, :]).then_inc(S("y_out"), 16)
            sp.wait_ge(S("y_out"), 16 * KD)

        @block.gpsimd
        def _(pool):
            def split(n, r, loads, first=False):
                pool.wait_ge(S(f"w_raw_in{r}"), loads)
                if not first:
                    pool.wait_ge(S("slab_done"), n + (1 - RING))
                    pool.nop(nofuse=True)
                nc.gpsimd.tensor_scalar(w_hi[:, r, :], w_raw[:, r, :], 1.0, 1.0, ALU.mult, ALU.mult).then_inc(S("w_hi"), 1)
                pool.wait_ge(S("w_hi"), n + 1)
                nc.gpsimd.tensor_tensor(w_lo[:, r, :], w_raw[:, r, :], w_hi[:, r, :], ALU.subtract).then_inc(S("w_split"), 1)

            for r in range(RING):
                split(r, r, 16, first=True)
            with pool.Fori(1, N_LOADS // RING) as i:
                for r in range(RING):
                    split(i * RING + r, r, i * 16 + 16)

        @block.tensor
        def _(pe):
            mm = nc.tensor.matmul
            def passes(out, hi, lo, rhs_hi, rhs_lo, start, stop):
                mm(out, hi, rhs_hi, start=start, stop=False, skip_group_check=True)
                mm(out, hi, rhs_lo, start=False, stop=False, skip_group_check=True)
                return mm(out, lo, rhs_hi, start=False, stop=stop, skip_group_check=True)

            def product(out, n, r, act_h, act_l, ks=range(KD), first=0, start=True, stop=True, wait_k=None, token_major=False):
                pe.wait_ge(S("w_split"), n + 1)
                for i, k in enumerate(ks):
                    if wait_k is not None:
                        wait_k(k)
                    w = slice(P * i, P * i + P)
                    hi, lo = w_hi[:, r, w], w_lo[:, r, w]
                    a, b = start and i == 0, stop and i == len(ks) - 1
                    if not token_major:
                        last = passes(out, hi, lo, act_h[:, first + k, :], act_l[:, first + k, :], a, b)
                        continue
                    for t in range(NT):
                        o, tok = out[:, P * t:P * t + P], slice(P * t, P * t + P)
                        mm(o, act_h[:, first + k, tok], hi, start=a and t == 0, stop=False, skip_group_check=True)
                        mm(o, act_l[:, first + k, tok], hi, start=False, stop=False, skip_group_check=True)
                        last = mm(o, act_h[:, first + k, tok], lo, start=False, stop=b, skip_group_check=True)
                return last

            def stat(out, square, mask, start, width):
                for t in range(NT):
                    last = mm(out[:, width * t:width * t + width], square[:, P * t:P * t + P], mask,
                              start=start and t == 0, stop=True, skip_group_check=True)
                return last

            def spread(out, cols, heads):
                w = P // heads
                for t in range(NT):
                    for e in range(heads):
                        c = cols[:, heads * t + e:heads * t + e + 1].to_broadcast([P, w])
                        if heads == 1:
                            last = nc.tensor.transpose(out[:, P * t:P * t + P], c, ident)
                        else:
                            last = mm(out[w * e:w * e + w, P * t:P * t + P], c, ident, start=True, stop=True,
                                      skip_group_check=True)
                return last

            def norm_stats(name, j):
                q = NORMS.index(name)
                pe.wait_ge(S("norm_square"), 8 * q + j + 1)
                stat(bank[7], tmp[:, j % 2, :], const("ones"), j == 0, 1).then_inc(S("norm_stat"), 1)

            def norm_spread(name):
                q = NORMS.index(name)
                pe.wait_ge(S("norm_rs"), q + 1)
                spread(bank[6], n_rs, 1).then_inc(S("norm_spread"), 1)

            def after_norm(name):
                q = NORMS.index(name)
                return lambda k: pe.wait_ge(S("norm_lo"), 8 * q + k + 1)

            def gate_up(name, o, norm):
                at = SLAB_AT[name]

                def pair(i, u, wait_k=None):
                    pe.wait_ge(S("ff_product"), i * 2 + (o + u + 1))
                    for m in range(2):
                        n = 2 * u + m
                        product(bank[n], i * 4 + (at + n), (at + n) % RING, h_hi, h_lo,
                                wait_k=wait_k if m == 0 else None).then_inc(S("slab_done"), 1)

                pair(0, 0, after_norm(norm))
                pair(0, 1)
                with pe.Fori(1, KF // 2) as i:
                    pair(i, 0)
                    pair(i, 1)

            def down(name, o, done, done_at, norm):
                at = SLAB_AT[name]
                for m in range(KD):
                    if m >= 4:
                        pe.wait_ge(S(done), done_at + m - 3)
                    elif name == "down3":
                        pe.wait_ge(S("taps"), 2 * KF + m + 1)
                    else:
                        pe.wait_ge(S("ff_product"), o + KF + m // 2 + 1)
                    for s, (k0, k1) in enumerate(DOWN_CUT):
                        n = at + 3 * m + s
                        wait_k = (lambda k: pe.wait_ge(S("act_lo"), o + 3 + k)) if m == 0 else None
                        product(bank[m % 4], n, n % RING, act_hi, act_lo, ks=range(k0, k1), start=s == 0, stop=s == 2,
                                wait_k=wait_k).then_inc(S("slab_done"), 1)
                    if m:
                        norm_stats(norm, m - 1)
                norm_stats(norm, KD - 1)
                norm_spread(norm)

            pe.wait_ge(S("tables_in"), 48)
            for j in range(KD):
                norm_stats("ffn1", j)
            norm_spread("ffn1")
            gate_up("gu1", 0, "ffn1")
            down("down1", 0, "x_new", 0, "mix")

            raw_n, spread_n = [0], [0]

            def head_stat(name, bk, col, mask, width, start):
                pe.wait_ge(S("hd_square"), raw_n[0] + 1)
                stat(bank[bk][:, col:col + NT * width], tmp[:, raw_n[0] % 2, :], const(mask)[:, 0:width], start, width)\
                    .then_inc(S("hd_stat"), 1)
                raw_n[0] += 1

            def head_spread(cols, heads):
                r = spread_n[0]
                if r >= 2:
                    pe.wait_ge(S("hd_applied"), r - 1)
                spread(bank[6 if r % 2 == 0 else 4], cols, heads).then_inc(S("hd_spread"), 1)
                spread_n[0] += 1

            at = SLAB_AT["in1"]
            stats_in1 = [("cq0", 7, 0, "ones", 1, True), ("cq1", 7, 0, "ones", 1, False), ("ckv0", 7, 4, "ones", 1, False),
                         ("kr0", 7, 8, "quarter", 1, False)] + \
                        [(IN1_RAW[4 + j], 5, 8 * j, "head2", 2, j == 0) for j in range(8)]
            pe.wait_ge(S("norm_std"), 2)
            for m in range(16):
                if m >= 4:
                    pe.wait_ge(S("in1_raw"), m - 3)
                product(bank[m % 4], at + m, (at + m) % RING, h_hi, h_lo, wait_k=after_norm("mix") if m == 0 else None,
                        token_major=m >= 12).then_inc(S("slab_done"), 1)
                if 1 <= m <= 12:
                    head_stat(*stats_in1[m - 1])
                if m == 6:
                    pe.wait_ge(S("hd_rs"), 1)
                    head_spread(hd_rs["lat"][:, 0:4], 1)
                    head_spread(hd_rs["lat"][:, 4:8], 1)
                if m == 7:
                    head_spread(hd_rs["lat"][:, 8:12], 1)
            for t in range(14):
                if t < 6:
                    n = SLAB_AT["uq"] + t // 3
                    ks, first, a_hi, a_lo = range(2), 2 * (t % 3), cq_hi, cq_lo
                else:
                    n = SLAB_AT["ukv"]
                    ks, first, a_hi, a_lo = range(1), t - 6, ckv_hi, ckv_lo
                r = n % RING
                if t in (0, 3, 6):
                    pe.wait_ge(S("w_split"), n + 1)
                if t == 0:
                    pe.wait_ge(S("cq_split"), 2)
                if t == 6:
                    pe.wait_ge(S("cq_split"), 3)
                pe.wait_ge(S("in1_raw"), 16 + t - 3)
                out = bank[t % 4]
                for k in ks:
                    w = slice(P * (first + k), P * (first + k) + P)
                    hi, lo = w_hi[:, r, w], w_lo[:, r, w]
                    a, b = k == 0, k == len(ks) - 1
                    if t < 10:
                        last = passes(out, hi, lo, a_hi[:, k, :], a_lo[:, k, :], a, b)
                    else:
                        for q in range(NT):
                            o, tok = out[:, P * q:P * q + P], slice(P * q, P * q + P)
                            mm(o, a_hi[:, k, tok], hi, start=q == 0, stop=False, skip_group_check=True)
                            mm(o, a_lo[:, k, tok], hi, start=False, stop=False, skip_group_check=True)
                            last = mm(o, a_hi[:, k, tok], lo, start=False, stop=True, skip_group_check=True)
                last.then_inc(S("slab_done" if t in (2, 5, 13) else "latent_mm"), 1)
                if 1 <= t <= 10:
                    i = t - 1
                    if i < 4:
                        spec = (i * 8, "head2", 2)
                    elif i < 6:
                        spec = (32 + 16 * (i - 4), "head4", 4)
                    else:
                        spec = (64 + 8 * (i - 6), "head2", 2)
                    head_stat(LATENT_RAW[i], 7, *spec, i == 0)
            pe.wait_ge(S("hd_rs"), 2)
            for j in range(8):
                head_spread(hd_rs["main"][:, 8 * j:8 * j + 8], 2)
            pe.wait_ge(S("hd_rs"), 3)
            for j in range(4):
                head_spread(hd_rs["up"][:, 8 * j:8 * j + 8], 2)
            for j in range(2):
                head_spread(hd_rs["up"][:, 32 + 16 * j:48 + 16 * j], 4)
            for j in range(4):
                head_spread(hd_rs["up"][:, 64 + 8 * j:72 + 8 * j], 2)
            for j, (m, need) in enumerate(((qr[:, 0, :], 16), (qr[:, 1, :], 17), (kr[:, 0, :], 17))):
                pe.wait_ge(S("hd_applied"), need)
                pe.wait_ge(S("in1_raw"), 30)
                mm(bank[j], const("swap"), m, start=True, stop=True).then_inc(S("swapped"), 1)

            def scores(s):
                h, q = divmod(s, NT)
                e, j, out = h % 2, (h % 8) // 2, bank[s % 3]
                L, e64 = P * (q + 1), slice(CH * e, CH * e + CH)
                if s == 0:
                    pe.wait_ge(S("hd_applied"), 21)
                    pe.wait_ge(S("roped"), 3)
                if s >= 3:
                    pe.wait_ge(S("probs"), s - 2)
                qs = slice(P * q, P * q + P)
                if h < 8:
                    mm(out[:, 0:L], qa[e64, j, qs], ka[e64, j, 0:L], start=True, stop=True).then_inc(S("scores"), 1)
                    return
                e32 = slice(32 * (h % 4), 32 * (h % 4) + 32)
                mm(out[:, 0:L], qn[e64, j, qs], kn[e64, j, 0:L], start=True, stop=False, skip_group_check=True)
                mm(out[:, 0:L], qr[e32, (h - 8) // 4, qs], kr[e32, 0, 0:L], start=False, stop=False,
                   skip_group_check=True, tile_position=(32 * (h % 4), 0))
                e1 = slice(32 * (h % 4), 32 * (h % 4) + 1)
                mm(out[:, L - CH:L], const("maskq")[e1, :], const("maskk")[e1, :], start=False, stop=True,
                   skip_group_check=True, tile_position=(32 * (h % 4), 0)).then_inc(S("scores"), 1)

            def turn(s):
                pe.wait_ge(S("probs_normed"), s + 1)
                if s >= 2:
                    pe.wait_ge(S("probT"), s - 1)
                for kt in range(s % NT + 1):
                    last = nc.tensor.transpose(bank[3 + s % 2][:, P * kt:P * kt + P], prob[:, s % 3, P * kt:P * kt + P], ident)
                last.then_inc(S("turned"), 1)

            def values(h):
                pe.wait_ge(S("probT"), NT * h + NT)
                if h % 2 == 0 and h >= 4:
                    pe.wait_ge(S("o_lo"), h // 2 - 1)
                v = va if h < 8 else vb
                for kt in range(NT):
                    last = mm(bank[5 + (h // 2) % 2][CH * (h % 2):CH * (h % 2) + CH, P * kt:T],
                              v[:, kt, CH * (h % 8):CH * (h % 8) + CH], probT[:, NT * (h % 2) + kt, P * kt:T],
                              start=kt == 0, stop=kt == NT - 1, skip_group_check=True)
                last.then_inc(S("values"), 1)

            def modulation(a):
                pe.wait_ge(S(f"ada_in{a % 2}"), 16 * (a // 2 + 1))
                if a == 0:
                    pe.wait_ge(S("silu_c"), 1)
                for k in range(KD):
                    last = mm(bank[7][:, a:a + 1], adaw[:, a % 2, P * k:P * k + P], silc[:, k:k + 1],
                              start=a == 0 and k == 0, stop=k == KD - 1, skip_group_check=True)
                last.then_inc(S("ada_mm"), 1)

            for s in range(16 * NT + 2):
                if s < 16 * NT:
                    scores(s)
                if s >= 2:
                    turn(s - 2)
                    if (s - 2) % NT != 0:
                        modulation(3 * ((s - 2) // NT) + (s - 2) % NT - 1)
                    elif s > 2:
                        values((s - 2) // NT - 1)
            values(15)

            def short(name, done, done_at, wait_k, norm):
                at = SLAB_AT[name]
                for m in range(KD):
                    if m >= 4:
                        pe.wait_ge(S(done), done_at + m - 3)
                    product(bank[m % 4], at + m, (at + m) % RING, h_hi, h_lo, wait_k=wait_k if m == 0 else None)\
                        .then_inc(S("slab_done"), 1)
                    if m:
                        norm_stats(norm, m - 1)
                norm_stats(norm, KD - 1)
                norm_spread(norm)

            pe.wait_ge(S("mod_ready"), 1)
            pe.wait_ge(S("probT"), 16 * NT)
            short("out1", "x_new", 8, lambda k: pe.wait_ge(S("o_lo"), k + 1), "ffn2")

            gate_up("gu2", KF, "ffn2")
            down("down2", KF, "x_new", 16, "final")

            for j in range(KD):
                norm_stats("mixpre", j)
            norm_spread("mixpre")
            at = SLAB_AT["in2"]

            def project(m):
                if m >= 4:
                    pe.wait_ge(S("in2_raw"), m - 3 if m <= 18 else 16 + (m - 19) // 2)
                product(bank[m % 4], at + m, (at + m) % RING, h_hi, h_lo, wait_k=after_norm("mixpre") if m == 0 else None)\
                    .then_inc(S("slab_done"), 1)

            made = []

            def made_in(pairs, name, g, half, bk=None, cs=range(NC)):
                out = bank[len(made) % 6]
                if len(made) >= 6:
                    before, value = made[-6]
                    pe.wait_ge(S("rk_" + before), value)
                made.append((name, 2 * half + g + 1))
                for i, (lhs, rhs, skip) in enumerate(pairs):
                    for c in range(NC):
                        if c < skip:
                            continue
                        for e in range(2):
                            r = const("eye64")[CH * e:CH * e + CH, :] if rhs is None else chunk(rhs, e, g, c)
                            last = mm(out[CH * e:CH * e + CH, CH * c:CH * c + CH], chunk(lhs, e, g, c), r,
                                      start=i == 0 and c == 0, stop=i == len(pairs) - 1, skip_group_check=True)
                return last.then_inc(S("rk_mm"), 1)

            def ready(name, g, half):
                pe.wait_ge(S("rk_" + name), 2 * half + g + 1)

            def recurrence(half):
                for g in range(2):
                    G = 2 * half + g
                    fs = slice(P * G, P * G + P)
                    for i in range(3):
                        n = 3 * G + i
                        if n == 0:
                            pe.wait_ge(S("lora_in"), 48)
                            pe.wait_ge(S("lora_act"), 3)
                        if n >= 2:
                            pe.wait_ge(S("lora_out"), n - 1)
                        out = bank[4 + n % 2]
                        if i < 2:
                            r = slice(CH * i, CH * i + CH)
                            mm(out[:, :], lora[r, 0, fs], lora_act[r, 0, :], start=True, stop=True).then_inc(S("lora_mm"), 1)
                        else:
                            mm(out[:, :], lora[:, 1, fs], lora_act[:, 1, :], start=True, stop=False)
                            mm(out[:, :], g2b[0:32, fs], lora_act2[0:32, :], start=False, stop=True).then_inc(S("lora_mm"), 1)
                for g in range(2):
                    v = 2 * half + g + 1
                    pe.wait_ge(S("rk_ksq"), v)
                    if v > 1:
                        pe.wait_ge(S("rk_rsd"), v - 1)
                    stat(bank[7], tmp[:, g, :], const("head2"), True, 2).then_inc(S("rk_kst"), 1)
                for g in range(2):
                    v = 2 * half + g + 1
                    pe.wait_ge(S("rk_krs"), 2 * half + 2)
                    spread(bank[6], rk_rs[:, 8 * g:8 * g + 8], 2).then_inc(S("rk_kspread"), 1)
                    pe.wait_ge(S("rk_bz"), v)
                    mm(bank[7][:, :], const("block"), mR[:, g, :], start=True, stop=True).then_inc(S("rk_bsum"), 1)
                    pe.wait_ge(S("rk_bonus"), v)
                for g in range(2):
                    pe.wait_ge(S("lora_out"), 6 * half + 6)
                    ready("factors", g, half)
                    made_in([(rk_v, None, 0)], "tv", g, half)
                    made_in([(rk_k, None, 0)], "tk", g, half)
                    made_in([(rk_a, None, 0)], "tb", g, half)
                    made_in([(rk_w, None, 0)], "tq", g, half)
                for g in range(2):
                    made_in([(rk_a, rk_w, 0)], "p0", g, half)
                    made_in([(rk_w, rk_a, 0)], "q0", g, half)
                    made_in([(rk_k, rk_w, 0)], "mt", g, half)
                    made_in([(rk_a, rk_r, 0)], "ar", g, half)
                    made_in([(rk_k, rk_r, 0)], "mr", g, half)
                for g in range(2):
                    ready("p0", g, half)
                    ready("q0", g, half)
                    made_in([(mP, mQ, 0)], "q1", g, half)
                    made_in([(mQ, mP, 0)], "p1", g, half)
                for g in range(2):
                    ready("r0", g, half)
                    ready("q1", g, half)
                    ready("p1", g, half)
                    made_in([(mQ, mR, 0)], "r1", g, half)
                    made_in([(mP, mQ, 0)], "q2", g, half)
                    made_in([(mQ, mP, 0)], "p2", g, half)
                for g in range(2):
                    ready("r1", g, half)
                    ready("q2", g, half)
                    ready("p2", g, half)
                    made_in([(mQ, mR, 0)], "r2", g, half)
                    made_in([(mP, mQ, 0)], "q3", g, half)
                for g in range(2):
                    ready("r2", g, half)
                    ready("q3", g, half)
                    made_in([(mQ, mR, 0)], "r3", g, half)
                for lvl, off in ((1, mO1), (2, mO2)):
                    for g in range(2):
                        ready("r3" if lvl == 1 else "r4", g, half)
                        made_in([(mR, None, 0)], f"rt{lvl}", g, half)
                        made_in([(off, mR, 0)], f"y{lvl}", g, half)
                    for g in range(2):
                        ready(f"rt{lvl}", g, half)
                        ready(f"y{lvl}", g, half)
                        made_in([(mP, mQ, 0)], "r4" if lvl == 1 else "r5", g, half)
                for g in range(2):
                    ready("mt", g, half)
                    ready("r5", g, half)
                    ready("tq", g, half)
                    made_in([(mMT, tokV, 0)], "x", g, half)
                    made_in([(mR, tokQ, 0)], "w", g, half)
                for g in range(2):
                    ready("x", g, half)
                    made_in([(mR, mX, 0)], "z", g, half)
                    ready("w", g, half)
                    made_in([(mW, tokB, 0)], "g", g, half)
                for g in range(2):
                    ready("z", g, half)
                    made_in([(tokK, tokV, 0), (tokB, mZ, 0)], "hd", g, half)
                    made_in([(mW, mAR, 0)], "rho", g, half)
                for c in range(1, NC - 1):
                    for g in range(2):
                        if c == 1:
                            ready("hd", g, half)
                            ready("g", g, half)
                        else:
                            pe.wait_ge(S(f"rk_state{g}"), (NC - 2) * half + c - 1)
                        src = mHD if c == 1 else mS
                        for e in range(2):
                            last = mm(bank[6 + g][CH * e:CH * e + CH, CH * c:CH * c + CH], chunk(mG, e, g, c),
                                      chunk(src, e, g, 0 if c == 1 else c), start=True, stop=True, skip_group_check=True)
                        last.then_inc(S(f"rk_step{g}"), 1)
                for g in range(2):
                    pe.wait_ge(S(f"rk_state{g}"), (NC - 2) * (half + 1))
                    ready("rho", g, half)
                    made_y(g, half)
                for g in range(2):
                    v = 2 * half + g + 1
                    ready("y", g, half)
                    made_plain("d", const("center"), mP, g, half)
                for g in range(2):
                    v = 2 * half + g + 1
                    pe.wait_ge(S("rk_dsq"), v)
                    stat(bank[7], tmp[:, g, :], const("head2"), True, 2).then_inc(S("rk_dst"), 1)
                    pe.wait_ge(S("rk_drs"), v)
                    spread(bank[6], rk_rs[:, 8 * g:8 * g + 8], 2).then_inc(S("rk_dspread"), 1)
                    pe.wait_ge(S("rk_out"), v)

            def made_y(g, half):
                out = bank[len(made) % 6]
                before, value = made[-6]
                pe.wait_ge(S("rk_" + before), value)
                made.append(("y", 2 * half + g + 1))
                for c in range(NC):
                    for e in range(2):
                        o = out[CH * e:CH * e + CH, CH * c:CH * c + CH]
                        mm(o, chunk(tokV, e, g, c), chunk(mMR, e, g, c), start=c == 0, stop=False, skip_group_check=True)
                        if c:
                            s = mHD if c == 1 else mS
                            mm(o, chunk(s, e, g, 0 if c == 1 else c), chunk(rk_r, e, g, c), start=False, stop=False,
                               skip_group_check=True)
                        last = mm(o, chunk(mZ, e, g, c), chunk(mAR, e, g, c), start=False, stop=True, skip_group_check=True)
                last.then_inc(S("rk_mm"), 1)

            def made_plain(name, lhs, rhs, g, half):
                out = bank[len(made) % 6]
                before, value = made[-6]
                pe.wait_ge(S("rk_" + before), value)
                made.append((name, 2 * half + g + 1))
                mm(out[:, :], lhs, rhs[:, g, :], start=True, stop=True).then_inc(S("rk_mm"), 1)

            for m in range(9):
                project(m)
            pe.wait_ge(S("in2_raw"), 9)
            recurrence(0)
            pe.wait_ge(S("rk_d"), 2)
            for m in range(9, 15):
                project(m)
            pe.wait_ge(S("in2_raw"), 15)
            recurrence(1)
            pe.wait_ge(S("rk_d"), 4)
            for m in range(15, 23):
                project(m)
            for j in range(4):
                pe.wait_ge(S("conv"), 4 * (CONV_K - 1) + j + 1)
                if j == 0:
                    pe.wait_ge(S("in2_raw"), 19)
                last = mm(bank[0][:, :], const("mean512"), conv_out[:, j, :], start=j == 0, stop=j == 3)
            last.then_inc(S("conv_mean"), 1)
            for j in range(4):
                pe.wait_ge(S("conv_square"), j + 1)
                stat(bank[7], tmp[:, j % 2, :], const("ones"), j == 0, 1).then_inc(S("conv_stat"), 1)
            pe.wait_ge(S("conv_rs"), 1)
            spread(bank[6], n_rs, 1).then_inc(S("conv_spread"), 1)
            short("out2", "mid_a", 0, lambda k: pe.wait_ge(S("mix_split"), k + 1), "mixpost")

            for j in range(KD):
                norm_stats("ffnpre", j)
            norm_spread("ffnpre")
            at = SLAB_AT["up"]

            def up_pair(i, u, wait_k=None):
                for m in range(2):
                    n = 2 * u + m
                    pe.wait_ge(S("taps"), i * 4 + (n + 1))
                    product(bank[n], i * 4 + (at + n), (at + n) % RING, h_hi, h_lo,
                            wait_k=wait_k if m == 0 else None).then_inc(S("slab_done"), 1)

            up_pair(0, 0, after_norm("ffnpre"))
            up_pair(0, 1)
            with pe.Fori(1, KF // 2) as i:
                up_pair(i, 0)
                up_pair(i, 1)
            down("down3", 2 * KF, "mid_h", 0, "ffnpost")

        @block.scalar
        def _(act):
            f = nc.scalar.activation

            def norm_squares(name, src, wait=None):
                q = NORMS.index(name)
                for j in range(KD):
                    if wait is not None:
                        wait(j)
                    if 8 * q + j >= 2:
                        act.wait_ge(S("norm_stat"), 8 * q + j - 1)
                    f(tmp[:, j % 2, :], src[:, j, :], ACT.Square).then_inc(S("norm_square"), 1)
                act.wait_ge(S("norm_stat"), 8 * q + 8)
                f(n_std, bank[7][:, 0:4], ACT.Sqrt, bias=EPS, scale=1.0 / D).then_inc(S("norm_std"), 1)

            def norm_hi(name):
                for j in range(KD):
                    act.wait_ge(S("norm_t"), 8 * SCALED_AT[name] + j + 1)
                    if name in shf:
                        f(h_hi[:, j, :], tmp[:, 4 + j % 2, :], ACT.Identity, bias=shf[name][:, j:j + 1]).then_inc(S("norm_hi"), 1)
                    else:
                        f(h_hi[:, j, :], tmp[:, 4 + j % 2, :], ACT.Copy).then_inc(S("norm_hi"), 1)

            def gate_up(name, o):
                at = SLAB_AT[name]
                with act.Fori(0, KF // 2) as i:
                    for u in range(2):
                        act.wait_ge(S("slab_done"), i * 4 + (at + 2 * u + 2))
                        act.wait_ge(S("ff_product"), i * 2 + (o + u + 1))
                        f(tmp[:, 2 + u, :], bank[2 * u][:, :], ACT.Silu).then_inc(S("silu"), 1)

            act.wait_ge(S("tables_in"), 48)
            act.wait_ge(S("x_in"), 16)
            norm_squares("ffn1", xT)
            norm_hi("ffn1")
            f(silc, vec("c", 0, 8), ACT.Silu).then_inc(S("silu_c"), 1)
            gate_up("gu1", 0)
            norm_squares("mix", xT, lambda j: act.wait_ge(S("x_new"), j + 1))
            act.wait_ge(S("slab_done"), SLAB_AT["in1"])
            act.dma_start(rope, rope_in).then_inc(S("rope_in"), 16)
            for h in range(2):
                act.dma_start(relb[:, h, :], relb_in[h]).then_inc(S(f"relb_in{h}"), 16)
            for a in range(2):
                act.dma_start(adaw[:, a, :], ada_in[a]).then_inc(S(f"ada_in{a}"), 16)
            norm_hi("mix")

            raw = {"cq0": cq[:, 0, :], "cq1": cq[:, 1, :], "ckv0": ckv[:, 0, :], "kr0": kr[:, 0, :]}
            for j in range(4):
                raw |= {f"qa{j}": qa[:, j, :], f"ka{j}": ka[:, j, :], f"qn{j}": qn[:, j, :], f"kn{j}": kn[:, j, :]}
            raw |= {"qr0": qr[:, 0, :], "qr1": qr[:, 1, :]}
            for i, name in enumerate(IN1_RAW + LATENT_RAW):
                act.wait_ge(S("in1_raw"), i + 1 if i < 12 else i + 5)
                if i >= 2:
                    act.wait_ge(S("hd_stat"), i - 1)
                f(tmp[:, i % 2, :], raw[name], ACT.Square).then_inc(S("hd_square"), 1)
                if i == 3:
                    act.wait_ge(S("hd_stat"), 4)
                    f(hd_rs["lat"][:, 0:4], bank[7][:, 0:4], ACT.Sqrt, bias=EPS, scale=1.0 / 256).then_inc(S("hd_std"), 1)
                    f(hd_rs["lat"][:, 4:8], bank[7][:, 4:8], ACT.Sqrt, bias=EPS, scale=1.0 / 128).then_inc(S("hd_std"), 1)
                    f(hd_rs["lat"][:, 8:12], bank[7][:, 8:12], ACT.Sqrt, bias=EPS, scale=1.0 / 32).then_inc(S("hd_std"), 1)
                if i == 11:
                    act.wait_ge(S("hd_stat"), 12)
                    f(hd_rs["main"], bank[5][:, 0:64], ACT.Sqrt, bias=EPS, scale=1.0 / 64).then_inc(S("hd_std"), 1)
                if i == 21:
                    act.wait_ge(S("hd_stat"), 22)
                    up = hd_rs["up"]
                    f(up[:, 0:32], bank[7][:, 0:32], ACT.Sqrt, bias=EPS, scale=1.0 / 64).then_inc(S("hd_std"), 1)
                    f(up[:, 32:64], bank[7][:, 32:64], ACT.Sqrt, bias=EPS, scale=1.0 / 32).then_inc(S("hd_std"), 1)
                    f(up[:, 64:96], bank[7][:, 64:96], ACT.Sqrt, bias=EPS, scale=1.0 / 64).then_inc(S("hd_std"), 1)

            def softmax(s):
                h, q = divmod(s, NT)
                L = P * (q + 1)
                act.wait_ge(S("row_nmax"), s + 1)
                if s >= 3:
                    act.wait_ge(S("turned"), s - 2)
                if s >= 4:
                    act.wait_ge(S("probs_normed"), s - 3)
                src = prob[:, s % 3, 0:L] if h < 8 else bank[s % 3][:, 0:L]
                f(prob[:, s % 3, 0:L], src, ACT.Exp, bias=row_nmax[:, s % 4:s % 4 + 1],
                  accum_out=row_sum[:, s % 4:s % 4 + 1]).then_inc(S("probs"), 1)

            def keep_turned(s):
                h, q = divmod(s, NT)
                act.wait_ge(S("turned"), s + 1)
                if q == 0 and h >= 2:
                    act.wait_ge(S("values"), h - 1)
                n = NT * (h % 2)
                f(probT[:, n:n + q + 1, P * q:P * q + P],
                  bank[3 + s % 2][:, 0:P * (q + 1)].rearrange("p (k c) -> p k c", c=P), ACT.Copy).then_inc(S("probT"), 1)

            def out_hi(p):
                act.wait_ge(S("values"), 2 * p + 2)
                f(h_hi[:, p, :], bank[5 + p % 2][:, :], ACT.Copy).then_inc(S("o_hi"), 1)

            for s in range(16 * NT + 2):
                if s < 16 * NT:
                    softmax(s)
                if s >= 2:
                    keep_turned(s - 2)
                    h, q = divmod(s - 2, NT)
                    if q == 3 and h < 6:
                        act.wait_ge(S("row_nmax"), NT * (h + 1))
                        act.dma_start(relb[:, h % 2, :], relb_in[h + 2]).then_inc(S(f"relb_in{h % 2}"), 16)
                    if q >= 1:
                        a = 3 * h + q - 1
                        if a + 2 < 48:
                            act.wait_ge(S("ada_mm"), a + 1)
                            act.dma_start(adaw[:, a % 2, :], ada_in[a + 2]).then_inc(S(f"ada_in{a % 2}"), 16)
                    if q == 2 and h >= 2 and h % 2 == 0:
                        out_hi(h // 2 - 1)
            out_hi(7)
            norm_squares("ffn2", xT, lambda j: act.wait_ge(S("x_new"), 8 + j + 1))

            act.wait_ge(S("slab_done"), SLAB_AT["gu2"])
            act.dma_start(block2_t[:, :], block2_in).then_inc(S("block2_in"), 16)
            act.dma_start(g2b[0:32, :], g2b_in).then_inc(S("lora_in"), 16)
            norm_hi("ffn2")
            gate_up("gu2", KF)
            norm_squares("final", xT, lambda j: act.wait_ge(S("x_new"), 16 + j + 1))
            act.wait_ge(S("slab_done"), SLAB_AT["in2"])
            for i in range(2):
                act.dma_start(lora[:, i, :], lora_in[:, i, :]).then_inc(S("lora_in"), 16)
            norm_squares("mixpre", xT, lambda j: act.wait_ge(S("norm_lo"), 8 * 3 + j + 1))
            norm_hi("mixpre")

            def raw_in(m):
                act.wait_ge(S("slab_done"), SLAB_AT["in2"] + m + 1)
                if m >= 2:
                    act.wait_ge(S("in2_shifted"), m - 1)
                else:
                    act.wait_ge(S("shift_zero"), 1)
                f(shift[:, m % 2, 4:516], bank[m % 4][:, :], ACT.Copy).then_inc(S("in2_raw"), 1)

            moved = [0]

            def move(name, dst, g, half, n_before, scale=1.0):
                n = MADE * half + n_before
                act.wait_ge(S("rk_mm"), n + 1)
                f(dst[:, g, :], bank[n % 6][:, :], ACT.Copy, scale=scale).then_inc(S("rk_" + name), 1)

            def head_std(stat_name, v, done, eps, scale):
                act.wait_ge(S(stat_name), v)
                g = (v - 1) % 2
                f(rk_rs[:, 8 * g:8 * g + 8], bank[7][:, 0:8], ACT.Sqrt, bias=eps, scale=scale).then_inc(S(done), 1)

            def recurrence(half):
                for g in range(2):
                    G = 2 * half + g
                    for i, (dst, bias) in enumerate(((rk_w, "w0"), (rk_a, "a0"), (rk_g, None))):
                        act.wait_ge(S("lora_mm"), 3 * G + i + 1)
                        src = bank[4 + (3 * G + i) % 2][:, :]
                        if bias:
                            f(dst[:, g, :], src, ACT.Sigmoid, bias=vec(bias, G)).then_inc(S("lora_out"), 1)
                        else:
                            f(dst[:, g, :], src, ACT.Copy).then_inc(S("lora_out"), 1)
                for g in range(2):
                    v = 2 * half + g + 1
                    act.wait_ge(S("rk_kk"), v)
                    f(tmp[:, g, :], mP[:, g, :], ACT.Square).then_inc(S("rk_ksq"), 1)
                for g in range(2):
                    head_std("rk_kst", 2 * half + g + 1, "rk_rsd", 0.0, 1.0)
                for g in range(2):
                    v = 2 * half + g + 1
                    act.wait_ge(S("rk_cum"), v)
                    f(mMR[:, g, :], mO1[:, g, :], ACT.Exp, scale=-DECAY).then_inc(S("rk_exp"), 1)
                    f(mAR[:, g, :], mO1[:, g, :], ACT.Exp, scale=DECAY).then_inc(S("rk_exp"), 1)
                    f(tokQ[:, g, :], mO2[:, g, :], ACT.Exp, scale=-DECAY).then_inc(S("rk_exp"), 1)
                for g in range(2):
                    move("tv", tokV, g, half, 4 * g)
                    move("tk", tokK, g, half, 4 * g + 1)
                    move("tb", tokB, g, half, 4 * g + 2, scale=-1.0)
                    move("tq", tokQ, g, half, 4 * g + 3)
                for g in range(2):
                    act.wait_ge(S("rk_mm"), MADE * half + 18 + 2 * g + 2)
                    act.wait_ge(S("rk_r0"), 2 * half + g + 1)
                    move("q1", mQ, g, half, 18 + 2 * g)
                    move("p1", mP, g, half, 18 + 2 * g + 1)
                for g in range(2):
                    act.wait_ge(S("rk_mm"), MADE * half + 22 + 3 * g + 3)
                    move("q2", mQ, g, half, 22 + 3 * g + 1)
                    move("p2", mP, g, half, 22 + 3 * g + 2)
                for g in range(2):
                    act.wait_ge(S("rk_mm"), MADE * half + 28 + 2 * g + 2)
                    move("q3", mQ, g, half, 28 + 2 * g + 1)
                n = 34
                for lvl in (1, 2):
                    for g in range(2):
                        act.wait_ge(S("rk_" + ("r3" if lvl == 1 else "r4")), 2 * half + g + 1)
                        move(f"rt{lvl}", mP, g, half, n + 2 * g)
                        move(f"y{lvl}", mQ, g, half, n + 2 * g + 1)
                    n += 6
                for g in range(2):
                    move("x", mX, g, half, n + 2 * g)
                    move("w", mW, g, half, n + 2 * g + 1)
                n += 4
                for g in range(2):
                    move("z", mZ, g, half, n + 2 * g)
                n += 8
                for g in range(2):
                    move("y", mP, g, half, n + g)
                for g in range(2):
                    move("d", mQ, g, half, n + 2 + g)
                    act.wait_ge(S("rk_d"), 2 * half + g + 1)
                    f(tmp[:, g, :], mQ[:, g, :], ACT.Square).then_inc(S("rk_dsq"), 1)
                    head_std("rk_dst", 2 * half + g + 1, "rk_dstd", 64e-5, 1.0 / 64)

            for m in range(9):
                raw_in(m)
                if m == 3:
                    act.wait_ge(S("in2_shifted"), 3)
                    f(lora_act[0:CH, 0, :], lora_act[0:CH, 0, :], ACT.Tanh).then_inc(S("lora_act"), 1)
                    f(lora_act[:, 1, :], lora_act[:, 1, :], ACT.Sigmoid).then_inc(S("lora_act"), 1)
                    f(lora_act2[0:32, :], lora_act2[0:32, :], ACT.Sigmoid).then_inc(S("lora_act"), 1)
            recurrence(0)
            for m in range(9, 15):
                raw_in(m)
            recurrence(1)

            for j in range(4):
                act.wait_ge(S("slab_done"), SLAB_AT["in2"] + 15 + 2 * j + 2)
                if j >= 2:
                    act.wait_ge(S("in2_raw"), 15 + j - 1)
                f(conv_gate[:, j % 2, :], bank[(15 + 2 * j + 1) % 4][:, :], ACT.Sigmoid).then_inc(S("conv_gate"), 1)
            for j in range(4):
                act.wait_ge(S("conv_d"), j + 1)
                if j >= 2:
                    act.wait_ge(S("conv_stat"), j - 1)
                f(tmp[:, j % 2, :], conv_out[:, j, :], ACT.Square).then_inc(S("conv_square"), 1)
            act.wait_ge(S("conv_stat"), 4)
            f(n_std, bank[7][:, 0:4], ACT.Sqrt, bias=1e-5, scale=1.0 / 512).then_inc(S("conv_std"), 1)
            for j in range(4):
                act.wait_ge(S("conv_t"), j + 1)
                f(conv_out[:, j, :], conv_out[:, j, :], ACT.Silu, bias=vec("conv_ln_b", j)).then_inc(S("conv_silu"), 1)
            norm_squares("mixpost", mid_a, lambda j: act.wait_ge(S("mid_a"), j + 1))

            norm_squares("ffnpre", xT, lambda j: act.wait_ge(S("norm_lo"), 8 * 5 + j + 1))
            norm_hi("ffnpre")
            with act.Fori(0, KF // 2) as i:
                for u in range(2):
                    act.wait_ge(S("up_product"), i * 2 + (u + 1))
                    for m in range(2):
                        n = 2 * u + m
                        act.wait_ge(S("slab_done"), i * 4 + (SLAB_AT["up"] + n + 1))
                        w2 = vec_t[:, bass.ds(i * 12 + (VEC_AT["ffn_dw_w"] + 3 * n + 2), 1)]
                        b = vec_t[:, bass.ds(i * 4 + (VEC_AT["ffn_dw_b"] + n), 1)]
                        f(tmp[:, n, :], bank[n][:, :], ACT.Identity, bias=b, scale=w2).then_inc(S("tap2"), 1)
                    act.wait_ge(S("taps"), i * 4 + (4 + 2 * u + 1))
                    f(tmp[:, 2 * u, :], tmp[:, 2 * u, :], ACT.Silu).then_inc(S("up_silu"), 1)
            norm_squares("ffnpost", mid_h, lambda j: act.wait_ge(S("mid_h"), j + 1))

        @block.vector
        def _(dve):
            v = nc.vector
            step = [0]

            def link(ins):
                step[0] += 1
                ins.then_inc(S("vector_step"), 1)
                dve.wait_ge(S("vector_step"), step[0])

            def norm_rs(name):
                q = NORMS.index(name)
                dve.wait_ge(S("norm_std"), q + 1)
                v.reciprocal(n_rs, n_std).then_inc(S("norm_rs"), 1)
                dve.wait_ge(S("norm_spread"), q + 1)

            def norm_split(name, gain):
                norm_rs(name)

                def lo(j):
                    dve.wait_ge(S("norm_hi"), 8 * HI_AT[name] + j + 1)
                    t = tmp[:, 4 + j % 2, :]
                    if name in shf:
                        v.scalar_tensor_tensor(out=h_lo[:, j, :], in0=t, scalar=shf[name][:, j:j + 1], in1=h_hi[:, j, :],
                                               op0=ALU.add, op1=ALU.subtract).then_inc(S("norm_lo"), 1)
                    else:
                        v.tensor_tensor(h_lo[:, j, :], t, h_hi[:, j, :], ALU.subtract).then_inc(S("norm_lo"), 1)

                for j in range(KD):
                    if j >= 2:
                        lo(j - 2)
                        dve.wait_ge(S("norm_lo"), 8 * NORMS.index(name) + j - 1)
                    v.scalar_tensor_tensor(out=tmp[:, 4 + j % 2, :], in0=xT[:, j, :], scalar=gain[:, j:j + 1], in1=bank[6][:, :],
                                           op0=ALU.mult, op1=ALU.mult).then_inc(S("norm_t"), 1)
                lo(KD - 2)
                lo(KD - 1)

            def norm_add(name, src):
                norm_rs(name)
                for j in range(KD):
                    v.scalar_tensor_tensor(out=src[:, j, :], in0=src[:, j, :], scalar=gp[name][:, j:j + 1], in1=bank[6][:, :],
                                           op0=ALU.mult, op1=ALU.mult).then_inc(S("norm_t"), 1)
                    dve.wait_ge(S("norm_t"), 8 * SCALED_AT[name] + j + 1)
                    v.tensor_tensor(xT[:, j, :], xT[:, j, :], src[:, j, :], ALU.add).then_inc(S("norm_lo"), 1)

            def hidden(i, u, o, product):
                t = tmp[:, 4 + u, :]
                at = i * 2 + u
                dve.wait_ge(S(product), i * 2 + ((o if product == "ff_product" else 0) + u + 3))
                hi = acth_t[:, bass.ds(at * T, T)]
                v.tensor_copy(hi, t).then_inc(S("act_hi"), 1)
                dve.wait_ge(S("act_hi"), i * 2 + (o + u + 1))
                v.tensor_tensor(actl_t[:, bass.ds(at * T, T)], t, hi, ALU.subtract).then_inc(S("act_lo"), 1)

            def gate_up(name, o):
                with dve.Fori(0, KF // 2) as i:
                    for u in range(2):
                        dve.wait_ge(S("silu"), i * 2 + (o + u + 1))
                        dve.wait_ge(S("act_lo"), i * 2 + (o + u + 1))
                        v.tensor_tensor(tmp[:, 4 + u, :], tmp[:, 2 + u, :], bank[2 * u + 1][:, :], ALU.mult)\
                            .then_inc(S("ff_product"), 1)
                        hidden(i, u, o, "ff_product")

            def add_half(o, at, n_slabs, scale):
                for m in range(KD):
                    dve.wait_ge(S("slab_done"), at + n_slabs * (m + 1))
                    v.scalar_tensor_tensor(out=xT[:, m, :], in0=bank[m % 4][:, :], scalar=scale, in1=xT[:, m, :],
                                           op0=ALU.mult, op1=ALU.add).then_inc(S("x_new"), 1)

            for name, n in (("ff_product", 2), ("act_lo", 2), ("taps", 4), ("up_product", 2)):
                for _ in range(n):
                    v.memset(small_t[:, 255:256], 0.0).then_inc(S(name), 1)
                    dve.wait_ge(S(name), _ + 1)

            dve.wait_ge(S("tables_in"), 48)
            dve.wait_ge(S("x_in"), 16)
            norm_split("ffn1", vec("ffn1_norm", 0, 8))
            gate_up("gu1", 0)
            add_half(0, SLAB_AT["down1"], 3, 0.5)
            norm_split("mix", vec("mix_norm", 0, 8))

            applied = [0]

            def apply(dst, gain, scale=None):
                r = applied[0]
                dve.wait_ge(S("hd_spread"), r + 1)
                ins = v.scalar_tensor_tensor(out=dst, in0=dst, scalar=gain, in1=bank[6 if r % 2 == 0 else 4][:, :],
                                             op0=ALU.mult, op1=ALU.mult)
                applied[0] += 1
                return ins

            def split_latent(src, hi, lo):
                link(v.tensor_copy(hi, src))
                v.tensor_tensor(lo, src, hi, ALU.subtract).then_inc(S("cq_split"), 1)

            dest = [cq[:, 0, :], cq[:, 1, :], ckv[:, 0, :], kr[:, 0, :]] + [qa[:, j, :] for j in range(4)] + \
                   [ka[:, j, :] for j in range(4)]
            link(v.tensor_scalar(row_max[:, 0:1], vec("a_q_norm"), 64.0 ** -0.5, None, ALU.mult))
            link(v.tensor_scalar(row_max[:, 1:2], vec("b_q_nope_norm"), 96.0 ** -0.5, None, ALU.mult))
            link(v.tensor_scalar(row_max[:, 2:3], vec("b_q_rope_norm"), 96.0 ** -0.5, None, ALU.mult))
            for m in range(16):
                dve.wait_ge(S("slab_done"), SLAB_AT["in1"] + m + 1)
                if m < 12:
                    v.tensor_copy(dest[m], bank[m % 4][:, :]).then_inc(S("in1_raw"), 1)
                else:
                    j = m - 12
                    v.tensor_copy(va[:, :, P * j:P * j + P], bank[m % 4][:, :].rearrange("p (t c) -> p t c", c=P))\
                        .then_inc(S("in1_raw"), 1)
                if m == 5:
                    dve.wait_ge(S("hd_std"), 3)
                    v.reciprocal(hd_rs["lat"], hd_rs["lat"]).then_inc(S("hd_rs"), 1)
                if m == 6:
                    dve.wait_ge(S("hd_spread"), 1)
                    link(v.scalar_tensor_tensor(out=cq[:, 0, :], in0=cq[:, 0, :], scalar=vec("b_q_lat_norm", 0),
                                                in1=bank[6][:, :], op0=ALU.mult, op1=ALU.mult))
                    apply(cq[:, 1, :], vec("b_q_lat_norm", 1)).then_inc(S("hd_applied"), 1)
                    dve.wait_ge(S("hd_applied"), 1)
                    for k in range(2):
                        split_latent(cq[:, k, :], cq_hi[:, k, :], cq_lo[:, k, :])
                    apply(ckv[:, 0, :], vec("b_kv_lat_norm")).then_inc(S("hd_applied"), 1)
                    dve.wait_ge(S("hd_applied"), 2)
                    split_latent(ckv[:, 0, :], ckv_hi[:, 0, :], ckv_lo[:, 0, :])
                if m == 8:
                    apply(kr[:, 0, :], vec("b_k_rope_norm")).then_inc(S("hd_applied"), 1)
                if m == 14:
                    dve.wait_ge(S("hd_std"), 4)
                    v.reciprocal(hd_rs["main"], hd_rs["main"]).then_inc(S("hd_rs"), 1)
            raw2 = [qn[:, j, :] for j in range(4)] + [qr[:, j, :] for j in range(2)] + [kn[:, j, :] for j in range(4)]
            latent_mm = 0
            for t in range(14):
                if t in (2, 5, 13):
                    dve.wait_ge(S("slab_done"), SLAB_AT["uq"] + (2, 5, 13).index(t) + 1)
                else:
                    latent_mm += 1
                    dve.wait_ge(S("latent_mm"), latent_mm)
                if t < 10:
                    v.tensor_copy(raw2[t], bank[t % 4][:, :]).then_inc(S("in1_raw"), 1)
                else:
                    j = t - 10
                    v.tensor_copy(vb[:, :, P * j:P * j + P], bank[t % 4][:, :].rearrange("p (t c) -> p t c", c=P))\
                        .then_inc(S("in1_raw"), 1)
            dve.wait_ge(S("hd_std"), 7)
            v.reciprocal(hd_rs["up"], hd_rs["up"]).then_inc(S("hd_rs"), 1)
            for j in range(4):
                apply(qa[:, j, :], row_max[:, 0:1]).then_inc(S("hd_applied"), 1)
            for j in range(4):
                apply(ka[:, j, :], vec("a_k_norm")).then_inc(S("hd_applied"), 1)
            for j in range(4):
                apply(qn[:, j, :], row_max[:, 1:2]).then_inc(S("hd_applied"), 1)
            for j in range(2):
                apply(qr[:, j, :], row_max[:, 2:3]).then_inc(S("hd_applied"), 1)
            for j in range(4):
                apply(kn[:, j, :], vec("b_k_nope_norm")).then_inc(S("hd_applied"), 1)
            dve.wait_ge(S("rope_in"), 16)
            for j, m in enumerate((qr[:, 0, :], qr[:, 1, :], kr[:, 0, :])):
                dve.wait_ge(S("swapped"), j + 1)
                link(v.tensor_tensor(m, m, rope[:, 0, :], ALU.mult))
                link(v.tensor_tensor(tmp[:, 4, :], bank[j][:, :], rope[:, 1, :], ALU.mult))
                v.tensor_tensor(m, m, tmp[:, 4, :], ALU.add).then_inc(S("roped"), 1)
                dve.wait_ge(S("roped"), j + 1)

            def score_max(s):
                h, q = divmod(s, NT)
                L, c = P * (q + 1), s % 4
                dve.wait_ge(S("scores"), s + 1)
                if s >= 4:
                    dve.wait_ge(S("probs"), s - 3)
                if h < 8:
                    if q == 0:
                        dve.wait_ge(S(f"relb_in{h % 2}"), 16 * (h // 2 + 1))
                    if s >= 3:
                        dve.wait_ge(S("turned"), s - 2)
                    link(v.tensor_tensor_reduce(out=prob[:, s % 3, 0:L], in0=bank[s % 3][:, 0:L],
                                                in1=relb[:, h % 2, T - L:T], scale=1.0, scalar=LOWEST,
                                                op0=ALU.add, op1=ALU.max, accum_out=row_max[:, c:c + 1]))
                    v.tensor_scalar(row_nmax[:, c:c + 1], row_max[:, c:c + 1], -1.0, None, ALU.mult).then_inc(S("row_nmax"), 1)
                else:
                    v.tensor_reduce(row_nmax[:, c:c + 1], bank[s % 3][:, 0:L], AXX, ALU.max, negate=True)\
                        .then_inc(S("row_nmax"), 1)

            def normalise(s):
                L, c = P * (s % NT + 1), s % 4
                dve.wait_ge(S("probs"), s + 1)
                link(v.reciprocal(row_sum[:, c:c + 1], row_sum[:, c:c + 1]))
                v.tensor_scalar(prob[:, s % 3, 0:L], prob[:, s % 3, 0:L], row_sum[:, c:c + 1], None, ALU.mult)\
                    .then_inc(S("probs_normed"), 1)

            def out_lo(p):
                dve.wait_ge(S("o_hi"), p + 1)
                v.tensor_tensor(h_lo[:, p, :], bank[5 + p % 2][:, :], h_hi[:, p, :], ALU.subtract).then_inc(S("o_lo"), 1)

            for s in range(16 * NT + 3):
                if s < 16 * NT:
                    score_max(s)
                if 1 <= s <= 16 * NT:
                    normalise(s - 1)
                if s >= 3:
                    h, q = divmod(s - 3, NT)
                    if q == 2 and h >= 2 and h % 2 == 0:
                        out_lo(h // 2 - 1)
            out_lo(7)
            dve.wait_ge(S("ada_mm"), 48)
            link(v.tensor_tensor(mod, bank[7][:, 0:48], vec("ada_b", 0, 48), ALU.add))
            v.scalar_tensor_tensor(out=gs["mixpre"], in0=mod[:, 8:16], scalar=1.0, in1=vec("mix_pre_g", 0, 8),
                                   op0=ALU.add, op1=ALU.mult)
            v.scalar_tensor_tensor(out=gs["ffnpre"], in0=mod[:, 32:40], scalar=1.0, in1=vec("ffn_pre_g", 0, 8),
                                   op0=ALU.add, op1=ALU.mult)
            v.tensor_tensor(gp["mixpost"], mod[:, 16:24], vec("mix_post_g", 0, 8), ALU.mult)
            v.tensor_tensor(gp["ffnpost"], mod[:, 40:48], vec("ffn_post_g", 0, 8), ALU.mult).then_inc(S("mod_ready"), 1)
            add_half(8, SLAB_AT["out1"], 1, 1.0)

            norm_split("ffn2", vec("ffn2_norm", 0, 8))
            gate_up("gu2", KF)
            add_half(16, SLAB_AT["down2"], 3, 0.5)
            norm_rs("final")
            for j in range(KD):
                v.scalar_tensor_tensor(out=xT[:, j, :], in0=xT[:, j, :], scalar=vec("final_norm", j), in1=bank[6][:, :],
                                       op0=ALU.mult, op1=ALU.mult).then_inc(S("norm_lo"), 1)

            dve.wait_ge(S("block2_in"), 16)
            norm_split("mixpre", gs["mixpre"])
            v.memset(tmp_t[:, 2 * T:2 * T + 4], 0.0)
            v.memset(tmp_t[:, 2 * T + 516:2 * T + 520], 0.0).then_inc(S("shift_zero"), 1)
            link(v.tensor_scalar(omka, vec("k_a", 0, 4), -1.0, 1.0, ALU.mult, ALU.add))

            def shifted(m, dst, rows_=slice(0, P)):
                raw = shift[:, m % 2, :]
                dve.wait_ge(S("in2_raw"), m + 1)
                link(v.tensor_tensor(dst, raw[rows_, 3:515], raw[rows_, 4:516], ALU.subtract))
                v.scalar_tensor_tensor(out=dst, in0=dst, scalar=vec("mu", m)[rows_, :], in1=raw[rows_, 4:516],
                                       op0=ALU.mult, op1=ALU.add).then_inc(S("in2_shifted"), 1)

            def move(name, half, n_before, g, ins):
                n = MADE * half + n_before
                dve.wait_ge(S("rk_mm"), n + 1)
                ins(bank[n % 6]).then_inc(S("rk_" + name), 1)

            def masked(dst, src, mask, g):
                return v.tensor_tensor(rows(dst, g), src[:, :].rearrange("p (c t) -> p c t", c=NC), every_chunk(const(mask)), ALU.mult)

            def recurrence(half):
                m0 = 3 + 6 * half
                for i, dst in enumerate((rk_r, rk_k, rk_v)):
                    for g in range(2):
                        shifted(m0 + 2 * i + g, dst[:, g, :])
                n0 = 2 * half
                for g in range(2):
                    G = n0 + g
                    dve.wait_ge(S("in2_shifted"), m0 + 6)
                    v.tensor_scalar(mP[:, g, :], rk_k[:, g, :], vec("k_k", G), None, ALU.mult).then_inc(S("rk_kk"), 1)
                    dve.wait_ge(S("lora_out"), 3 * G + 3)
                    link(v.tensor_scalar(mQ[:, g, :], rk_a[:, g, :], vec("k_a", G), omka[:, G:G + 1], ALU.mult, ALU.add))
                    link(v.tensor_tensor(rk_k[:, g, :], rk_k[:, g, :], mQ[:, g, :], ALU.mult))
                    v.scalar_tensor_tensor(out=mR[:, g, :], in0=rk_r[:, g, :], scalar=vec("r_k", G), in1=rk_k[:, g, :],
                                           op0=ALU.mult, op1=ALU.mult).then_inc(S("rk_bz"), 1)
                    link(v.tensor_tensor_scan(mO1[:, g, :], const("keep"), rk_w[:, g, :], 0.0, ALU.mult, ALU.add))
                    v.tensor_tensor(mO2[:, g, :], mO1[:, g, :], rk_w[:, g, :], ALU.subtract).then_inc(S("rk_cum"), 1)
                for g in range(2):
                    r = rk_rs[:, 8 * g:8 * g + 8]
                    dve.wait_ge(S("rk_rsd"), n0 + g + 1)
                    link(v.tensor_scalar(r, r, 1e-12, None, ALU.max))
                    v.reciprocal(r, r).then_inc(S("rk_krs"), 1)
                for g in range(2):
                    dve.wait_ge(S("rk_kspread"), n0 + g + 1)
                    link(v.tensor_tensor(mP[:, g, :], mP[:, g, :], bank[6][:, :], ALU.mult))
                    dve.wait_ge(S("rk_bsum"), n0 + g + 1)
                    v.tensor_tensor(rk_b[:, g, :], rk_v[:, g, :], bank[7][:, :], ALU.mult).then_inc(S("rk_bonus"), 1)
                for g in range(2):
                    dve.wait_ge(S("rk_exp"), 3 * (n0 + g) + 3)
                    link(v.tensor_tensor(rk_a[:, g, :], rk_a[:, g, :], mP[:, g, :], ALU.mult))
                    v.tensor_tensor(rk_a[:, g, :], rk_a[:, g, :], mAR[:, g, :], ALU.mult)
                    v.tensor_tensor(rk_k[:, g, :], rk_k[:, g, :], mAR[:, g, :], ALU.mult)
                    v.tensor_tensor(rk_r[:, g, :], rk_r[:, g, :], mMR[:, g, :], ALU.mult)
                    v.tensor_copy(d_end[:, 8 * g:8 * g + 8], rows(mMR, g)[:, :, CH - 1])
                    v.tensor_tensor(rk_w[:, g, :], mP[:, g, :], tokQ[:, g, :], ALU.mult).then_inc(S("rk_factors"), 1)
                for g in range(2):
                    move("p0", half, 8 + 5 * g, g, lambda b: masked(mP, b, "np0", g))
                    dve.wait_ge(S("rk_p0"), n0 + g + 1)
                    v.tensor_tensor(rows(mR, g), rows(mP, g), every_chunk(const("eye64")), ALU.add).then_inc(S("rk_r0"), 1)
                    n = MADE * half + 8 + 5 * g + 1
                    dve.wait_ge(S("rk_mm"), n + 1)
                    masked(mO1, bank[n % 6], "off32", g)
                    masked(mO2, bank[n % 6], "off64", g)
                    masked(mQ, bank[n % 6], "nq0", g).then_inc(S("rk_q0"), 1)
                    move("mt", half, 8 + 5 * g + 2, g, lambda b: masked(mMT, b, "su", g))
                    move("ar", half, 8 + 5 * g + 3, g, lambda b: masked(mAR, b, "niu", g))
                    move("mr", half, 8 + 5 * g + 4, g, lambda b: masked(mMR, b, "iu", g))

                def add_r(name, n_before, g, op=ALU.add):
                    move(name, half, n_before, g, lambda b: v.tensor_tensor(mR[:, g, :], mR[:, g, :], b[:, :], op))

                for g in range(2):
                    dve.wait_ge(S("rk_r0"), n0 + g + 1)
                    add_r("r1", 22 + 3 * g, g)
                for g in range(2):
                    dve.wait_ge(S("rk_r1"), n0 + g + 1)
                    add_r("r2", 28 + 2 * g, g)
                for g in range(2):
                    dve.wait_ge(S("rk_r2"), n0 + g + 1)
                    add_r("r3", 32 + g, g)
                n = 34
                for lvl in (1, 2):
                    for g in range(2):
                        dve.wait_ge(S("rk_r3" if lvl == 1 else "rk_r4"), n0 + g + 1)
                        add_r("r4" if lvl == 1 else "r5", n + 4 + g, g, ALU.subtract)
                    n += 6
                n += 4
                for g in range(2):
                    move("g", half, n + 2 * g + 1, g,
                         lambda b: v.tensor_tensor(rows(mG, g), b[:, :].rearrange("p (c t) -> p c t", c=NC),
                                                   every_chunk(const("eye64")), ALU.add))
                n += 4
                for g in range(2):
                    de = d_end[:, 8 * g:8 * g + 8].unsqueeze(2).to_broadcast([P, NC, CH])
                    move("hd", half, n + 2 * g, g,
                         lambda b: v.tensor_tensor(rows(mHD, g), b[:, :].rearrange("p (c t) -> p c t", c=NC), de, ALU.mult))
                    move("rho", half, n + 2 * g + 1, g,
                         lambda b: v.tensor_tensor(rk_r[:, g, :], rk_r[:, g, :], b[:, :], ALU.add))
                n += 4
                for c in range(1, NC - 1):
                    for g in range(2):
                        dve.wait_ge(S(f"rk_step{g}"), (NC - 2) * half + c)
                        dve.wait_ge(S("rk_hd"), n0 + g + 1)
                        v.scalar_tensor_tensor(out=mS[:, g, CH * (c + 1):CH * (c + 2)], in0=bank[6 + g][:, CH * c:CH * c + CH],
                                               scalar=d_end[:, 8 * g + c:8 * g + c + 1], in1=mHD[:, g, CH * c:CH * c + CH],
                                               op0=ALU.mult, op1=ALU.add).then_inc(S(f"rk_state{g}"), 1)
                out = y_keep if half == 0 else rk_b
                for g in range(2):
                    G = n0 + g
                    r = rk_rs[:, 8 * g:8 * g + 8]
                    dve.wait_ge(S("rk_dstd"), G + 1)
                    v.reciprocal(r, r).then_inc(S("rk_drs"), 1)
                    dve.wait_ge(S("rk_dspread"), G + 1)
                    link(v.scalar_tensor_tensor(out=mP[:, g, :], in0=mQ[:, g, :], scalar=vec("lnx_g", G), in1=bank[6][:, :],
                                                op0=ALU.mult, op1=ALU.mult))
                    link(v.scalar_tensor_tensor(out=mP[:, g, :], in0=mP[:, g, :], scalar=vec("lnx_b", G), in1=rk_b[:, g, :],
                                                op0=ALU.add, op1=ALU.add))
                    v.tensor_tensor(out[:, g, :], mP[:, g, :], rk_g[:, g, :], ALU.mult).then_inc(S("rk_out"), 1)

            shifted(0, lora_act[:, 0, :])
            shifted(1, lora_act[:, 1, :])
            shifted(2, lora_act2[0:32, :], slice(0, 32))
            recurrence(0)
            recurrence(1)

            dve.wait_ge(S("rk_out"), 4)
            for j in range(4):
                link(v.memset(conv_in[:, j, 0:32], 0.0))
            for j in range(4):
                dve.wait_ge(S("conv_gate"), j + 1)
                v.tensor_tensor(conv_in[:, j, 32:], conv_gate[:, j % 2, :], bank[(15 + 2 * j) % 4][:, :], ALU.mult)\
                    .then_inc(S("in2_raw"), 1)
            for k in range(CONV_K):
                for j in range(4):
                    w, src = vec("conv_w", CONV_K * j + k), conv_in[:, j, 2 + k:2 + k + T]
                    if k == 0:
                        dve.wait_ge(S("in2_raw"), 15 + j + 1)
                        v.tensor_scalar(conv_out[:, j, :], src, w, vec("conv_b", j), ALU.mult, ALU.add).then_inc(S("conv"), 1)
                        continue
                    dve.wait_ge(S("conv"), 4 * (k - 1) + j + 1)
                    v.scalar_tensor_tensor(out=conv_out[:, j, :], in0=src, scalar=w, in1=conv_out[:, j, :],
                                           op0=ALU.mult, op1=ALU.add).then_inc(S("conv"), 1)
            dve.wait_ge(S("conv_mean"), 1)
            for j in range(4):
                dve.wait_ge(S("conv"), 4 * (CONV_K - 1) + j + 1)
                v.tensor_tensor(conv_out[:, j, :], conv_out[:, j, :], bank[0][:, :], ALU.subtract).then_inc(S("conv_d"), 1)
            dve.wait_ge(S("conv_std"), 1)
            v.reciprocal(n_rs, n_std).then_inc(S("conv_rs"), 1)
            dve.wait_ge(S("conv_spread"), 1)
            for j in range(4):
                dve.wait_ge(S("conv_d"), j + 1)
                v.scalar_tensor_tensor(out=conv_out[:, j, :], in0=conv_out[:, j, :], scalar=vec("conv_ln_g", j),
                                       in1=bank[6][:, :], op0=ALU.mult, op1=ALU.mult).then_inc(S("conv_t"), 1)
            dve.wait_ge(S("slab_done"), SLAB_AT["out2"])
            for j in range(8):
                if j < 4:
                    dve.wait_ge(S("conv_silu"), j + 1)
                src = conv_out[:, j, :] if j < 4 else (y_keep if j < 6 else rk_b)[:, j % 2, :]
                link(v.tensor_copy(h_hi[:, j, :], src))
                v.tensor_tensor(h_lo[:, j, :], src, h_hi[:, j, :], ALU.subtract).then_inc(S("mix_split"), 1)
            for m in range(KD):
                dve.wait_ge(S("slab_done"), SLAB_AT["out2"] + m + 1)
                v.tensor_copy(mid_a[:, m, :], bank[m % 4][:, :]).then_inc(S("mid_a"), 1)
            norm_add("mixpost", mid_a)

            norm_split("ffnpre", gs["ffnpre"])
            with dve.Fori(0, KF // 2) as i:
                for u in range(2):
                    for m in range(2):
                        n = 2 * u + m
                        w = [vec_t[:, bass.ds(i * 12 + (VEC_AT["ffn_dw_w"] + 3 * n + k), 1)] for k in range(2)]
                        dve.wait_ge(S("tap2"), i * 4 + (n + 1))
                        v.scalar_tensor_tensor(out=tmp[:, n, 1:T], in0=bank[n][:, 0:T - 1], scalar=w[1], in1=tmp[:, n, 1:T],
                                               op0=ALU.mult, op1=ALU.add).then_inc(S("tap1"), 1)
                        dve.wait_ge(S("tap1"), i * 4 + (n + 1))
                        v.scalar_tensor_tensor(out=tmp[:, n, 2:T], in0=bank[n][:, 0:T - 2], scalar=w[0], in1=tmp[:, n, 2:T],
                                               op0=ALU.mult, op1=ALU.add).then_inc(S("taps"), 1)
                    dve.wait_ge(S("up_silu"), i * 2 + (u + 1))
                    dve.wait_ge(S("taps"), i * 4 + (4 + 2 * u + 2))
                    dve.wait_ge(S("act_lo"), i * 2 + (2 * KF + u + 1))
                    v.tensor_tensor(tmp[:, 4 + u, :], tmp[:, 2 * u, :], tmp[:, 2 * u + 1, :], ALU.mult).then_inc(S("up_product"), 1)
                    hidden(i, u, 2 * KF, "up_product")
            for m in range(KD):
                dve.wait_ge(S("slab_done"), SLAB_AT["down3"] + 3 * (m + 1))
                v.tensor_copy(mid_h[:, m, :], bank[m % 4][:, :]).then_inc(S("mid_h"), 1)
            norm_add("ffnpost", mid_h)


def _columns(v, n):
    return np.ascontiguousarray(np.asarray(v).reshape(n, P).T)


def _slabs(w, order=None):
    k, m = w.shape[0] // P, w.shape[1] // P
    return w.reshape(k, P, m, P).transpose(2, 1, 0, 3).reshape(m, P, k * P)


def _layout(inp):
    g = {k: np.asarray(v) for k, v in inp.items()}
    w = {k: v[0] for k, v in g.items() if k != "x" and k != "c_2"}

    def padded(a):
        out = np.zeros((a.shape[0], P, SLAB), np.float32)
        out[:, :, :a.shape[2]] = a
        return out

    def gate_up(a, b):
        return np.stack([_slabs(a), _slabs(b)], 1).reshape(2 * KF, P, SLAB)

    def down(a):
        s = _slabs(a)
        return np.concatenate([padded(s[:, :, P * k0:P * k1])[:, None] for k0, k1 in DOWN_CUT], 1).reshape(24, P, SLAB)

    win = w["w_in"]
    kr = win[:, 1920:1952]
    in1 = np.concatenate([win[:, 1536:1920], kr, kr, kr, kr, win[:, 0:1536]], 1)
    uq = w["b_w_uq"].reshape(256, 8, 96)
    uq = np.concatenate([uq[:, :, :64].reshape(256, 512), uq[:, :, 64:].reshape(256, 256)], 1)
    uq = padded(_slabs(uq).reshape(2, 3, P, 2 * P).transpose(0, 2, 1, 3).reshape(2, P, 6 * P))
    ukv = w["b_w_ukv"].reshape(P, 8, 128)
    ukv = np.concatenate([ukv[:, :, :64].reshape(P, 512), ukv[:, :, 64:].reshape(P, 512)], 1)[None]
    w2 = w["w_in_2"]
    rw, zero = w2[:, 1024:], np.zeros((D, 96), np.float32)
    cols = [rw[:, 1536:1664], rw[:, 1664:1792], np.concatenate([rw[:, 1792:1824], zero], 1)]
    mu = w["rwkv_mu_2"]
    mus = [mu[1536:1664], mu[1664:1792], np.concatenate([mu[1792:1824], zero[0]])]
    for half in range(2):
        for i in range(3):
            a = 512 * i + 256 * half
            cols.append(rw[:, a:a + 256])
            mus.append(mu[a:a + 256])
    for j in range(4):
        cols += [w2[:, P * j:P * j + P], w2[:, 512 + P * j:512 + P * j + P]]
    slabs = np.concatenate([
        gate_up(w["ffn1_w_gate"], w["ffn1_w_up"]), down(w["ffn1_w_down"]), _slabs(in1), uq, ukv, _slabs(w["w_out"]),
        gate_up(w["ffn2_w_gate"], w["ffn2_w_up"]), down(w["ffn2_w_down"]), _slabs(np.concatenate(cols, 1)),
        _slabs(w["w_out_2"]), gate_up(w["w_up_2"][:, :DFF], w["w_up_2"][:, DFF:]), down(w["w_down_2"]),
        np.zeros((N_LOADS - N_SLABS, P, SLAB), np.float32)])
    pair = lambda v, n: _columns(np.tile(v, n), 1)
    dw = w["ffn_dw_w_2"].reshape(3, 2, KF, P).transpose(3, 2, 1, 0).reshape(P, 6 * KF)
    db = w["ffn_dw_b_2"].reshape(2, KF, P).transpose(2, 1, 0).reshape(P, 2 * KF)
    v = {"ffn1_norm": _columns(w["ffn1_norm"], 8), "mix_norm": _columns(w["mix_norm"], 8),
         "a_q_norm": pair(w["a_q_norm"], 2), "a_k_norm": pair(w["a_k_norm"], 2),
         "b_q_lat_norm": _columns(w["b_q_lat_norm"], 2), "b_kv_lat_norm": _columns(w["b_kv_lat_norm"], 1),
         "b_q_nope_norm": pair(w["b_q_nope_norm"], 2), "b_q_rope_norm": pair(w["b_q_rope_norm"], 4),
         "b_k_nope_norm": pair(w["b_k_nope_norm"], 2), "b_k_rope_norm": pair(w["b_k_rope_norm"], 4),
         "ffn2_norm": _columns(w["ffn2_norm"], 8), "final_norm": _columns(w["final_norm"], 8),
         "c": _columns(g["c_2"][0], 8), "ada_b": _columns(w["ada_b_2"], 48),
         "mix_pre_g": _columns(w["mix_pre_g_2"], 8), "mix_post_g": _columns(w["mix_post_g_2"], 8),
         "conv_w": w["conv_dw_w_2"].reshape(CONV_K, 4, P).transpose(2, 1, 0).reshape(P, 4 * CONV_K),
         "mu": _columns(np.concatenate(mus), 15), "ffn_dw_w": dw, "ffn_dw_b": db,
         "r_k": _columns(w["r_k_2"].reshape(-1), 4),
         "ffn_pre_g": _columns(w["ffn_pre_g_2"], 8), "ffn_post_g": _columns(w["ffn_post_g_2"], 8)}
    for k, name in (("conv_b", "conv_dw_b_2"), ("conv_ln_g", "conv_ln_g_2"), ("conv_ln_b", "conv_ln_b_2"), ("w0", "w0_2"),
                    ("a0", "a0_2"), ("k_k", "k_k_2"), ("k_a", "k_a_2"), ("lnx_g", "lnx_g_2"), ("lnx_b", "lnx_b_2")):
        v[k] = _columns(w[name], 4)
    p, c = np.arange(P)[:, None], np.arange(T)[None, :]
    rel = np.clip(384 + p - c, -128, 128) + 128
    relb = w["a_rel_bias"][:, rel]
    relb = np.where(((c >= 448) & (p < CH))[None], np.float32(-1e30), relb)
    both, block1, block2, rope = constants()
    lora = np.stack([np.concatenate([w["w2_2"], w["a2_2"]], 0), w["g2_2"][:P]], 1)
    arrays = {
        "x": g["x"][0].T.reshape(KD, P, T).transpose(1, 0, 2), "slabs": slabs,
        "ada": _slabs(w["ada_w_2"]), "vec": np.concatenate([v[k] for k, _ in VEC_COLS], 1),
        "both": both, "block1": block1, "block2": block2, "rope": rope, "relb": relb, "lora": lora,
        "g2b": w["g2_2"][P:]}
    return {k: np.ascontiguousarray(a) for k, a in arrays.items()}


def kernel(**inputs):
    import concourse.bacc as bacc
    from concourse.bass_utils import run_bass_kernel_spmd

    nc = bacc.Bacc("TRN2", target_bir_lowering=False, num_devices=1)
    arrays = {f"in_{k}": a for k, a in _layout(inputs).items()}
    args = [nc.dram_tensor(k, a.shape, mybir.dt.from_np(a.dtype), kind="ExternalInput").ap() for k, a in arrays.items()]
    y = nc.dram_tensor("out_y", (P, KD, T), F32, kind="ExternalOutput").ap()
    build(nc, *args, y)
    r = run_bass_kernel_spmd(nc, [arrays], core_ids=[0])
    got = r.results[0]["out_y"]
    return np.ascontiguousarray(got.transpose(1, 0, 2).reshape(D, T).T)[None]
```

```python
from contextlib import ExitStack

import numpy as np

import concourse.bass as bass
from concourse import mybir

P = 128
T = 512
NT = T // P
D = 1024
KD = D // P
DFF = 2816
KF = DFF // P
CH = 64
NC = T // CH
RING = 4
SLAB = KD * P
DOWN_CUT = [(0, 8), (8, 16), (16, 22)]
CONV_K = 31
DECAY = float(np.exp(-0.5))
EPS = 1e-6
LOWEST = -3e38

F32 = mybir.dt.float32
F32R = mybir.dt.float32r
ALU = mybir.AluOpType
ACT = mybir.ActivationFunctionType
AXX = mybir.AxisListType.X

SLABS = [("gu1", 2 * KF), ("down1", 24), ("in1", 16), ("uq", 2), ("ukv", 1), ("out1", 8),
         ("gu2", 2 * KF), ("down2", 24), ("in2", 23), ("out2", 8), ("up", 2 * KF), ("down3", 24)]


def starts(items):
    at, n = {}, 0
    for name, count in items:
        at[name] = n
        n += count
    return at, n


SLAB_AT, N_SLABS = starts(SLABS)
N_LOADS = -(-N_SLABS // RING) * RING

VEC_COLS = [("ffn1_norm", 8), ("mix_norm", 8), ("a_q_norm", 1), ("a_k_norm", 1), ("b_q_lat_norm", 2),
            ("b_kv_lat_norm", 1), ("b_q_nope_norm", 1), ("b_q_rope_norm", 1), ("b_k_nope_norm", 1),
            ("b_k_rope_norm", 1), ("ffn2_norm", 8), ("final_norm", 8), ("ada_b", 48),
            ("mix_pre_g", 8), ("mix_post_g", 8), ("conv_w", 4 * CONV_K), ("conv_b", 4),
            ("conv_ln_g", 4), ("conv_ln_b", 4), ("mu", 15), ("w0", 4), ("a0", 4), ("k_k", 4),
            ("k_a", 4), ("r_k", 4), ("lnx_g", 4), ("lnx_b", 4), ("ffn_pre_g", 8), ("ffn_post_g", 8),
            ("ffn_dw_w", 3 * 2 * KF), ("ffn_dw_b", 2 * KF)]
VEC_AT, N_VEC = starts(VEC_COLS)

BOTH_COLS = [("ident", 128), ("head2", 2), ("ones", 1)]
BLOCK1_COLS = [("head4", 4), ("quarter", 1), ("swap", 128), ("maskq", 128), ("maskk", 64)]
BLOCK2_COLS = [("eye64", 64), ("su", 64), ("iu", 64), ("niu", 64), ("np0", 64), ("nq0", 64),
               ("off32", 64), ("off64", 64), ("center", 128), ("block", 128), ("mean512", 128), ("keep", 512)]
BOTH_AT, N_BOTH = starts(BOTH_COLS)
BLOCK1_AT, N_BLOCK1 = starts(BLOCK1_COLS)
BLOCK2_AT, N_BLOCK2 = starts(BLOCK2_COLS)

MADE = 62

HI_AT = {"ffn1": 0, "mix": 1, "ffn2": 2, "mixpre": 3, "ffnpre": 4}
SCALED_AT = {"ffn1": 0, "mix": 1, "ffn2": 2, "mixpre": 3, "mixpost": 4, "ffnpre": 5, "ffnpost": 6}
NORMS = ["ffn1", "mix", "ffn2", "final", "mixpre", "mixpost", "ffnpre", "ffnpost"]

IN1_RAW = ["cq0", "cq1", "ckv0", "kr0"] + [f"qa{j}" for j in range(4)] + [f"ka{j}" for j in range(4)]
LATENT_RAW = ["qn0", "qn1", "qn2", "qn3", "qr0", "qr1", "kn0", "kn1", "kn2", "kn3"]


def constants():
    p = np.arange(P)
    t = np.arange(CH)
    s = p[:, None] % CH
    c = {
        "ident": np.eye(P), "swap": np.eye(P)[:, (p // 32) * 32 + (p + 16) % 32],
        "head2": p[:, None] // 64 == np.arange(2), "head4": p[:, None] // 32 == np.arange(4),
        "ones": np.ones((P, 1)), "quarter": p[:, None] < 32,
        "eye64": s == t, "su": s < t, "iu": s <= t, "niu": -1.0 * (s <= t),
        "np0": -1.0 * ((s < t) & (s // 16 == t // 16)), "nq0": -1.0 * ((s > t) & (s // 16 == t // 16)),
        "off32": (s // 32 == t // 32) & (s // 16 > t // 16),
        "off64": s // 32 > t // 32,
        "keep": np.broadcast_to(np.arange(T) % CH != 0, (P, T)),
        "block": p[:, None] // 64 == p[None, :] // 64,
        "center": np.eye(P) - (p[:, None] // 64 == p[None, :] // 64) / 64.0,
        "mean512": np.full((P, P), 1.0 / 512),
        "maskq": np.broadcast_to(p[None, :] < CH, (P, P)),
        "maskk": np.full((P, CH), -1e30),
    }
    tables = [np.ascontiguousarray(np.concatenate([np.asarray(c[k]).astype(np.float32) for k, _ in cols], 1))
              for cols in (BOTH_COLS, BLOCK1_COLS, BLOCK2_COLS)]
    inv = (1.0 / (np.float32(10000.0) ** (np.arange(0, 32, 2, dtype=np.float32) / np.float32(32)))).astype(np.float32)
    ang = (np.arange(T, dtype=np.float32)[:, None] * inv[None, :]).astype(np.float32)
    j = p % 16
    sign = np.where(p % 32 < 16, -1.0, 1.0)[:, None]
    rope = np.stack([np.cos(ang).T[j], np.sin(ang).T[j] * sign], 1).astype(np.float32)
    return (*tables, np.ascontiguousarray(rope))


def build(nc, x_in, slabs, ada_in, vec_in, both_in, block1_in, block2_in, rope_in, relb_in, lora_in, g2b_in,
          y_out):
    ctx = ExitStack()
    with ctx:
        base = -(-nc.sbuf_base // 64) * 64
        cursor = [base]

        def place(name, cols, dt=F32, offset=None):
            if offset is None:
                offset = cursor[0]
                cursor[0] += -(-4 * cols // 32) * 32
            return nc.alloc_sbuf_tensor_at(name, [P, cols], dt, offset=offset)

        def tiles(t, n, w=T):
            return t[:, 0:n * w].rearrange("p (n w) -> p n w", n=n)

        xT_t = place("xT", KD * T)
        h_at = cursor[0]
        hi_t, lo_t = place("h_hi", KD * T, F32R), place("h_lo", KD * T, F32R)
        wraw_t, whi_t, wlo_t = place("w_raw", RING * SLAB), place("w_hi", RING * SLAB, F32R), place("w_lo", RING * SLAB, F32R)
        tmp_t = place("tmp", 6 * T)
        vec_t, both_t = place("vec", N_VEC), place("both", N_BOTH)
        block_at = cursor[0]
        block2_t = place("block2", N_BLOCK2)
        block1_t = place("block1", N_BLOCK1, offset=block_at)
        mod_t, small_t = place("mod", 48 + 32), place("small", 256)
        g2b_t = place("g2b", T)
        arena = cursor[0]
        acth_t, actl_t = place("act_hi", KF * T, F32R), place("act_lo", KF * T, F32R)
        assert cursor[0] <= nc.sbuf_usable_end, (cursor[0], nc.sbuf_usable_end)
        xT, h_hi, h_lo = tiles(xT_t, KD), tiles(hi_t, KD), tiles(lo_t, KD)
        w_raw, w_hi, w_lo = (tiles(t, RING, SLAB) for t in (wraw_t, whi_t, wlo_t))
        tmp = tiles(tmp_t, 6)
        act_hi, act_lo = tiles(acth_t, KF), tiles(actl_t, KF)

        def slot(name, at, n, dt=F32, w=T):
            assert at * T + n * w <= 2 * KF * T, name
            return tiles(place(name, n * w, dt, offset=arena + 4 * T * at), n, w)

        qa, ka, qn, kn = slot("qa", 0, 4), slot("ka", 4, 4), slot("qn", 8, 4), slot("kn", 12, 4)
        qr, kr, va = slot("qr", 16, 2), slot("kr", 18, 1), slot("va", 19, 4)
        cq, ckv = slot("cq", 23, 2), slot("ckv", 25, 1)
        cq_hi, cq_lo = slot("cq_hi", 26, 2, F32R), slot("cq_lo", 28, 2, F32R)
        ckv_hi, ckv_lo = slot("ckv_hi", 30, 1, F32R), slot("ckv_lo", 31, 1, F32R)
        rope, vb, relb = slot("rope", 32, 2), slot("vb", 34, 4), slot("relb", 38, 2)
        adaw = slot("adaw", 40, 2, w=SLAB)
        probT = slot("probT", 23, 8)
        prob = slot("prob", 31, 3)
        conv_in, conv_out, conv_gate = slot("conv_in", 0, 4, w=T + 32), slot("conv_out", 5, 4), slot("conv_gate", 9, 1)
        rk_r, rk_k, rk_v = (slot("rk_" + n, 10 + 4 * i, 4) for i, n in enumerate("rkv"))
        rk_w, rk_a, rk_g = (slot("rk_" + n, 22 + 2 * i, 2) for i, n in enumerate("wag"))
        mP, mQ, mR, mO1, mO2 = (slot("m_" + n, 28 + 2 * i, 2) for i, n in enumerate(("p", "q", "r", "o1", "o2")))
        rk_b, lora, lora_act = slot("rk_b", 38, 2), slot("lora", 40, 2), slot("lora_act", 42, 2)
        tokV, tokK, tokB, tokQ, mMT, mMR, mAR = (
            tiles(place("h_" + n, 2 * T, offset=h_at + 8 * T * i), 2)
            for i, n in enumerate(("tok_v", "tok_k", "tok_b", "tok_q", "mt", "mr", "ar")))
        mX, mZ = rk_w, rk_a
        mG, mHD = mO1, mO2
        g2b, lora_act2 = g2b_t, tmp[:, 5, :]
        shift = tmp_t[:, 2 * T:2 * T + 2 * 516].rearrange("p (n w) -> p n w", n=2)

        def of_half(m, half):
            return m[:, 2 * half:2 * half + 2, :]

        mid_a = slot("mid_a", 0, KD)
        mid_h = tiles(place("mid_h", KD * T, offset=h_at), KD)

        bank = [ctx.enter_context(nc.psum_tensor(f"bank{i}", [P, T], F32))[:, :] for i in range(8)]

        def vec(k, j=0, n=1):
            return vec_t[:, VEC_AT[k] + j:VEC_AT[k] + j + n]

        def const(k):
            for t, at, cols in ((both_t, BOTH_AT, BOTH_COLS), (block1_t, BLOCK1_AT, BLOCK1_COLS),
                                (block2_t, BLOCK2_AT, BLOCK2_COLS)):
                if k in at:
                    return t[:, at[k]:at[k] + dict(cols)[k]]

        ident = const("ident")
        mod = mod_t[:, 0:48]
        gs = {"mixpre": mod_t[:, 48:56], "ffnpre": mod_t[:, 56:64]}
        gp = {"mixpost": mod_t[:, 64:72], "ffnpost": mod_t[:, 72:80]}
        shf = {"mixpre": mod_t[:, 0:8], "ffnpre": mod_t[:, 24:32]}
        n_std, n_rs = small_t[:, 0:4], small_t[:, 4:8]
        silc, mod_product = tmp_t[:, 2 * T:4 * T], tmp_t[:, 4 * T:6 * T]
        hd_rs = {"lat": small_t[:, 16:28], "main": small_t[:, 28:92], "up": small_t[:, 92:188]}
        row_max, row_nmax, row_sum = small_t[:, 188:192], small_t[:, 192:196], small_t[:, 196:200]
        rk_rs, d_end, omka = small_t[:, 200:216], small_t[:, 216:232], small_t[:, 232:236]

        sems = {}

        def S(name):
            if name not in sems:
                sems[name] = ctx.enter_context(nc.semaphore(name))
            return sems[name]

        def chunk(m, e, g, c):
            return m[CH * e:CH * e + CH, g, CH * c:CH * c + CH]

        def rows(m, g=slice(None)):
            return m[:, g, :].rearrange("p (c t) -> p c t", c=NC)

        def every_chunk(t64):
            return t64.unsqueeze(1).to_broadcast([P, NC, CH])

        block = ctx.enter_context(nc.Block())

        @block.sync
        def _(sp):
            for h in range(2):
                sp.dma_start(xT[:, 4 * h:4 * h + 4, :], x_in[:, 4 * h:4 * h + 4, :]).then_inc(S(f"x_in{h}"), 16)
            for dst, src in ((both_t, both_in), (vec_t, vec_in), (block1_t, block1_in)):
                sp.dma_start(dst[:, :], src).then_inc(S("tables_in"), 16)
            for r in range(RING):
                sp.dma_start(w_raw[:, r, :], slabs[r]).then_inc(S(f"w_raw_in{r}"), 16)
            with sp.Fori(1, N_LOADS // RING) as i:
                for r in range(RING):
                    sp.wait_ge(S("w_split"), i * RING + (r + 1 - RING))
                    sp.dma_start(w_raw[:, r, :], slabs[i * RING + r]).then_inc(S(f"w_raw_in{r}"), 16)
            for j in range(KD):
                sp.wait_ge(S("norm_lo"), 8 * NORMS.index("ffnpost") + j + 1)
                sp.dma_start(y_out[:, j, :], xT[:, j, :]).then_inc(S("y_out"), 16)
            sp.wait_ge(S("y_out"), 16 * KD)

        @block.gpsimd
        def _(pool):
            def split(n, r, loads, first=False):
                pool.wait_ge(S(f"w_raw_in{r}"), loads)
                if not first:
                    pool.wait_ge(S("slab_done"), n + (1 - RING))
                    pool.nop(nofuse=True)
                nc.gpsimd.tensor_scalar(w_hi[:, r, :], w_raw[:, r, :], 1.0, 1.0, ALU.mult, ALU.mult).then_inc(S("w_hi"), 1)
                pool.wait_ge(S("w_hi"), n + 1)
                nc.gpsimd.tensor_tensor(w_lo[:, r, :], w_raw[:, r, :], w_hi[:, r, :], ALU.subtract).then_inc(S("w_split"), 1)

            for r in range(RING):
                split(r, r, 16, first=True)
            with pool.Fori(1, N_LOADS // RING) as i:
                for r in range(RING):
                    split(i * RING + r, r, i * 16 + 16)

        @block.tensor
        def _(pe):
            mm = nc.tensor.matmul
            def passes(out, hi, lo, rhs_hi, rhs_lo, start, stop):
                mm(out, hi, rhs_hi, start=start, stop=False, skip_group_check=True)
                mm(out, hi, rhs_lo, start=False, stop=False, skip_group_check=True)
                return mm(out, lo, rhs_hi, start=False, stop=stop, skip_group_check=True)

            def product(out, n, r, act_h, act_l, ks=range(KD), first=0, start=True, stop=True, wait_k=None):
                pe.wait_ge(S("w_split"), n + 1)
                for i, k in enumerate(ks):
                    if wait_k is not None:
                        wait_k(k)
                    w = slice(P * i, P * i + P)
                    hi, lo = w_hi[:, r, w], w_lo[:, r, w]
                    a, b = start and i == 0, stop and i == len(ks) - 1
                    last = passes(out, hi, lo, act_h[:, first + k, :], act_l[:, first + k, :], a, b)
                return last

            def turned_passes(out, act_h, act_l, k, t, r, half, start, stop):
                tok, w = slice(P * t, P * t + P), slice(T * half, T * half + T)
                mm(out, act_h[:, k, tok], w_hi[:, r, w], start=start, stop=False, skip_group_check=True)
                mm(out, act_h[:, k, tok], w_lo[:, r, w], start=False, stop=False, skip_group_check=True)
                return mm(out, act_l[:, k, tok], w_hi[:, r, w], start=False, stop=stop, skip_group_check=True)

            def stat(out, square, mask, start, width):
                for t in range(NT):
                    last = mm(out[:, width * t:width * t + width], square[:, P * t:P * t + P], mask,
                              start=start and t == 0, stop=True, skip_group_check=True)
                return last

            def spread(out, cols, heads):
                w = P // heads
                for t in range(NT):
                    for e in range(heads):
                        c = cols[:, heads * t + e:heads * t + e + 1].to_broadcast([P, w])
                        if heads == 1:
                            last = nc.tensor.transpose(out[:, P * t:P * t + P], c, ident)
                        else:
                            last = mm(out[w * e:w * e + w, P * t:P * t + P], c, ident, start=True, stop=True,
                                      skip_group_check=True)
                return last

            def norm_stats(name):
                q = NORMS.index(name)
                pe.wait_ge(S("norm_acc"), 6 * q + 6)
                stat(bank[7], tmp[:, 4, :], const("ones"), True, 1).then_inc(S("norm_stat"), 1)
                pe.wait_ge(S("norm_square"), 8 * q + 8)
                stat(bank[7], tmp[:, 1, :], const("ones"), False, 1).then_inc(S("norm_stat"), 1)

            def norm_spread(name):
                q = NORMS.index(name)
                pe.wait_ge(S("norm_rs"), q + 1)
                spread(bank[6], n_rs, 1).then_inc(S("norm_spread"), 1)

            def after_norm(name):
                q = NORMS.index(name)
                return lambda k: pe.wait_ge(S("norm_lo"), 8 * q + k + 1)

            def gate_up(name, o, norm):
                at = SLAB_AT[name]

                def pair(i, u, wait_k=None):
                    pe.wait_ge(S("ff_product"), i * 2 + (o + u + 1))
                    for m in range(2):
                        n = 2 * u + m
                        product(bank[n], i * 4 + (at + n), (at + n) % RING, h_hi, h_lo,
                                wait_k=wait_k if m == 0 else None).then_inc(S("slab_done"), 1)

                pair(0, 0, after_norm(norm))
                pair(0, 1)
                with pe.Fori(1, KF // 2) as i:
                    pair(i, 0)
                    pair(i, 1)

            def down(name, o, done, done_at, norm):
                at = SLAB_AT[name]
                for m in range(KD):
                    if m >= 4:
                        pe.wait_ge(S(done), done_at + m - 3)
                    elif name == "down3":
                        pe.wait_ge(S("taps"), 2 * KF + m + 1)
                    else:
                        pe.wait_ge(S("ff_product"), o + KF + m // 2 + 1)
                    for s, (k0, k1) in enumerate(DOWN_CUT):
                        n = at + 3 * m + s
                        wait_k = (lambda k: pe.wait_ge(S("act_lo"), o + 3 + k)) if m == 0 else None
                        product(bank[m % 4], n, n % RING, act_hi, act_lo, ks=range(k0, k1), start=s == 0, stop=s == 2,
                                wait_k=wait_k).then_inc(S("slab_done"), 1)
                norm_stats(norm)
                norm_spread(norm)

            pe.wait_ge(S("tables_in"), 48)
            norm_stats("ffn1")
            norm_spread("ffn1")
            gate_up("gu1", 0, "ffn1")
            down("down1", 0, "x_new", 0, "mix")

            raw_n, spread_n = [0], [0]

            def head_stat(name, bk, col, mask, width, start):
                pe.wait_ge(S("hd_square"), raw_n[0] + 1)
                stat(bank[bk][:, col:col + NT * width], tmp[:, raw_n[0] % 2, :], const(mask)[:, 0:width], start, width)\
                    .then_inc(S("hd_stat"), 1)
                raw_n[0] += 1

            def head_spread(cols, heads):
                r = spread_n[0]
                if r >= 2:
                    pe.wait_ge(S("hd_applied"), r - 1)
                spread(bank[6 if r % 2 == 0 else 4], cols, heads).then_inc(S("hd_spread"), 1)
                spread_n[0] += 1

            at = SLAB_AT["in1"]
            stats_in1 = [("cq0", 7, 0, "ones", 1, True), ("cq1", 7, 0, "ones", 1, False), ("ckv0", 7, 4, "ones", 1, False),
                         ("kr0", 7, 8, "quarter", 1, False)] + \
                        [(IN1_RAW[4 + j], 5, 8 * j, "head2", 2, j == 0) for j in range(8)]
            pe.wait_ge(S("norm_std"), 2)
            for m in range(16):
                if m < 12:
                    if m >= 4:
                        pe.wait_ge(S("in1_raw"), m - 3)
                    product(bank[m % 4], at + m, (at + m) % RING, h_hi, h_lo, wait_k=after_norm("mix") if m == 0 else None)\
                        .then_inc(S("slab_done"), 1)
                else:
                    pe.wait_ge(S("w_split"), at + m + 1)
                    for k in (2 * (m - 12), 2 * (m - 12) + 1):
                        for t in range(NT):
                            if k == 0:
                                pe.wait_ge(S("in1_raw"), 9 + t)
                            last = turned_passes(bank[t], h_hi, h_lo, k, t, (at + m) % RING, k % 2, k == 0, k == KD - 1)
                    last.then_inc(S("slab_done"), 1)
                if 1 <= m <= 12:
                    head_stat(*stats_in1[m - 1])
                if m == 6:
                    pe.wait_ge(S("hd_rs"), 1)
                    head_spread(hd_rs["lat"][:, 0:4], 1)
                    head_spread(hd_rs["lat"][:, 4:8], 1)
                if m == 7:
                    head_spread(hd_rs["lat"][:, 8:12], 1)
            for t in range(14):
                if t < 6:
                    n = SLAB_AT["uq"] + t // 3
                    ks, first, a_hi, a_lo = range(2), 2 * (t % 3), cq_hi, cq_lo
                else:
                    n = SLAB_AT["ukv"]
                    ks, first, a_hi, a_lo = range(1), t - 6, ckv_hi, ckv_lo
                r = n % RING
                if t in (0, 3, 6):
                    pe.wait_ge(S("w_split"), n + 1)
                if t == 0:
                    pe.wait_ge(S("cq_split"), 2)
                if t == 6:
                    pe.wait_ge(S("cq_split"), 3)
                pe.wait_ge(S("in1_raw"), 16 + t - 3)
                for k in ks:
                    w = slice(P * (first + k), P * (first + k) + P)
                    if t < 10:
                        last = passes(bank[t % 4], w_hi[:, r, w], w_lo[:, r, w], a_hi[:, k, :], a_lo[:, k, :],
                                      k == 0, k == len(ks) - 1)
                    else:
                        last = turned_passes(bank[t % 4], a_hi, a_lo, 0, t - 10, r, 1, True, True)
                last.then_inc(S("slab_done" if t in (2, 5, 13) else "latent_mm"), 1)
                if 1 <= t <= 10:
                    i = t - 1
                    if i < 4:
                        spec = (i * 8, "head2", 2)
                    elif i < 6:
                        spec = (32 + 16 * (i - 4), "head4", 4)
                    else:
                        spec = (64 + 8 * (i - 6), "head2", 2)
                    head_stat(LATENT_RAW[i], 7, *spec, i == 0)
            pe.wait_ge(S("hd_rs"), 2)
            for j in range(8):
                head_spread(hd_rs["main"][:, 8 * j:8 * j + 8], 2)
            pe.wait_ge(S("hd_rs"), 3)
            for j in range(4):
                head_spread(hd_rs["up"][:, 8 * j:8 * j + 8], 2)
            for j in range(2):
                head_spread(hd_rs["up"][:, 32 + 16 * j:48 + 16 * j], 4)
            for j in range(4):
                head_spread(hd_rs["up"][:, 64 + 8 * j:72 + 8 * j], 2)
            for j, (m, need) in enumerate(((qr[:, 0, :], 16), (qr[:, 1, :], 17), (kr[:, 0, :], 17))):
                pe.wait_ge(S("hd_applied"), need)
                pe.wait_ge(S("in1_raw"), 30)
                mm(bank[j], const("swap"), m, start=True, stop=True).then_inc(S("swapped"), 1)

            def scores(s):
                h, q = divmod(s, NT)
                e, j, out = h % 2, (h % 8) // 2, bank[s % 3]
                L, e64 = P * (q + 1), slice(CH * e, CH * e + CH)
                if s == 0:
                    pe.wait_ge(S("hd_applied"), 21)
                    pe.wait_ge(S("roped"), 3)
                if s >= 3:
                    pe.wait_ge(S("probs"), s - 2)
                qs = slice(P * q, P * q + P)
                if h < 8:
                    mm(out[:, 0:L], qa[e64, j, qs], ka[e64, j, 0:L], start=True, stop=True).then_inc(S("scores"), 1)
                    return
                e32 = slice(32 * (h % 4), 32 * (h % 4) + 32)
                mm(out[:, 0:L], qn[e64, j, qs], kn[e64, j, 0:L], start=True, stop=False, skip_group_check=True)
                mm(out[:, 0:L], qr[e32, (h - 8) // 4, qs], kr[e32, 0, 0:L], start=False, stop=False,
                   skip_group_check=True, tile_position=(32 * (h % 4), 0))
                e1 = slice(32 * (h % 4), 32 * (h % 4) + 1)
                mm(out[:, L - CH:L], const("maskq")[e1, :], const("maskk")[e1, :], start=False, stop=True,
                   skip_group_check=True, tile_position=(32 * (h % 4), 0)).then_inc(S("scores"), 1)

            def turn(s):
                pe.wait_ge(S("probs_normed"), s + 1)
                if s >= 2:
                    pe.wait_ge(S("probT"), s - 1)
                for kt in range(s % NT + 1):
                    last = nc.tensor.transpose(bank[3 + s % 2][:, P * kt:P * kt + P], prob[:, s % 3, P * kt:P * kt + P], ident)
                last.then_inc(S("turned"), 1)

            def values(h):
                pe.wait_ge(S("probT"), NT * h + NT)
                if h % 2 == 0 and h >= 4:
                    pe.wait_ge(S("o_lo"), h // 2 - 1)
                v = va if h < 8 else vb
                for kt in range(NT):
                    last = mm(bank[5 + (h // 2) % 2][CH * (h % 2):CH * (h % 2) + CH, P * kt:T],
                              v[:, kt, CH * (h % 8):CH * (h % 8) + CH], probT[:, NT * (h % 2) + kt, P * kt:T],
                              start=kt == 0, stop=kt == NT - 1, skip_group_check=True)
                last.then_inc(S("values"), 1)

            for s in range(16 * NT + 2):
                if s < 16 * NT:
                    scores(s)
                if s >= 2:
                    turn(s - 2)
                    if (s - 2) % NT == 0 and s > 2:
                        values((s - 2) // NT - 1)
            values(15)

            def short(name, done, done_at, wait_k, norm):
                at = SLAB_AT[name]
                for m in range(KD):
                    if m >= 4:
                        pe.wait_ge(S(done), done_at + m - 3)
                    product(bank[m % 4], at + m, (at + m) % RING, h_hi, h_lo, wait_k=wait_k if m == 0 else None)\
                        .then_inc(S("slab_done"), 1)
                norm_stats(norm)
                norm_spread(norm)

            pe.wait_ge(S("probT"), 16 * NT)
            short("out1", "x_new", 8, lambda k: pe.wait_ge(S("o_lo"), k + 1), "ffn2")

            gate_up("gu2", KF, "ffn2")
            down("down2", KF, "x_new", 16, "final")

            norm_stats("mixpre")
            norm_spread("mixpre")
            at = SLAB_AT["in2"]

            def project(m):
                if m >= 4:
                    pe.wait_ge(S("in2_raw"), m - 3 if m <= 18 else 16 + (m - 19) // 2)
                product(bank[m % 4], at + m, (at + m) % RING, h_hi, h_lo, wait_k=after_norm("mixpre") if m == 0 else None)\
                    .then_inc(S("slab_done"), 1)

            made = []

            def made_in(pairs, name, g, half, bk=None, cs=range(NC)):
                out = bank[len(made) % 6]
                if len(made) >= 6:
                    before, value = made[-6]
                    pe.wait_ge(S("rk_" + before), value)
                made.append((name, 2 * half + g + 1))
                for i, (lhs, rhs, skip) in enumerate(pairs):
                    for c in range(NC):
                        if c < skip:
                            continue
                        for e in range(2):
                            r = const("eye64")[CH * e:CH * e + CH, :] if rhs is None else chunk(rhs, e, g, c)
                            last = mm(out[CH * e:CH * e + CH, CH * c:CH * c + CH], chunk(lhs, e, g, c), r,
                                      start=i == 0 and c == 0, stop=i == len(pairs) - 1, skip_group_check=True)
                return last.then_inc(S("rk_mm"), 1)

            def ready(name, g, half):
                pe.wait_ge(S("rk_" + name), 2 * half + g + 1)

            def lora_products(half):
                for n in range(6 * half, 6 * half + 6):
                    G, i = divmod(n, 3)
                    fs = slice(P * G, P * G + P)
                    if n == 0:
                        pe.wait_ge(S("lora_in"), 48)
                        pe.wait_ge(S("lora_act"), 3)
                    if n >= 2:
                        pe.wait_ge(S("lora_out"), n - 1)
                    out = bank[4 + n % 2]
                    if i < 2:
                        r = slice(CH * i, CH * i + CH)
                        mm(out[:, :], lora[r, 0, fs], lora_act[r, 0, :], start=True, stop=True).then_inc(S("lora_mm"), 1)
                    else:
                        mm(out[:, :], lora[:, 1, fs], lora_act[:, 1, :], start=True, stop=False)
                        mm(out[:, :], g2b[0:32, fs], lora_act2[0:32, :], start=False, stop=True).then_inc(S("lora_mm"), 1)

            def key_norms(half):
                for g in range(2):
                    v = 2 * half + g + 1
                    pe.wait_ge(S("rk_ksq"), v)
                    if v > 1:
                        pe.wait_ge(S("rk_rsd" if g else "rk_dstd"), v - 1)
                    stat(bank[7], tmp[:, g, :], const("head2"), True, 2).then_inc(S("rk_kst"), 1)

            def key_spread(half, g):
                v = 2 * half + g + 1
                pe.wait_ge(S("rk_krs"), 2 * half + 2)
                if v > 1:
                    pe.wait_ge(S("rk_bonus"), v - 1)
                pe.wait_ge(S("rk_rsd"), 2 * half + 2)
                spread(bank[6], rk_rs[:, 8 * g:8 * g + 8], 2).then_inc(S("rk_kspread"), 1)
                pe.wait_ge(S("rk_bz"), v)
                mm(bank[7][:, :], const("block"), mR[:, g, :], start=True, stop=True).then_inc(S("rk_bsum"), 1)

            def recurrence(half):
                r_, k_, v_ = (of_half(m, half) for m in (rk_r, rk_k, rk_v))
                mW, mS = k_, v_
                for g in range(2):
                    pe.wait_ge(S("in2_shifted"), 9 + 6 * half)
                    made_in([(v_, None, 0)], "tv", g, half)
                for g in range(2):
                    ready("factors", g, half)
                    made_in([(k_, None, 0)], "tk", g, half)
                    made_in([(rk_a, None, 0)], "tb", g, half)
                    made_in([(rk_w, None, 0)], "tq", g, half)
                for g in range(2):
                    made_in([(rk_a, rk_w, 0)], "p0", g, half)
                    made_in([(rk_w, rk_a, 0)], "q0", g, half)
                    made_in([(k_, rk_w, 0)], "mt", g, half)
                    made_in([(rk_a, r_, 0)], "ar", g, half)
                    made_in([(k_, r_, 0)], "mr", g, half)
                for g in range(2):
                    ready("p0", g, half)
                    ready("q0", g, half)
                    made_in([(mP, mQ, 0)], "q1", g, half)
                    made_in([(mQ, mP, 0)], "p1", g, half)
                for g in range(2):
                    ready("r0", g, half)
                    ready("q1", g, half)
                    ready("p1", g, half)
                    made_in([(mQ, mR, 0)], "r1", g, half)
                    made_in([(mP, mQ, 0)], "q2", g, half)
                    made_in([(mQ, mP, 0)], "p2", g, half)
                for g in range(2):
                    ready("r1", g, half)
                    ready("q2", g, half)
                    ready("p2", g, half)
                    made_in([(mQ, mR, 0)], "r2", g, half)
                    made_in([(mP, mQ, 0)], "q3", g, half)
                for g in range(2):
                    ready("r2", g, half)
                    ready("q3", g, half)
                    made_in([(mQ, mR, 0)], "r3", g, half)
                if half:
                    conv_mean()
                for lvl, off in ((1, mO1), (2, mO2)):
                    for g in range(2):
                        ready("r3" if lvl == 1 else "r4", g, half)
                        made_in([(mR, None, 0)], f"rt{lvl}", g, half)
                        made_in([(off, mR, 0)], f"y{lvl}", g, half)
                    for g in range(2):
                        ready(f"rt{lvl}", g, half)
                        ready(f"y{lvl}", g, half)
                        made_in([(mP, mQ, 0)], "r4" if lvl == 1 else "r5", g, half)
                    if half and lvl == 1:
                        conv_stats()
                for g in range(2):
                    ready("mt", g, half)
                    ready("r5", g, half)
                    ready("tq", g, half)
                    made_in([(mMT, tokV, 0)], "x", g, half)
                    made_in([(mR, tokQ, 0)], "w", g, half)
                for g in range(2):
                    ready("x", g, half)
                    made_in([(mR, mX, 0)], "z", g, half)
                    ready("w", g, half)
                    made_in([(mW, tokB, 0)], "g", g, half)
                for g in range(2):
                    ready("z", g, half)
                    made_in([(tokK, tokV, 0), (tokB, mZ, 0)], "hd", g, half)
                    made_in([(mW, mAR, 0)], "rho", g, half)
                if half:
                    conv_spread()
                for c in range(1, NC - 1):
                    for g in range(2):
                        if c == 1:
                            ready("hd", g, half)
                            ready("g", g, half)
                            if half:
                                pe.wait_ge(S("conv_t"), 4)
                        else:
                            pe.wait_ge(S(f"rk_state{g}"), (NC - 2) * half + c - 1)
                        src = mHD if c == 1 else mS
                        for e in range(2):
                            last = mm(bank[6 + g][CH * e:CH * e + CH, CH * c:CH * c + CH], chunk(mG, e, g, c),
                                      chunk(src, e, g, 0 if c == 1 else c), start=True, stop=True, skip_group_check=True)
                        last.then_inc(S(f"rk_step{g}"), 1)
                for g in range(2):
                    pe.wait_ge(S(f"rk_state{g}"), (NC - 2) * (half + 1))
                    ready("rho", g, half)
                    made_y(g, half, r_, mS)
                for g in range(2):
                    ready("y", g, half)
                    made_plain("d", const("center"), mP, g, half)
                for g in range(2):
                    v = 2 * half + g + 1
                    pe.wait_ge(S("rk_dsq"), v)
                    stat(bank[7], tmp[:, g, :], const("head2"), True, 2).then_inc(S("rk_dst"), 1)
                    pe.wait_ge(S("rk_drs"), v)
                    spread(bank[6], rk_rs[:, 8 * g:8 * g + 8], 2).then_inc(S("rk_dspread"), 1)
                    pe.wait_ge(S("rk_out"), v)

            def made_y(g, half, r_, mS):
                out = bank[len(made) % 6]
                before, value = made[-6]
                pe.wait_ge(S("rk_" + before), value)
                made.append(("y", 2 * half + g + 1))
                for c in range(NC):
                    for e in range(2):
                        o = out[CH * e:CH * e + CH, CH * c:CH * c + CH]
                        mm(o, chunk(tokV, e, g, c), chunk(mMR, e, g, c), start=c == 0, stop=False, skip_group_check=True)
                        if c:
                            s = mHD if c == 1 else mS
                            mm(o, chunk(s, e, g, 0 if c == 1 else c), chunk(r_, e, g, c), start=False, stop=False,
                               skip_group_check=True)
                        last = mm(o, chunk(mZ, e, g, c), chunk(mAR, e, g, c), start=False, stop=True, skip_group_check=True)
                last.then_inc(S("rk_mm"), 1)

            def made_plain(name, lhs, rhs, g, half):
                out = bank[len(made) % 6]
                before, value = made[-6]
                pe.wait_ge(S("rk_" + before), value)
                made.append((name, 2 * half + g + 1))
                mm(out[:, :], lhs, rhs[:, g, :], start=True, stop=True).then_inc(S("rk_mm"), 1)

            def conv_mean():
                for j in range(4):
                    pe.wait_ge(S("conv"), 4 * (CONV_K - 1) + j + 1)
                    last = mm(bank[6][:, :], const("mean512"), conv_out[:, j, :], start=j == 0, stop=j == 3)
                last.then_inc(S("conv_mean"), 1)

            def conv_stats():
                for j in range(4):
                    pe.wait_ge(S("conv_square"), j + 1)
                    stat(bank[7], tmp[:, j, :], const("ones"), j == 0, 1).then_inc(S("conv_stat"), 1)

            def conv_spread():
                pe.wait_ge(S("conv_rs"), 1)
                pe.wait_ge(S("conv_d"), 4)
                spread(bank[6], n_rs, 1).then_inc(S("conv_spread"), 1)

            for m in range(23):
                project(m)
                if m == 9:
                    lora_products(0)
                if m == 11:
                    key_norms(0)
                if m in (13, 14):
                    key_spread(0, m - 13)
            for half in range(2):
                if half:
                    lora_products(1)
                    key_norms(1)
                    key_spread(1, 0)
                    key_spread(1, 1)
                else:
                    pe.wait_ge(S("in2_raw"), 19)
                pe.wait_ge(S("rk_bonus"), 2 * half + 2)
                recurrence(half)
            pe.wait_ge(S("rk_out"), 4)
            short("out2", "mid_a", 0, lambda k: pe.wait_ge(S("mix_split"), k + 1), "mixpost")

            norm_stats("ffnpre")
            norm_spread("ffnpre")
            at = SLAB_AT["up"]

            def up_pair(i, u, wait_k=None):
                for m in range(2):
                    n = 2 * u + m
                    pe.wait_ge(S("taps"), i * 4 + (n + 1))
                    product(bank[n], i * 4 + (at + n), (at + n) % RING, h_hi, h_lo,
                            wait_k=wait_k if m == 0 else None).then_inc(S("slab_done"), 1)

            up_pair(0, 0, after_norm("ffnpre"))
            up_pair(0, 1)
            with pe.Fori(1, KF // 2) as i:
                up_pair(i, 0)
                up_pair(i, 1)
            down("down3", 2 * KF, "mid_h", 0, "ffnpost")

        @block.scalar
        def _(act):
            f = nc.scalar.activation

            def norm_squares(name, src, wait=None):
                q = NORMS.index(name)
                for j in range(KD):
                    if wait is not None:
                        wait(j)
                    if j >= 3:
                        act.wait_ge(S("norm_acc"), 6 * q + j - 2)
                    f(tmp[:, j % 2 if j else 4, :], src[:, j, :], ACT.Square).then_inc(S("norm_square"), 1)
                act.wait_ge(S("norm_stat"), 2 * q + 2)
                f(n_std, bank[7][:, 0:4], ACT.Sqrt, bias=EPS, scale=1.0 / D).then_inc(S("norm_std"), 1)

            def norm_hi(name):
                for j in range(KD):
                    act.wait_ge(S("norm_t"), 8 * SCALED_AT[name] + j + 1)
                    if name in shf:
                        f(h_hi[:, j, :], tmp[:, 4 + j % 2, :], ACT.Identity, bias=shf[name][:, j:j + 1]).then_inc(S("norm_hi"), 1)
                    else:
                        f(h_hi[:, j, :], tmp[:, 4 + j % 2, :], ACT.Copy).then_inc(S("norm_hi"), 1)

            def gate_up(name, o):
                at = SLAB_AT[name]
                with act.Fori(0, KF // 2) as i:
                    for u in range(2):
                        act.wait_ge(S("slab_done"), i * 4 + (at + 2 * u + 2))
                        act.wait_ge(S("ff_product"), i * 2 + (o + u + 1))
                        f(tmp[:, 2 + u, :], bank[2 * u][:, :], ACT.Silu).then_inc(S("silu"), 1)

            norm_squares("ffn1", xT, lambda j: act.wait_ge(S(f"x_in{j // 4}"), 16) if j % 4 == 0 else None)
            norm_hi("ffn1")
            gate_up("gu1", 0)
            norm_squares("mix", xT, lambda j: act.wait_ge(S("x_new"), j + 1))
            act.wait_ge(S("slab_done"), SLAB_AT["in1"])
            act.dma_start(rope, rope_in).then_inc(S("rope_in"), 16)
            for h in range(2):
                act.dma_start(relb[:, h, :], relb_in[h]).then_inc(S(f"relb_in{h}"), 16)
            act.dma_start(silc, ada_in[48]).then_inc(S("c_in"), 16)
            for a in range(2):
                act.dma_start(adaw[:, a, :], ada_in[a]).then_inc(S(f"ada_in{a}"), 16)
            norm_hi("mix")
            act.wait_ge(S("c_in"), 16)
            f(silc, silc, ACT.Silu).then_inc(S("silu_c"), 1)

            def next_modulation(a):
                if a + 2 < 48:
                    act.wait_ge(S("ada_sum"), a + 1)
                    act.dma_start(adaw[:, a % 2, :], ada_in[a + 2]).then_inc(S(f"ada_in{a % 2}"), 16)


            raw = {"cq0": cq[:, 0, :], "cq1": cq[:, 1, :], "ckv0": ckv[:, 0, :], "kr0": kr[:, 0, :]}
            for j in range(4):
                raw |= {f"qa{j}": qa[:, j, :], f"ka{j}": ka[:, j, :], f"qn{j}": qn[:, j, :], f"kn{j}": kn[:, j, :]}
            raw |= {"qr0": qr[:, 0, :], "qr1": qr[:, 1, :]}
            for i, name in enumerate(IN1_RAW + LATENT_RAW):
                act.wait_ge(S("in1_raw"), i + 1 if i < 12 else i + 5)
                if i >= 2:
                    act.wait_ge(S("hd_stat"), i - 1)
                f(tmp[:, i % 2, :], raw[name], ACT.Square).then_inc(S("hd_square"), 1)
                if i < 16:
                    next_modulation(i)
                if i == 3:
                    act.wait_ge(S("hd_stat"), 4)
                    f(hd_rs["lat"][:, 0:4], bank[7][:, 0:4], ACT.Sqrt, bias=EPS, scale=1.0 / 256).then_inc(S("hd_std"), 1)
                    f(hd_rs["lat"][:, 4:8], bank[7][:, 4:8], ACT.Sqrt, bias=EPS, scale=1.0 / 128).then_inc(S("hd_std"), 1)
                    f(hd_rs["lat"][:, 8:12], bank[7][:, 8:12], ACT.Sqrt, bias=EPS, scale=1.0 / 32).then_inc(S("hd_std"), 1)
                if i == 11:
                    act.wait_ge(S("hd_stat"), 12)
                    f(hd_rs["main"], bank[5][:, 0:64], ACT.Sqrt, bias=EPS, scale=1.0 / 64).then_inc(S("hd_std"), 1)
                if i == 21:
                    act.wait_ge(S("hd_stat"), 22)
                    up = hd_rs["up"]
                    f(up[:, 0:32], bank[7][:, 0:32], ACT.Sqrt, bias=EPS, scale=1.0 / 64).then_inc(S("hd_std"), 1)
                    f(up[:, 32:64], bank[7][:, 32:64], ACT.Sqrt, bias=EPS, scale=1.0 / 32).then_inc(S("hd_std"), 1)
                    f(up[:, 64:96], bank[7][:, 64:96], ACT.Sqrt, bias=EPS, scale=1.0 / 64).then_inc(S("hd_std"), 1)

            def softmax(s):
                h, q = divmod(s, NT)
                L = P * (q + 1)
                act.wait_ge(S("row_nmax"), s + 1)
                if s >= 3:
                    act.wait_ge(S("turned"), s - 2)
                if s >= 4:
                    act.wait_ge(S("probs_normed"), s - 3)
                src = prob[:, s % 3, 0:L] if h < 8 else bank[s % 3][:, 0:L]
                f(prob[:, s % 3, 0:L], src, ACT.Exp, bias=row_nmax[:, s % 4:s % 4 + 1],
                  accum_out=row_sum[:, s % 4:s % 4 + 1]).then_inc(S("probs"), 1)

            def keep_turned(s):
                h, q = divmod(s, NT)
                act.wait_ge(S("turned"), s + 1)
                if q == 0 and h >= 2:
                    act.wait_ge(S("values"), h - 1)
                n = NT * (h % 2)
                f(probT[:, n:n + q + 1, P * q:P * q + P],
                  bank[3 + s % 2][:, 0:P * (q + 1)].rearrange("p (k c) -> p k c", c=P), ACT.Copy).then_inc(S("probT"), 1)

            def out_hi(p):
                act.wait_ge(S("values"), 2 * p + 2)
                f(h_hi[:, p, :], bank[5 + p % 2][:, :], ACT.Copy).then_inc(S("o_hi"), 1)

            for s in range(16 * NT + 2):
                if s < 16 * NT:
                    softmax(s)
                if s >= 2:
                    keep_turned(s - 2)
                    h, q = divmod(s - 2, NT)
                    if q == 3 and h < 6:
                        act.wait_ge(S("row_nmax"), NT * (h + 1))
                        act.dma_start(relb[:, h % 2, :], relb_in[h + 2]).then_inc(S(f"relb_in{h % 2}"), 16)
                    if q % 2:
                        next_modulation(16 + 2 * h + q // 2)
                    if q == 2 and h >= 2 and h % 2 == 0:
                        out_hi(h // 2 - 1)
            out_hi(7)
            norm_squares("ffn2", xT, lambda j: act.wait_ge(S("x_new"), 8 + j + 1))

            act.wait_ge(S("slab_done"), SLAB_AT["gu2"])
            act.dma_start(block2_t[:, :], block2_in).then_inc(S("block2_in"), 16)
            act.dma_start(g2b[0:32, :], g2b_in).then_inc(S("lora_in"), 16)
            norm_hi("ffn2")
            gate_up("gu2", KF)
            norm_squares("final", xT, lambda j: act.wait_ge(S("x_new"), 16 + j + 1))
            act.wait_ge(S("slab_done"), SLAB_AT["in2"])
            for i in range(2):
                act.dma_start(lora[:, i, :], lora_in[:, i, :]).then_inc(S("lora_in"), 16)
            norm_squares("mixpre", xT, lambda j: act.wait_ge(S("norm_lo"), 8 * 3 + j + 1))
            norm_hi("mixpre")

            def raw_in(m):
                act.wait_ge(S("slab_done"), SLAB_AT["in2"] + m + 1)
                if m >= 2:
                    act.wait_ge(S("in2_shifted"), m - 1)
                else:
                    act.wait_ge(S("shift_zero"), 1)
                f(shift[:, m % 2, 4:516], bank[m % 4][:, :], ACT.Copy).then_inc(S("in2_raw"), 1)

            moved = [0]

            def move(name, dst, g, half, n_before, scale=1.0):
                n = MADE * half + n_before
                act.wait_ge(S("rk_mm"), n + 1)
                f(dst[:, g, :], bank[n % 6][:, :], ACT.Copy, scale=scale).then_inc(S("rk_" + name), 1)

            def head_std(stat_name, v, done, eps, scale):
                act.wait_ge(S(stat_name), v)
                g = (v - 1) % 2
                f(rk_rs[:, 8 * g:8 * g + 8], bank[7][:, 0:8], ACT.Sqrt, bias=eps, scale=scale).then_inc(S(done), 1)

            def lora_outs(half):
                for g in range(2):
                    G = 2 * half + g
                    for i, (dst, bias) in enumerate(((rk_w, "w0"), (rk_a, "a0"), (rk_g, None))):
                        act.wait_ge(S("lora_mm"), 3 * G + i + 1)
                        src = bank[4 + (3 * G + i) % 2][:, :]
                        if bias:
                            f(dst[:, g, :], src, ACT.Sigmoid, bias=vec(bias, G)).then_inc(S("lora_out"), 1)
                        else:
                            if half:
                                act.wait_ge(S("rk_out"), 2)
                            f(dst[:, g, :], src, ACT.Copy).then_inc(S("lora_out"), 1)

            def key_squares(half):
                for g in range(2):
                    act.wait_ge(S("rk_kk"), 2 * half + g + 1)
                    f(tmp[:, g, :], mP[:, g, :], ACT.Square).then_inc(S("rk_ksq"), 1)

            def key_stds(half):
                for g in range(2):
                    head_std("rk_kst", 2 * half + g + 1, "rk_rsd", 0.0, 1.0)

            def decays(half):
                for g in range(2):
                    act.wait_ge(S("rk_cum"), 2 * half + g + 1)
                    f(mMR[:, g, :], mO1[:, g, :], ACT.Exp, scale=-DECAY).then_inc(S("rk_exp"), 1)
                    f(mAR[:, g, :], mO1[:, g, :], ACT.Exp, scale=DECAY).then_inc(S("rk_exp"), 1)
                    f(tokQ[:, g, :], mO2[:, g, :], ACT.Exp, scale=-DECAY).then_inc(S("rk_exp"), 1)

            def recurrence(half):
                mW = of_half(rk_k, half)
                for g in range(2):
                    move("tv", tokV, g, half, g)
                for g in range(2):
                    move("tk", tokK, g, half, 2 + 3 * g)
                    move("tb", tokB, g, half, 3 + 3 * g, scale=-1.0)
                    move("tq", tokQ, g, half, 4 + 3 * g)
                for g in range(2):
                    act.wait_ge(S("rk_mm"), MADE * half + 18 + 2 * g + 2)
                    act.wait_ge(S("rk_r0"), 2 * half + g + 1)
                    move("q1", mQ, g, half, 18 + 2 * g)
                    move("p1", mP, g, half, 18 + 2 * g + 1)
                for g in range(2):
                    act.wait_ge(S("rk_mm"), MADE * half + 22 + 3 * g + 3)
                    move("q2", mQ, g, half, 22 + 3 * g + 1)
                    move("p2", mP, g, half, 22 + 3 * g + 2)
                for g in range(2):
                    act.wait_ge(S("rk_mm"), MADE * half + 28 + 2 * g + 2)
                    move("q3", mQ, g, half, 28 + 2 * g + 1)
                if half:
                    for j in range(4):
                        act.wait_ge(S("conv_d"), j + 1)
                        f(tmp[:, j, :], conv_out[:, j, :], ACT.Square).then_inc(S("conv_square"), 1)
                n = 34
                for lvl in (1, 2):
                    for g in range(2):
                        act.wait_ge(S("rk_" + ("r3" if lvl == 1 else "r4")), 2 * half + g + 1)
                        move(f"rt{lvl}", mP, g, half, n + 2 * g)
                        move(f"y{lvl}", mQ, g, half, n + 2 * g + 1)
                    n += 6
                if half:
                    act.wait_ge(S("conv_stat"), 4)
                    f(n_std, bank[7][:, 0:4], ACT.Sqrt, bias=1e-5, scale=1.0 / 512).then_inc(S("conv_std"), 1)
                for g in range(2):
                    move("x", mX, g, half, n + 2 * g)
                    move("w", mW, g, half, n + 2 * g + 1)
                n += 4
                for g in range(2):
                    move("z", mZ, g, half, n + 2 * g)
                n += 8
                for g in range(2):
                    move("y", mP, g, half, n + g)
                for g in range(2):
                    move("d", mQ, g, half, n + 2 + g)
                    act.wait_ge(S("rk_d"), 2 * half + g + 1)
                    f(tmp[:, g, :], mQ[:, g, :], ACT.Square).then_inc(S("rk_dsq"), 1)
                    head_std("rk_dst", 2 * half + g + 1, "rk_dstd", 64e-5, 1.0 / 64)

            for m in range(15):
                raw_in(m)
                if m == 3:
                    act.wait_ge(S("in2_shifted"), 3)
                    f(lora_act[0:CH, 0, :], lora_act[0:CH, 0, :], ACT.Tanh).then_inc(S("lora_act"), 1)
                    f(lora_act[:, 1, :], lora_act[:, 1, :], ACT.Sigmoid).then_inc(S("lora_act"), 1)
                    f(lora_act2[0:32, :], lora_act2[0:32, :], ACT.Sigmoid).then_inc(S("lora_act"), 1)
                if m == 9:
                    lora_outs(0)
                if m == 11:
                    key_squares(0)
                    key_stds(0)
            for j in range(4):
                act.wait_ge(S("slab_done"), SLAB_AT["in2"] + 15 + 2 * j + 2)
                if j >= 1:
                    act.wait_ge(S("in2_raw"), 15 + j)
                f(conv_gate[:, 0, :], bank[(15 + 2 * j + 1) % 4][:, :], ACT.Sigmoid).then_inc(S("conv_gate"), 1)
            for half in range(2):
                if half:
                    lora_outs(1)
                    key_squares(1)
                    key_stds(1)
                decays(half)
                recurrence(half)
            for j in range(4):
                act.wait_ge(S("conv_t"), j + 1)
                f(conv_out[:, j, :], conv_out[:, j, :], ACT.Silu, bias=vec("conv_ln_b", j)).then_inc(S("conv_silu"), 1)
            norm_squares("mixpost", mid_a, lambda j: act.wait_ge(S("mid_a"), j + 1))

            norm_squares("ffnpre", xT, lambda j: act.wait_ge(S("norm_lo"), 8 * 5 + j + 1))
            norm_hi("ffnpre")
            with act.Fori(0, KF // 2) as i:
                for u in range(2):
                    act.wait_ge(S("up_product"), i * 2 + (u + 1))
                    for m in range(2):
                        n = 2 * u + m
                        act.wait_ge(S("slab_done"), i * 4 + (SLAB_AT["up"] + n + 1))
                        w2 = vec_t[:, bass.ds(i * 12 + (VEC_AT["ffn_dw_w"] + 3 * n + 2), 1)]
                        b = vec_t[:, bass.ds(i * 4 + (VEC_AT["ffn_dw_b"] + n), 1)]
                        f(tmp[:, n, :], bank[n][:, :], ACT.Identity, bias=b, scale=w2).then_inc(S("tap2"), 1)
                    act.wait_ge(S("taps"), i * 4 + (4 + 2 * u + 1))
                    f(tmp[:, 2 * u, :], tmp[:, 2 * u, :], ACT.Silu).then_inc(S("up_silu"), 1)
            norm_squares("ffnpost", mid_h, lambda j: act.wait_ge(S("mid_h"), j + 1))

        @block.vector
        def _(dve):
            v = nc.vector
            step = [0]

            def link(ins):
                step[0] += 1
                ins.then_inc(S("vector_step"), 1)
                dve.wait_ge(S("vector_step"), step[0])

            def sum_squares(name, j):
                if not 1 <= j <= 6:
                    return
                q = NORMS.index(name)
                dve.wait_ge(S("norm_square"), 8 * q + j + 1)
                if 6 * q + j > 1:
                    dve.wait_ge(S("norm_acc"), 6 * q + j - 1)
                v.tensor_tensor(tmp[:, 4, :], tmp[:, 4, :], tmp[:, j % 2, :], ALU.add).then_inc(S("norm_acc"), 1)

            def norm_rs(name):
                q = NORMS.index(name)
                dve.wait_ge(S("norm_std"), q + 1)
                v.reciprocal(n_rs, n_std).then_inc(S("norm_rs"), 1)
                dve.wait_ge(S("norm_spread"), q + 1)

            def norm_split(name, gain):
                norm_rs(name)

                def lo(j):
                    dve.wait_ge(S("norm_hi"), 8 * HI_AT[name] + j + 1)
                    t = tmp[:, 4 + j % 2, :]
                    if name in shf:
                        v.scalar_tensor_tensor(out=h_lo[:, j, :], in0=t, scalar=shf[name][:, j:j + 1], in1=h_hi[:, j, :],
                                               op0=ALU.add, op1=ALU.subtract).then_inc(S("norm_lo"), 1)
                    else:
                        v.tensor_tensor(h_lo[:, j, :], t, h_hi[:, j, :], ALU.subtract).then_inc(S("norm_lo"), 1)

                for j in range(KD):
                    if j >= 2:
                        lo(j - 2)
                        dve.wait_ge(S("norm_lo"), 8 * NORMS.index(name) + j - 1)
                    v.scalar_tensor_tensor(out=tmp[:, 4 + j % 2, :], in0=xT[:, j, :], scalar=gain[:, j:j + 1], in1=bank[6][:, :],
                                           op0=ALU.mult, op1=ALU.mult).then_inc(S("norm_t"), 1)
                lo(KD - 2)
                lo(KD - 1)

            def norm_add(name, src, after=None):
                norm_rs(name)
                for j in range(KD):
                    v.scalar_tensor_tensor(out=src[:, j, :], in0=src[:, j, :], scalar=gp[name][:, j:j + 1], in1=bank[6][:, :],
                                           op0=ALU.mult, op1=ALU.mult).then_inc(S("norm_t"), 1)
                    dve.wait_ge(S("norm_t"), 8 * SCALED_AT[name] + j + 1)
                    v.tensor_tensor(xT[:, j, :], xT[:, j, :], src[:, j, :], ALU.add).then_inc(S("norm_lo"), 1)
                    if after:
                        sum_squares(after, j - 1)

            def hidden(i, u, o, product):
                t = tmp[:, 4 + u, :]
                at = i * 2 + u
                dve.wait_ge(S(product), i * 2 + ((o if product == "ff_product" else 0) + u + 3))
                hi = acth_t[:, bass.ds(at * T, T)]
                v.tensor_copy(hi, t).then_inc(S("act_hi"), 1)
                dve.wait_ge(S("act_hi"), i * 2 + (o + u + 1))
                v.tensor_tensor(actl_t[:, bass.ds(at * T, T)], t, hi, ALU.subtract).then_inc(S("act_lo"), 1)

            def gate_up(name, o):
                with dve.Fori(0, KF // 2) as i:
                    for u in range(2):
                        dve.wait_ge(S("silu"), i * 2 + (o + u + 1))
                        dve.wait_ge(S("act_lo"), i * 2 + (o + u + 1))
                        v.tensor_tensor(tmp[:, 4 + u, :], tmp[:, 2 + u, :], bank[2 * u + 1][:, :], ALU.mult)\
                            .then_inc(S("ff_product"), 1)
                        hidden(i, u, o, "ff_product")

            def add_half(o, at, n_slabs, scale, norm):
                for m in range(KD):
                    sum_squares(norm, m - 1)
                    dve.wait_ge(S("slab_done"), at + n_slabs * (m + 1))
                    v.scalar_tensor_tensor(out=xT[:, m, :], in0=bank[m % 4][:, :], scalar=scale, in1=xT[:, m, :],
                                           op0=ALU.mult, op1=ALU.add).then_inc(S("x_new"), 1)

            for name, n in (("ff_product", 2), ("act_lo", 2), ("taps", 4), ("up_product", 2)):
                for _ in range(n):
                    v.memset(small_t[:, 255:256], 0.0).then_inc(S(name), 1)
                    dve.wait_ge(S(name), _ + 1)

            for j in range(KD):
                sum_squares("ffn1", j)
            dve.wait_ge(S("tables_in"), 48)
            norm_split("ffn1", vec("ffn1_norm", 0, 8))
            gate_up("gu1", 0)
            add_half(0, SLAB_AT["down1"], 3, 0.5, "mix")
            norm_split("mix", vec("mix_norm", 0, 8))

            def modulation(a):
                dve.wait_ge(S(f"ada_in{a % 2}"), 16 * (a // 2 + 1))
                if a == 0:
                    dve.wait_ge(S("silu_c"), 1)
                else:
                    dve.wait_ge(S("ada_sum"), a)
                v.tensor_tensor_reduce(out=mod_product, in0=adaw[:, a % 2, :], in1=silc, scale=1.0, scalar=0.0,
                                       op0=ALU.mult, op1=ALU.add, accum_out=mod[:, a:a + 1]).then_inc(S("ada_sum"), 1)

            applied = [0]

            def apply(dst, gain, scale=None):
                r = applied[0]
                dve.wait_ge(S("hd_spread"), r + 1)
                ins = v.scalar_tensor_tensor(out=dst, in0=dst, scalar=gain, in1=bank[6 if r % 2 == 0 else 4][:, :],
                                             op0=ALU.mult, op1=ALU.mult)
                applied[0] += 1
                return ins

            def split_latent(src, hi, lo):
                link(v.tensor_copy(hi, src))
                v.tensor_tensor(lo, src, hi, ALU.subtract).then_inc(S("cq_split"), 1)

            dest = [cq[:, 0, :], cq[:, 1, :], ckv[:, 0, :], kr[:, 0, :]] + [qa[:, j, :] for j in range(4)] + \
                   [ka[:, j, :] for j in range(4)] + [va[:, t, :] for t in range(NT)]
            link(v.tensor_scalar(row_max[:, 0:1], vec("a_q_norm"), 64.0 ** -0.5, None, ALU.mult))
            link(v.tensor_scalar(row_max[:, 1:2], vec("b_q_nope_norm"), 96.0 ** -0.5, None, ALU.mult))
            link(v.tensor_scalar(row_max[:, 2:3], vec("b_q_rope_norm"), 96.0 ** -0.5, None, ALU.mult))
            for m in range(16):
                dve.wait_ge(S("slab_done"), SLAB_AT["in1"] + (m + 1 if m < 12 else 16))
                v.tensor_copy(dest[m], bank[m % 4][:, :]).then_inc(S("in1_raw"), 1)
                if 1 <= m < 13:
                    modulation(m - 1)
                if m == 5:
                    dve.wait_ge(S("hd_std"), 3)
                    v.reciprocal(hd_rs["lat"], hd_rs["lat"]).then_inc(S("hd_rs"), 1)
                if m == 6:
                    dve.wait_ge(S("hd_spread"), 1)
                    link(v.scalar_tensor_tensor(out=cq[:, 0, :], in0=cq[:, 0, :], scalar=vec("b_q_lat_norm", 0),
                                                in1=bank[6][:, :], op0=ALU.mult, op1=ALU.mult))
                    apply(cq[:, 1, :], vec("b_q_lat_norm", 1)).then_inc(S("hd_applied"), 1)
                    dve.wait_ge(S("hd_applied"), 1)
                    for k in range(2):
                        split_latent(cq[:, k, :], cq_hi[:, k, :], cq_lo[:, k, :])
                    apply(ckv[:, 0, :], vec("b_kv_lat_norm")).then_inc(S("hd_applied"), 1)
                    dve.wait_ge(S("hd_applied"), 2)
                    split_latent(ckv[:, 0, :], ckv_hi[:, 0, :], ckv_lo[:, 0, :])
                if m == 8:
                    apply(kr[:, 0, :], vec("b_k_rope_norm")).then_inc(S("hd_applied"), 1)
                if m == 14:
                    dve.wait_ge(S("hd_std"), 4)
                    v.reciprocal(hd_rs["main"], hd_rs["main"]).then_inc(S("hd_rs"), 1)
            raw2 = [qn[:, j, :] for j in range(4)] + [qr[:, j, :] for j in range(2)] + [kn[:, j, :] for j in range(4)] + \
                   [vb[:, t, :] for t in range(NT)]
            latent_mm = 0
            for t in range(14):
                if t in (2, 5, 13):
                    dve.wait_ge(S("slab_done"), SLAB_AT["uq"] + (2, 5, 13).index(t) + 1)
                else:
                    latent_mm += 1
                    dve.wait_ge(S("latent_mm"), latent_mm)
                v.tensor_copy(raw2[t], bank[t % 4][:, :]).then_inc(S("in1_raw"), 1)
                if t < 4:
                    modulation(12 + t)
            dve.wait_ge(S("hd_std"), 7)
            v.reciprocal(hd_rs["up"], hd_rs["up"]).then_inc(S("hd_rs"), 1)
            for j in range(4):
                apply(qa[:, j, :], row_max[:, 0:1]).then_inc(S("hd_applied"), 1)
            for j in range(4):
                apply(ka[:, j, :], vec("a_k_norm")).then_inc(S("hd_applied"), 1)
            for j in range(4):
                apply(qn[:, j, :], row_max[:, 1:2]).then_inc(S("hd_applied"), 1)
            for j in range(2):
                apply(qr[:, j, :], row_max[:, 2:3]).then_inc(S("hd_applied"), 1)
            for j in range(4):
                apply(kn[:, j, :], vec("b_k_nope_norm")).then_inc(S("hd_applied"), 1)
            dve.wait_ge(S("rope_in"), 16)
            for j, m in enumerate((qr[:, 0, :], qr[:, 1, :], kr[:, 0, :])):
                dve.wait_ge(S("swapped"), j + 1)
                link(v.tensor_tensor(m, m, rope[:, 0, :], ALU.mult))
                dve.wait_ge(S("ada_sum"), 16)
                link(v.tensor_tensor(tmp[:, 4, :], bank[j][:, :], rope[:, 1, :], ALU.mult))
                v.tensor_tensor(m, m, tmp[:, 4, :], ALU.add).then_inc(S("roped"), 1)
                dve.wait_ge(S("roped"), j + 1)

            def score_max(s):
                h, q = divmod(s, NT)
                L, c = P * (q + 1), s % 4
                dve.wait_ge(S("scores"), s + 1)
                if s >= 4:
                    dve.wait_ge(S("probs"), s - 3)
                if h < 8:
                    if q == 0:
                        dve.wait_ge(S(f"relb_in{h % 2}"), 16 * (h // 2 + 1))
                    if s >= 3:
                        dve.wait_ge(S("turned"), s - 2)
                    link(v.tensor_tensor_reduce(out=prob[:, s % 3, 0:L], in0=bank[s % 3][:, 0:L],
                                                in1=relb[:, h % 2, T - L:T], scale=1.0, scalar=LOWEST,
                                                op0=ALU.add, op1=ALU.max, accum_out=row_max[:, c:c + 1]))
                    v.tensor_scalar(row_nmax[:, c:c + 1], row_max[:, c:c + 1], -1.0, None, ALU.mult).then_inc(S("row_nmax"), 1)
                else:
                    v.tensor_reduce(row_nmax[:, c:c + 1], bank[s % 3][:, 0:L], AXX, ALU.max, negate=True)\
                        .then_inc(S("row_nmax"), 1)

            def normalise(s):
                L, c = P * (s % NT + 1), s % 4
                dve.wait_ge(S("probs"), s + 1)
                link(v.reciprocal(row_sum[:, c:c + 1], row_sum[:, c:c + 1]))
                v.tensor_scalar(prob[:, s % 3, 0:L], prob[:, s % 3, 0:L], row_sum[:, c:c + 1], None, ALU.mult)\
                    .then_inc(S("probs_normed"), 1)

            def out_lo(p):
                dve.wait_ge(S("o_hi"), p + 1)
                v.tensor_tensor(h_lo[:, p, :], bank[5 + p % 2][:, :], h_hi[:, p, :], ALU.subtract).then_inc(S("o_lo"), 1)

            for s in range(16 * NT + 3):
                if s < 16 * NT:
                    score_max(s)
                if 1 <= s <= 16 * NT:
                    normalise(s - 1)
                    if s % 2 == 0:
                        modulation(16 + s // 2 - 1)
                if s >= 3:
                    h, q = divmod(s - 3, NT)
                    if q == 2 and h >= 2 and h % 2 == 0:
                        out_lo(h // 2 - 1)
            out_lo(7)
            dve.wait_ge(S("ada_sum"), 48)
            link(v.tensor_tensor(mod, mod, vec("ada_b", 0, 48), ALU.add))
            v.scalar_tensor_tensor(out=gs["mixpre"], in0=mod[:, 8:16], scalar=1.0, in1=vec("mix_pre_g", 0, 8),
                                   op0=ALU.add, op1=ALU.mult)
            v.scalar_tensor_tensor(out=gs["ffnpre"], in0=mod[:, 32:40], scalar=1.0, in1=vec("ffn_pre_g", 0, 8),
                                   op0=ALU.add, op1=ALU.mult)
            v.tensor_tensor(gp["mixpost"], mod[:, 16:24], vec("mix_post_g", 0, 8), ALU.mult)
            v.tensor_tensor(gp["ffnpost"], mod[:, 40:48], vec("ffn_post_g", 0, 8), ALU.mult).then_inc(S("mod_ready"), 1)
            add_half(8, SLAB_AT["out1"], 1, 1.0, "ffn2")

            norm_split("ffn2", vec("ffn2_norm", 0, 8))
            gate_up("gu2", KF)
            add_half(16, SLAB_AT["down2"], 3, 0.5, "final")
            norm_rs("final")
            for j in range(KD):
                v.scalar_tensor_tensor(out=xT[:, j, :], in0=xT[:, j, :], scalar=vec("final_norm", j), in1=bank[6][:, :],
                                       op0=ALU.mult, op1=ALU.mult).then_inc(S("norm_lo"), 1)
                sum_squares("mixpre", j - 1)

            dve.wait_ge(S("block2_in"), 16)
            norm_split("mixpre", gs["mixpre"])
            v.memset(tmp_t[:, 2 * T:2 * T + 4], 0.0)
            v.memset(tmp_t[:, 2 * T + 516:2 * T + 520], 0.0).then_inc(S("shift_zero"), 1)
            link(v.tensor_scalar(omka, vec("k_a", 0, 4), -1.0, 1.0, ALU.mult, ALU.add))

            def shifted(m, dst, rows_=slice(0, P)):
                raw = shift[:, m % 2, :]
                dve.wait_ge(S("in2_raw"), m + 1)
                link(v.tensor_tensor(dst, raw[rows_, 3:515], raw[rows_, 4:516], ALU.subtract))
                v.scalar_tensor_tensor(out=dst, in0=dst, scalar=vec("mu", m)[rows_, :], in1=raw[rows_, 4:516],
                                       op0=ALU.mult, op1=ALU.add).then_inc(S("in2_shifted"), 1)

            def move(name, half, n_before, g, ins):
                n = MADE * half + n_before
                dve.wait_ge(S("rk_mm"), n + 1)
                ins(bank[n % 6]).then_inc(S("rk_" + name), 1)

            def masked(dst, src, mask, g):
                return v.tensor_tensor(rows(dst, g), src[:, :].rearrange("p (c t) -> p c t", c=NC), every_chunk(const(mask)), ALU.mult)

            def shifted_half(half, i):
                shifted(3 + 6 * half + i, (rk_r, rk_k, rk_v)[i // 2][:, 2 * half + i % 2, :])

            def prepare(half, g):
                G = 2 * half + g
                r_, k_ = rk_r[:, G, :], rk_k[:, G, :]
                dve.wait_ge(S("in2_shifted"), 9 + 6 * half)
                v.tensor_scalar(mP[:, g, :], k_, vec("k_k", G), None, ALU.mult).then_inc(S("rk_kk"), 1)
                dve.wait_ge(S("lora_out"), 3 * G + 3)
                link(v.tensor_scalar(mQ[:, g, :], rk_a[:, g, :], vec("k_a", G), omka[:, G:G + 1], ALU.mult, ALU.add))
                link(v.tensor_tensor(k_, k_, mQ[:, g, :], ALU.mult))
                v.scalar_tensor_tensor(out=mR[:, g, :], in0=r_, scalar=vec("r_k", G), in1=k_,
                                       op0=ALU.mult, op1=ALU.mult).then_inc(S("rk_bz"), 1)
                link(v.tensor_tensor_scan(mO1[:, g, :], const("keep"), rk_w[:, g, :], 0.0, ALU.mult, ALU.add))
                v.tensor_tensor(mO2[:, g, :], mO1[:, g, :], rk_w[:, g, :], ALU.subtract).then_inc(S("rk_cum"), 1)

            def key_rs(half):
                for g in range(2):
                    r = rk_rs[:, 8 * g:8 * g + 8]
                    dve.wait_ge(S("rk_rsd"), 2 * half + g + 1)
                    link(v.tensor_scalar(r, r, 1e-12, None, ALU.max))
                    v.reciprocal(r, r).then_inc(S("rk_krs"), 1)

            def key_scale(half, g):
                G = 2 * half + g
                dve.wait_ge(S("rk_kspread"), G + 1)
                link(v.tensor_tensor(mP[:, g, :], mP[:, g, :], bank[6][:, :], ALU.mult))
                dve.wait_ge(S("rk_bsum"), G + 1)
                v.tensor_tensor(rk_b[:, g, :], rk_v[:, G, :], bank[7][:, :], ALU.mult).then_inc(S("rk_bonus"), 1)

            taps = [(k, j) for k in range(CONV_K) for j in range(4)]

            def convolve(n):
                for k, j in taps[:n]:
                    w, src = vec("conv_w", CONV_K * j + k), conv_in[:, j, 2 + k:2 + k + T]
                    if k == 0:
                        dve.wait_ge(S("in2_raw"), 15 + j + 1)
                        v.tensor_scalar(conv_out[:, j, :], src, w, vec("conv_b", j), ALU.mult, ALU.add).then_inc(S("conv"), 1)
                        continue
                    dve.wait_ge(S("conv"), 4 * (k - 1) + j + 1)
                    v.scalar_tensor_tensor(out=conv_out[:, j, :], in0=src, scalar=w, in1=conv_out[:, j, :],
                                           op0=ALU.mult, op1=ALU.add).then_inc(S("conv"), 1)
                del taps[:n]

            def recurrence(half):
                n0 = 2 * half
                r_, k_, mS = (of_half(m, half) for m in (rk_r, rk_k, rk_v))
                for g in range(2):
                    dve.wait_ge(S("rk_exp"), 3 * (n0 + g) + 3)
                    link(v.tensor_tensor(rk_a[:, g, :], rk_a[:, g, :], mP[:, g, :], ALU.mult))
                    v.tensor_tensor(rk_a[:, g, :], rk_a[:, g, :], mAR[:, g, :], ALU.mult)
                    v.tensor_tensor(k_[:, g, :], k_[:, g, :], mAR[:, g, :], ALU.mult)
                    v.tensor_tensor(r_[:, g, :], r_[:, g, :], mMR[:, g, :], ALU.mult)
                    v.tensor_copy(d_end[:, 8 * g:8 * g + 8], rows(mMR, g)[:, :, CH - 1])
                    v.tensor_tensor(rk_w[:, g, :], mP[:, g, :], tokQ[:, g, :], ALU.mult).then_inc(S("rk_factors"), 1)
                for g in range(2):
                    move("p0", half, 8 + 5 * g, g, lambda b: masked(mP, b, "np0", g))
                    dve.wait_ge(S("rk_p0"), n0 + g + 1)
                    v.tensor_tensor(rows(mR, g), rows(mP, g), every_chunk(const("eye64")), ALU.add).then_inc(S("rk_r0"), 1)
                    n = MADE * half + 8 + 5 * g + 1
                    dve.wait_ge(S("rk_mm"), n + 1)
                    masked(mO1, bank[n % 6], "off32", g)
                    masked(mO2, bank[n % 6], "off64", g)
                    masked(mQ, bank[n % 6], "nq0", g).then_inc(S("rk_q0"), 1)
                    move("mt", half, 8 + 5 * g + 2, g, lambda b: masked(mMT, b, "su", g))
                    move("ar", half, 8 + 5 * g + 3, g, lambda b: masked(mAR, b, "niu", g))
                    move("mr", half, 8 + 5 * g + 4, g, lambda b: masked(mMR, b, "iu", g))
                    convolve(5)

                def add_r(name, n_before, g, op=ALU.add):
                    move(name, half, n_before, g, lambda b: v.tensor_tensor(mR[:, g, :], mR[:, g, :], b[:, :], op))

                for g in range(2):
                    dve.wait_ge(S("rk_r0"), n0 + g + 1)
                    add_r("r1", 22 + 3 * g, g)
                    convolve(7)
                for g in range(2):
                    dve.wait_ge(S("rk_r1"), n0 + g + 1)
                    add_r("r2", 28 + 2 * g, g)
                    convolve(6)
                for g in range(2):
                    dve.wait_ge(S("rk_r2"), n0 + g + 1)
                    add_r("r3", 32 + g, g)
                    convolve(5)
                if half:
                    convolve(len(taps))
                    dve.wait_ge(S("conv_mean"), 1)
                    for j in range(4):
                        v.tensor_tensor(conv_out[:, j, :], conv_out[:, j, :], bank[6][:, :], ALU.subtract).then_inc(S("conv_d"), 1)
                n = 34
                for lvl in (1, 2):
                    for g in range(2):
                        dve.wait_ge(S("rk_r3" if lvl == 1 else "rk_r4"), n0 + g + 1)
                        add_r("r4" if lvl == 1 else "r5", n + 4 + g, g, ALU.subtract)
                        convolve(6 if lvl == 1 else 4)
                    n += 6
                if half:
                    dve.wait_ge(S("conv_std"), 1)
                    v.reciprocal(n_rs, n_std).then_inc(S("conv_rs"), 1)
                n += 4
                for g in range(2):
                    move("g", half, n + 2 * g + 1, g,
                         lambda b: v.tensor_tensor(rows(mG, g), b[:, :].rearrange("p (c t) -> p c t", c=NC),
                                                   every_chunk(const("eye64")), ALU.add))
                n += 4
                for g in range(2):
                    de = d_end[:, 8 * g:8 * g + 8].unsqueeze(2).to_broadcast([P, NC, CH])
                    move("hd", half, n + 2 * g, g,
                         lambda b: v.tensor_tensor(rows(mHD, g), b[:, :].rearrange("p (c t) -> p c t", c=NC), de, ALU.mult))
                    move("rho", half, n + 2 * g + 1, g,
                         lambda b: v.tensor_tensor(r_[:, g, :], r_[:, g, :], b[:, :], ALU.add))
                n += 4
                if half:
                    dve.wait_ge(S("conv_spread"), 1)
                    for j in range(4):
                        v.scalar_tensor_tensor(out=conv_out[:, j, :], in0=conv_out[:, j, :], scalar=vec("conv_ln_g", j),
                                               in1=bank[6][:, :], op0=ALU.mult, op1=ALU.mult).then_inc(S("conv_t"), 1)
                for c in range(1, NC - 1):
                    for g in range(2):
                        dve.wait_ge(S(f"rk_step{g}"), (NC - 2) * half + c)
                        dve.wait_ge(S("rk_hd"), n0 + g + 1)
                        v.scalar_tensor_tensor(out=mS[:, g, CH * (c + 1):CH * (c + 2)], in0=bank[6 + g][:, CH * c:CH * c + CH],
                                               scalar=d_end[:, 8 * g + c:8 * g + c + 1], in1=mHD[:, g, CH * c:CH * c + CH],
                                               op0=ALU.mult, op1=ALU.add).then_inc(S(f"rk_state{g}"), 1)
                for g in range(2):
                    G = n0 + g
                    r = rk_rs[:, 8 * g:8 * g + 8]
                    dve.wait_ge(S("rk_dstd"), G + 1)
                    v.reciprocal(r, r).then_inc(S("rk_drs"), 1)
                    dve.wait_ge(S("rk_dspread"), G + 1)
                    link(v.scalar_tensor_tensor(out=mP[:, g, :], in0=mQ[:, g, :], scalar=vec("lnx_g", G), in1=bank[6][:, :],
                                                op0=ALU.mult, op1=ALU.mult))
                    link(v.scalar_tensor_tensor(out=mP[:, g, :], in0=mP[:, g, :], scalar=vec("lnx_b", G), in1=rk_b[:, g, :],
                                                op0=ALU.add, op1=ALU.add))
                    v.tensor_tensor(r_[:, g, :], mP[:, g, :], rk_g[:, g, :], ALU.mult).then_inc(S("rk_out"), 1)

            shifted(0, lora_act[:, 0, :])
            shifted(1, lora_act[:, 1, :])
            shifted(2, lora_act2[0:32, :], slice(0, 32))
            for j in range(4):
                v.memset(conv_in[:, j, 0:32], 0.0).then_inc(S("conv_zero"), 1)
            for m in range(3, 15):
                shifted_half((m - 3) // 6, (m - 3) % 6)
                if m in (9, 10):
                    prepare(0, m - 9)
                if m == 11:
                    key_rs(0)
                if m in (13, 14):
                    key_scale(0, m - 13)
            for j in range(4):
                dve.wait_ge(S("conv_gate"), j + 1)
                v.tensor_tensor(conv_in[:, j, 32:], conv_gate[:, 0, :], bank[(15 + 2 * j) % 4][:, :], ALU.mult)\
                    .then_inc(S("in2_raw"), 1)
            dve.wait_ge(S("conv_zero"), 4)
            for half in range(2):
                if half:
                    for g in range(2):
                        prepare(1, g)
                    key_rs(1)
                    for g in range(2):
                        key_scale(1, g)
                recurrence(half)
            dve.wait_ge(S("rk_out"), 4)
            for j in range(8):
                if j < 4:
                    dve.wait_ge(S("conv_silu"), j + 1)
                src = conv_out[:, j, :] if j < 4 else rk_r[:, j - 4, :]
                link(v.tensor_copy(h_hi[:, j, :], src))
                v.tensor_tensor(h_lo[:, j, :], src, h_hi[:, j, :], ALU.subtract).then_inc(S("mix_split"), 1)
            for m in range(KD):
                dve.wait_ge(S("slab_done"), SLAB_AT["out2"] + m + 1)
                sum_squares("mixpost", m - 1)
                v.tensor_copy(mid_a[:, m, :], bank[m % 4][:, :]).then_inc(S("mid_a"), 1)
            norm_add("mixpost", mid_a, "ffnpre")

            norm_split("ffnpre", gs["ffnpre"])
            with dve.Fori(0, KF // 2) as i:
                for u in range(2):
                    for m in range(2):
                        n = 2 * u + m
                        w = [vec_t[:, bass.ds(i * 12 + (VEC_AT["ffn_dw_w"] + 3 * n + k), 1)] for k in range(2)]
                        dve.wait_ge(S("tap2"), i * 4 + (n + 1))
                        v.scalar_tensor_tensor(out=tmp[:, n, 1:T], in0=bank[n][:, 0:T - 1], scalar=w[1], in1=tmp[:, n, 1:T],
                                               op0=ALU.mult, op1=ALU.add).then_inc(S("tap1"), 1)
                        dve.wait_ge(S("tap1"), i * 4 + (n + 1))
                        v.scalar_tensor_tensor(out=tmp[:, n, 2:T], in0=bank[n][:, 0:T - 2], scalar=w[0], in1=tmp[:, n, 2:T],
                                               op0=ALU.mult, op1=ALU.add).then_inc(S("taps"), 1)
                    dve.wait_ge(S("up_silu"), i * 2 + (u + 1))
                    dve.wait_ge(S("taps"), i * 4 + (4 + 2 * u + 2))
                    dve.wait_ge(S("act_lo"), i * 2 + (2 * KF + u + 1))
                    v.tensor_tensor(tmp[:, 4 + u, :], tmp[:, 2 * u, :], tmp[:, 2 * u + 1, :], ALU.mult).then_inc(S("up_product"), 1)
                    hidden(i, u, 2 * KF, "up_product")
            for m in range(KD):
                dve.wait_ge(S("slab_done"), SLAB_AT["down3"] + 3 * (m + 1))
                sum_squares("ffnpost", m - 1)
                v.tensor_copy(mid_h[:, m, :], bank[m % 4][:, :]).then_inc(S("mid_h"), 1)
            norm_add("ffnpost", mid_h)


def _columns(v, n):
    return np.ascontiguousarray(np.asarray(v).reshape(n, P).T)


def _slabs(w, order=None):
    k, m = w.shape[0] // P, w.shape[1] // P
    return w.reshape(k, P, m, P).transpose(2, 1, 0, 3).reshape(m, P, k * P)


def _layout(inp):
    g = {k: np.asarray(v) for k, v in inp.items()}
    w = {k: v[0] for k, v in g.items() if k != "x" and k != "c_2"}

    def padded(a):
        out = np.zeros((a.shape[0], P, SLAB), np.float32)
        out[:, :, :a.shape[2]] = a
        return out

    def gate_up(a, b):
        return np.stack([_slabs(a), _slabs(b)], 1).reshape(2 * KF, P, SLAB)

    def down(a):
        s = _slabs(a)
        return np.concatenate([padded(s[:, :, P * k0:P * k1])[:, None] for k0, k1 in DOWN_CUT], 1).reshape(24, P, SLAB)

    win = w["w_in"]
    kr = win[:, 1920:1952]
    in1 = np.concatenate([win[:, 1536:1920], kr, kr, kr, kr, win[:, 0:1536]], 1)
    values = in1[:, 1536:].reshape(4, 2, P, T).transpose(0, 2, 1, 3).reshape(4, P, SLAB)
    uq = w["b_w_uq"].reshape(256, 8, 96)
    uq = np.concatenate([uq[:, :, :64].reshape(256, 512), uq[:, :, 64:].reshape(256, 256)], 1)
    uq = padded(_slabs(uq).reshape(2, 3, P, 2 * P).transpose(0, 2, 1, 3).reshape(2, P, 6 * P))
    ukv = w["b_w_ukv"].reshape(P, 8, 128)
    ukv = np.concatenate([ukv[:, :, :64].reshape(P, 512), ukv[:, :, 64:].reshape(P, 512)], 1)[None]
    w2 = w["w_in_2"]
    rw, zero = w2[:, 1024:], np.zeros((D, 96), np.float32)
    cols = [rw[:, 1536:1664], rw[:, 1664:1792], np.concatenate([rw[:, 1792:1824], zero], 1)]
    mu = w["rwkv_mu_2"]
    mus = [mu[1536:1664], mu[1664:1792], np.concatenate([mu[1792:1824], zero[0]])]
    for half in range(2):
        for i in range(3):
            a = 512 * i + 256 * half
            cols.append(rw[:, a:a + 256])
            mus.append(mu[a:a + 256])
    for j in range(4):
        cols += [w2[:, P * j:P * j + P], w2[:, 512 + P * j:512 + P * j + P]]
    slabs = np.concatenate([
        gate_up(w["ffn1_w_gate"], w["ffn1_w_up"]), down(w["ffn1_w_down"]), _slabs(in1[:, :1536]), values, uq, ukv, _slabs(w["w_out"]),
        gate_up(w["ffn2_w_gate"], w["ffn2_w_up"]), down(w["ffn2_w_down"]), _slabs(np.concatenate(cols, 1)),
        _slabs(w["w_out_2"]), gate_up(w["w_up_2"][:, :DFF], w["w_up_2"][:, DFF:]), down(w["w_down_2"]),
        np.zeros((N_LOADS - N_SLABS, P, SLAB), np.float32)])
    pair = lambda v, n: _columns(np.tile(v, n), 1)
    dw = w["ffn_dw_w_2"].reshape(3, 2, KF, P).transpose(3, 2, 1, 0).reshape(P, 6 * KF)
    db = w["ffn_dw_b_2"].reshape(2, KF, P).transpose(2, 1, 0).reshape(P, 2 * KF)
    v = {"ffn1_norm": _columns(w["ffn1_norm"], 8), "mix_norm": _columns(w["mix_norm"], 8),
         "a_q_norm": pair(w["a_q_norm"], 2), "a_k_norm": pair(w["a_k_norm"], 2),
         "b_q_lat_norm": _columns(w["b_q_lat_norm"], 2), "b_kv_lat_norm": _columns(w["b_kv_lat_norm"], 1),
         "b_q_nope_norm": pair(w["b_q_nope_norm"], 2), "b_q_rope_norm": pair(w["b_q_rope_norm"], 4),
         "b_k_nope_norm": pair(w["b_k_nope_norm"], 2), "b_k_rope_norm": pair(w["b_k_rope_norm"], 4),
         "ffn2_norm": _columns(w["ffn2_norm"], 8), "final_norm": _columns(w["final_norm"], 8),
         "ada_b": _columns(w["ada_b_2"], 48),
         "mix_pre_g": _columns(w["mix_pre_g_2"], 8), "mix_post_g": _columns(w["mix_post_g_2"], 8),
         "conv_w": w["conv_dw_w_2"].reshape(CONV_K, 4, P).transpose(2, 1, 0).reshape(P, 4 * CONV_K),
         "mu": _columns(np.concatenate(mus), 15), "ffn_dw_w": dw, "ffn_dw_b": db,
         "r_k": _columns(w["r_k_2"].reshape(-1), 4),
         "ffn_pre_g": _columns(w["ffn_pre_g_2"], 8), "ffn_post_g": _columns(w["ffn_post_g_2"], 8)}
    for k, name in (("conv_b", "conv_dw_b_2"), ("conv_ln_g", "conv_ln_g_2"), ("conv_ln_b", "conv_ln_b_2"), ("w0", "w0_2"),
                    ("a0", "a0_2"), ("k_k", "k_k_2"), ("k_a", "k_a_2"), ("lnx_g", "lnx_g_2"), ("lnx_b", "lnx_b_2")):
        v[k] = _columns(w[name], 4)
    p, c = np.arange(P)[:, None], np.arange(T)[None, :]
    rel = np.clip(384 + p - c, -128, 128) + 128
    relb = w["a_rel_bias"][:, rel]
    relb = np.where(((c >= 448) & (p < CH))[None], np.float32(-1e30), relb)
    both, block1, block2, rope = constants()
    lora = np.stack([np.concatenate([w["w2_2"], w["a2_2"]], 0), w["g2_2"][:P]], 1)
    arrays = {
        "x": g["x"][0].T.reshape(KD, P, T).transpose(1, 0, 2), "slabs": slabs,
        "ada": np.concatenate([w["ada_w_2"].T.reshape(48, P, SLAB), np.broadcast_to(g["c_2"][0], (1, P, SLAB))]), "vec": np.concatenate([v[k] for k, _ in VEC_COLS], 1),
        "both": both, "block1": block1, "block2": block2, "rope": rope, "relb": relb, "lora": lora,
        "g2b": w["g2_2"][P:]}
    return {k: np.ascontiguousarray(a) for k, a in arrays.items()}


def kernel(**inputs):
    import concourse.bacc as bacc
    from concourse.bass_utils import run_bass_kernel_spmd

    nc = bacc.Bacc("TRN2", target_bir_lowering=False, num_devices=1)
    arrays = {f"in_{k}": a for k, a in _layout(inputs).items()}
    args = [nc.dram_tensor(k, a.shape, mybir.dt.from_np(a.dtype), kind="ExternalInput").ap() for k, a in arrays.items()]
    y = nc.dram_tensor("out_y", (P, KD, T), F32, kind="ExternalOutput").ap()
    build(nc, *args, y)
    r = run_bass_kernel_spmd(nc, [arrays], core_ids=[0])
    got = r.results[0]["out_y"]
    return np.ascontiguousarray(got.transpose(1, 0, 2).reshape(D, T).T)[None]
```

```python
from contextlib import ExitStack

import numpy as np

import concourse.bass as bass
from concourse import mybir

P = 128
T = 512
NT = T // P
D = 1024
KD = D // P
DFF = 2816
KF = DFF // P
CH = 64
NC = T // CH
RING = 4
SLAB = KD * P
DOWN_CUT = [(0, 8), (8, 16), (16, 22)]
CONV_K = 31
DECAY = float(np.exp(-0.5))
EPS = 1e-6
LOWEST = -3e38

F32 = mybir.dt.float32
F32R = mybir.dt.float32r
ALU = mybir.AluOpType
ACT = mybir.ActivationFunctionType
AXX = mybir.AxisListType.X

SLABS = [("gu1", 2 * KF), ("down1", 24), ("in1", 16), ("uq", 2), ("ukv", 1), ("out1", 8),
         ("gu2", 2 * KF), ("down2", 24), ("in2", 23), ("out2", 8), ("up", 2 * KF), ("down3", 24)]


def starts(items):
    at, n = {}, 0
    for name, count in items:
        at[name] = n
        n += count
    return at, n


SLAB_AT, N_SLABS = starts(SLABS)
N_LOADS = -(-N_SLABS // RING) * RING

VEC_COLS = [("ffn1_norm", 8), ("mix_norm", 8), ("a_q_norm", 1), ("a_k_norm", 1), ("b_q_lat_norm", 2),
            ("b_kv_lat_norm", 1), ("b_q_nope_norm", 1), ("b_q_rope_norm", 1), ("b_k_nope_norm", 1),
            ("b_k_rope_norm", 1), ("ffn2_norm", 8), ("final_norm", 8), ("ada_b", 48),
            ("mix_pre_g", 8), ("mix_post_g", 8), ("conv_w", 4 * CONV_K), ("conv_b", 4),
            ("conv_ln_g", 4), ("conv_ln_b", 4), ("mu", 15), ("w0", 4), ("a0", 4), ("k_k", 4),
            ("k_a", 4), ("r_k", 4), ("lnx_g", 4), ("lnx_b", 4), ("ffn_pre_g", 8), ("ffn_post_g", 8),
            ("ffn_dw_w", 3 * 2 * KF), ("ffn_dw_b", 2 * KF)]
VEC_AT, N_VEC = starts(VEC_COLS)

BOTH_COLS = [("ident", 128), ("head2", 2), ("ones", 1)]
BLOCK1_COLS = [("head4", 4), ("quarter", 1), ("swap", 128), ("maskq", 128), ("maskk", 64)]
BLOCK2_COLS = [("eye64", 64), ("su", 64), ("iu", 64), ("niu", 64), ("np0", 64), ("nq0", 64),
               ("off32", 64), ("off64", 64), ("center", 128), ("block", 128), ("mean512", 128), ("keep", 512)]
BOTH_AT, N_BOTH = starts(BOTH_COLS)
BLOCK1_AT, N_BLOCK1 = starts(BLOCK1_COLS)
BLOCK2_AT, N_BLOCK2 = starts(BLOCK2_COLS)

HI_AT = {"ffn1": 0, "mix": 1, "ffn2": 2, "mixpre": 3, "ffnpre": 4}
SCALED_AT = {"ffn1": 0, "mix": 1, "ffn2": 2, "mixpre": 3, "mixpost": 4, "ffnpre": 5, "ffnpost": 6}
NORMS = ["ffn1", "mix", "ffn2", "mixpre", "mixpost", "ffnpre", "ffnpost"]
LATE = ["ffn1", "mix", "ffn2"]
SUMMED = [n for n in NORMS if n != "ffnpre"]

RK_STEPS = ["tv", "tk tb tq", "ar+p0 mr+mt", "q0", "q1 p1", "x", "p2+r1", "q2", "r2 q3", "r3", "rt1 y1", "r4",
            "rt2 y2", "r5", "w+z", "g+rho", "hd", "y", "d"]


def recurrence_plan():
    plan, made, unit = {}, 0, 0
    order = [(0, step) for step in RK_STEPS[:-1]] + [(1, RK_STEPS[0]), (0, RK_STEPS[-1])] + [(1, step) for step in RK_STEPS[1:]]
    for half, step in order:
        for g in range(2):
            for item in step.split():
                parts = item.split("+")
                unit += unit % 2 if len(parts) == 2 else 0
                made += 1
                for i, name in enumerate(parts):
                    plan[half, name, g] = (made, unit % 6, i, len(parts))
                unit += len(parts)
    return plan


RK_PLAN = recurrence_plan()

LORA = [(0, 0, 4), (0, 1, 5), (0, 2, 4), (1, 0, 5), (1, 1, 4), (1, 2, 5), (2, 2, 6), (3, 2, 7),
        (2, 0, 6), (3, 0, 7), (2, 1, 6), (3, 1, 7)]
LORA_AT = {(G, i): n + 1 for n, (G, i, _) in enumerate(LORA)}

IN1_RAW = ["cq0", "cq1", "ckv0", "kr0"] + [f"qa{j}" for j in range(4)] + [f"ka{j}" for j in range(4)]
LATENT_RAW = ["qn0", "qn1", "qn2", "qn3", "qr0", "qr1", "kn0", "kn1", "kn2", "kn3"]


def constants():
    p = np.arange(P)
    t = np.arange(CH)
    s = p[:, None] % CH
    c = {
        "ident": np.eye(P), "swap": np.eye(P)[:, (p // 32) * 32 + (p + 16) % 32],
        "head2": p[:, None] // 64 == np.arange(2), "head4": p[:, None] // 32 == np.arange(4),
        "ones": np.ones((P, 1)), "quarter": p[:, None] < 32,
        "eye64": s == t, "su": s < t, "iu": s <= t, "niu": -1.0 * (s <= t),
        "np0": -1.0 * ((s < t) & (s // 16 == t // 16)), "nq0": -1.0 * ((s > t) & (s // 16 == t // 16)),
        "off32": (s // 32 == t // 32) & (s // 16 > t // 16),
        "off64": s // 32 > t // 32,
        "keep": np.broadcast_to(np.arange(T) % CH != 0, (P, T)),
        "block": p[:, None] // 64 == p[None, :] // 64,
        "center": np.eye(P) - (p[:, None] // 64 == p[None, :] // 64) / 64.0,
        "mean512": np.full((P, P), 1.0 / 512),
        "maskq": np.broadcast_to(p[None, :] < CH, (P, P)),
        "maskk": np.full((P, CH), -1e30),
    }
    tables = [np.ascontiguousarray(np.concatenate([np.asarray(c[k]).astype(np.float32) for k, _ in cols], 1))
              for cols in (BOTH_COLS, BLOCK1_COLS, BLOCK2_COLS)]
    inv = (1.0 / (np.float32(10000.0) ** (np.arange(0, 32, 2, dtype=np.float32) / np.float32(32)))).astype(np.float32)
    ang = (np.arange(T, dtype=np.float32)[:, None] * inv[None, :]).astype(np.float32)
    j = p % 16
    sign = np.where(p % 32 < 16, -1.0, 1.0)[:, None]
    rope = np.stack([np.cos(ang).T[j], np.sin(ang).T[j] * sign], 1).astype(np.float32)
    return (*tables, np.ascontiguousarray(rope))


def build(nc, x_in, slabs, ada_in, vec_in, both_in, block1_in, block2_in, rope_in, relb_in, lora_in, g2b_in,
          y_out):
    ctx = ExitStack()
    with ctx:
        base = -(-nc.sbuf_base // 64) * 64
        cursor = [base]

        def place(name, cols, dt=F32, offset=None):
            if offset is None:
                offset = cursor[0]
                cursor[0] += -(-4 * cols // 32) * 32
            return nc.alloc_sbuf_tensor_at(name, [P, cols], dt, offset=offset)

        def tiles(t, n, w=T):
            return t[:, 0:n * w].rearrange("p (n w) -> p n w", n=n)

        xT_t = place("xT", KD * T)
        h_at = cursor[0]
        hi_t, lo_t = place("h_hi", KD * T, F32R), place("h_lo", KD * T, F32R)
        wraw_t, whi_t, wlo_t = place("w_raw", RING * SLAB), place("w_hi", RING * SLAB, F32R), place("w_lo", RING * SLAB, F32R)
        tmp_t = place("tmp", 6 * T)
        vec_t, both_t = place("vec", N_VEC), place("both", N_BOTH)
        block_at = cursor[0]
        block2_t = place("block2", N_BLOCK2)
        block1_t = place("block1", N_BLOCK1, offset=block_at)
        mod_t, small_t = place("mod", 48 + 32), place("small", 256)
        g2b_t = place("g2b", T)
        arena = cursor[0]
        acth_t, actl_t = place("act_hi", KF * T, F32R), place("act_lo", KF * T, F32R)
        assert cursor[0] <= nc.sbuf_usable_end, (cursor[0], nc.sbuf_usable_end)
        xT, h_hi, h_lo = tiles(xT_t, KD), tiles(hi_t, KD), tiles(lo_t, KD)
        w_raw, w_hi, w_lo = (tiles(t, RING, SLAB) for t in (wraw_t, whi_t, wlo_t))
        tmp = tiles(tmp_t, 6)
        act_hi, act_lo = tiles(acth_t, KF), tiles(actl_t, KF)

        def slot(name, at, n, dt=F32, w=T):
            assert at * T + n * w <= 2 * KF * T, name
            return tiles(place(name, n * w, dt, offset=arena + 4 * T * at), n, w)

        qa, ka, qn, kn = slot("qa", 0, 4), slot("ka", 4, 4), slot("qn", 8, 4), slot("kn", 12, 4)
        qr, kr, va = slot("qr", 16, 2), slot("kr", 18, 1), slot("va", 19, 4)
        cq, ckv = slot("cq", 23, 2), slot("ckv", 25, 1)
        cq_hi, cq_lo = slot("cq_hi", 26, 2, F32R), slot("cq_lo", 28, 2, F32R)
        ckv_hi, ckv_lo = slot("ckv_hi", 30, 1, F32R), slot("ckv_lo", 31, 1, F32R)
        rope, vb, relb = tmp[:, 0:2, :], slot("vb", 34, 4), slot("relb", 38, 2)
        adaw = slot("adaw", 40, 2, w=SLAB)
        probT = slot("probT", 23, 8)
        prob = slot("prob", 31, 3)
        arena_t = place("in_arena", 2 * KF * T, offset=arena)
        in_arena = tiles(arena_t, 2 * KF)
        in_h = tiles(place("in_h", 2 * KD * T, offset=h_at), 2 * KD)
        conv_in, conv_out, conv_gate = tiles(arena_t, 4, T + 32), in_arena[:, 5:9, :], in_arena[:, 9:10, :]
        rk_r, rk_k, rk_v = (in_arena[:, 10 + 4 * i:14 + 4 * i, :] for i in range(3))
        rk_w, rk_a, rk_g, mP, mQ, mR, mO1, mO2, rk_b, lora, lora_act = (
            in_arena[:, 22 + 2 * i:24 + 2 * i, :] for i in range(11))
        tokV, tokK, mMT, mMR, tokB, mAR, tokQ, mX = (in_h[:, 2 * i:2 * i + 2, :] for i in range(8))
        mZ = rk_a
        gate = [rk_g[:, 0, :], rk_g[:, 1, :], conv_gate[:, 0, :], tmp[:, 4, :]]
        decay_at = ((conv_out[:, 0:2, :], conv_out[:, 2:4, :], mQ), (mMR, mAR, tokQ))
        key_at, prepare_at = (mP, mMT), (mQ, tokK)
        mG, mHD = mO1, mO2
        g2b, lora_act2 = g2b_t, tmp[:, 5, :]
        shift = tmp_t[:, 2 * T:2 * T + 2 * 516].rearrange("p (n w) -> p n w", n=2)

        def of_half(m, half):
            return m[:, 2 * half:2 * half + 2, :]

        mid_a = slot("mid_a", 0, KD)
        mid_h = tiles(place("mid_h", KD * T, offset=h_at), KD)

        bank_pair = [ctx.enter_context(nc.psum_tensor(f"banks{i}", [P, 2 * T], F32)) for i in range(4)]
        bank = [bank_pair[i // 2][:, T * (i % 2):T * (i % 2) + T] for i in range(8)]

        def vec(k, j=0, n=1):
            return vec_t[:, VEC_AT[k] + j:VEC_AT[k] + j + n]

        def const(k):
            for t, at, cols in ((both_t, BOTH_AT, BOTH_COLS), (block1_t, BLOCK1_AT, BLOCK1_COLS),
                                (block2_t, BLOCK2_AT, BLOCK2_COLS)):
                if k in at:
                    return t[:, at[k]:at[k] + dict(cols)[k]]

        ident = const("ident")
        mod = mod_t[:, 0:48]
        gs = {"mixpre": mod_t[:, 48:56], "ffnpre": mod_t[:, 56:64]}
        gp = {"mixpost": mod_t[:, 64:72], "ffnpost": mod_t[:, 72:80]}
        shf = {"mixpre": mod_t[:, 0:8], "ffnpre": mod_t[:, 24:32]}
        n_std, n_rs = small_t[:, 0:4], small_t[:, 4:8]
        both_ms, both_std, both_rs2, both_rs = (small_t[:, 8 + 4 * i:12 + 4 * i] for i in range(4))
        silc, mod_product = tmp_t[:, 2 * T:4 * T], tmp_t[:, 4 * T:6 * T]
        hd_rs = {"lat": small_t[:, 16:28], "main": small_t[:, 28:92], "up": small_t[:, 92:188]}
        gain_q = small_t[:, 200:203]
        row_max, row_nmax, row_sum = small_t[:, 188:192], small_t[:, 192:196], small_t[:, 196:200]
        d_end, omka = small_t[:, 216:232], small_t[:, 232:236]

        sems = {}

        def S(name):
            if name not in sems:
                sems[name] = ctx.enter_context(nc.semaphore(name))
            return sems[name]

        def chunk(m, e, g, c):
            return m[CH * e:CH * e + CH, g, CH * c:CH * c + CH]

        def two_chunks(m, first, apart, e, g, c):
            both = m[CH * e:CH * e + CH, first:first + 2 * apart, :].rearrange("p (n d) w -> p n d w", n=2)
            return both[:, :, g, CH * c:CH * c + CH]

        def made_at(half, name, g):
            _, b, part, parts = RK_PLAN[half, name, g]
            if parts == 1:
                return bank[b].rearrange("p (c t) -> p c t", c=NC)
            return bank_pair[b // 2][:, :].rearrange("p (c n t) -> p c n t", c=NC, n=2)[:, :, part, :]

        def spread_bank(r):
            return 7 if r >= 11 else 6 if r % 2 == 0 else 4

        def rows(m, g=slice(None)):
            return m[:, g, :].rearrange("p (c t) -> p c t", c=NC)

        def every_chunk(t64):
            return t64.unsqueeze(1).to_broadcast([P, NC, CH])

        block = ctx.enter_context(nc.Block())

        @block.sync
        def _(sp):
            for dst, src in ((both_t, both_in), (vec_t, vec_in)):
                sp.dma_start(dst[:, :], src).then_inc(S("tables_in"), 16)
            for h in range(2):
                sp.dma_start(xT[:, 4 * h:4 * h + 4, :], x_in[:, 4 * h:4 * h + 4, :]).then_inc(S(f"x_in{h}"), 16)
                for r in (2 * h, 2 * h + 1):
                    sp.dma_start(w_raw[:, r, :], slabs[r]).then_inc(S(f"w_raw_in{r}"), 16)
            sp.dma_start(block1_t[:, :], block1_in).then_inc(S("block1_in"), 16)
            with sp.Fori(1, N_LOADS // RING) as i:
                for r in range(RING):
                    sp.wait_ge(S("w_split"), i * RING + (r + 1 - RING))
                    sp.dma_start(w_raw[:, r, :], slabs[i * RING + r]).then_inc(S(f"w_raw_in{r}"), 16)
            for j in range(KD):
                sp.wait_ge(S("norm_lo"), 8 * NORMS.index("ffnpost") + j + 1)
                sp.dma_start(y_out[:, j, :], xT[:, j, :]).then_inc(S("y_out"), 16)
            sp.wait_ge(S("y_out"), 16 * KD)

        @block.gpsimd
        def _(pool):
            def split(n, r, loads, first=False):
                pool.wait_ge(S(f"w_raw_in{r}"), loads)
                if not first:
                    pool.wait_ge(S("slab_done"), n + (1 - RING))
                    pool.nop(nofuse=True)
                nc.gpsimd.tensor_scalar(w_hi[:, r, :], w_raw[:, r, :], 1.0, 1.0, ALU.mult, ALU.mult).then_inc(S("w_hi"), 1)
                pool.wait_ge(S("w_hi"), n + 1)
                nc.gpsimd.tensor_tensor(w_lo[:, r, :], w_raw[:, r, :], w_hi[:, r, :], ALU.subtract).then_inc(S("w_split"), 1)

            for r in range(RING):
                split(r, r, 16, first=True)
            with pool.Fori(1, N_LOADS // RING) as i:
                for r in range(RING):
                    split(i * RING + r, r, i * 16 + 16)

        @block.tensor
        def _(pe):
            mm = nc.tensor.matmul
            def passes(out, hi, lo, rhs_hi, rhs_lo, start, stop):
                mm(out, hi, rhs_hi, start=start, stop=False, skip_group_check=True)
                mm(out, hi, rhs_lo, start=False, stop=False, skip_group_check=True)
                return mm(out, lo, rhs_hi, start=False, stop=stop, skip_group_check=True)

            def product(out, n, r, act_h, act_l, ks=range(KD), first=0, start=True, stop=True, wait_k=None, at_slab=0):
                pe.wait_ge(S("w_split"), n + 1)
                for i, k in enumerate(ks):
                    if wait_k is not None:
                        wait_k(k)
                    w = slice(P * (at_slab + i), P * (at_slab + i) + P)
                    hi, lo = w_hi[:, r, w], w_lo[:, r, w]
                    a, b = start and i == 0, stop and i == len(ks) - 1
                    last = passes(out, hi, lo, act_h[:, first + k, :], act_l[:, first + k, :], a, b)
                return last

            def first_two(at, wait_k, wait_bank, late=None):
                for k in range(KD):
                    if late and k == 5:
                        norm_stats(late)
                    for n in range(2):
                        if k == 0:
                            wait_bank(n)
                            pe.wait_ge(S("w_split"), at + n + 1)
                        if n == 0:
                            wait_k(k)
                        w, r = slice(P * k, P * k + P), (at + n) % RING
                        last = passes(bank[n], w_hi[:, r, w], w_lo[:, r, w], h_hi[:, k, :], h_lo[:, k, :], k == 0, k == KD - 1)
                        if k == KD - 1:
                            last.then_inc(S("slab_done"), 1)
                if late:
                    norm_spread(late)

            def turned_passes(out, act_h, act_l, k, t, r, half, start, stop):
                tok, w = slice(P * t, P * t + P), slice(T * half, T * half + T)
                mm(out, act_h[:, k, tok], w_hi[:, r, w], start=start, stop=False, skip_group_check=True)
                mm(out, act_h[:, k, tok], w_lo[:, r, w], start=False, stop=False, skip_group_check=True)
                return mm(out, act_l[:, k, tok], w_hi[:, r, w], start=False, stop=stop, skip_group_check=True)

            def stat(out, square, mask, start, width):
                for t in range(NT):
                    last = mm(out[:, width * t:width * t + width], square[:, P * t:P * t + P], mask,
                              start=start and t == 0, stop=True, skip_group_check=True)
                return last

            def spread(out, cols, heads):
                w = P // heads
                for t in range(NT):
                    for e in range(heads):
                        c = cols[:, heads * t + e:heads * t + e + 1].to_broadcast([P, w])
                        if heads == 1:
                            last = nc.tensor.transpose(out[:, P * t:P * t + P], c, ident)
                        else:
                            last = mm(out[w * e:w * e + w, P * t:P * t + P], c, ident, start=True, stop=True,
                                      skip_group_check=True)
                return last

            def norm_stats(name):
                if name == "ffnpre":
                    for j in range(KD):
                        pe.wait_ge(S("pre_square"), j + 1)
                        stat(bank[7], tmp[:, j % 4, :], const("ones"), j == 0, 1).then_inc(S("pre_stat"), 1)
                    return
                q = SUMMED.index(name)
                pe.wait_ge(S("norm_acc"), 6 * q + 6)
                stat(bank[7], tmp[:, 4, :], const("ones"), True, 1).then_inc(S("norm_stat"), 1)
                pe.wait_ge(S("norm_square"), 8 * q + 8)
                stat(bank[7], tmp[:, 1, :], const("ones"), False, 1).then_inc(S("norm_stat"), 1)

            def gained_stats():
                pe.wait_ge(S("gained_acc"), 6)
                stat(bank[4], tmp[:, 5, :], const("ones"), True, 1).then_inc(S("gained_stat"), 1)
                pe.wait_ge(S("gained_square"), 8)
                stat(bank[4], tmp[:, 3, :], const("ones"), False, 1).then_inc(S("gained_stat"), 1)

            def norm_spread(name):
                q = NORMS.index(name)
                pe.wait_ge(S("norm_rs"), q + 1)
                spread(bank[6], n_rs, 1).then_inc(S("norm_spread"), 1)

            def after_norm(name):
                q = NORMS.index(name)
                return lambda k: pe.wait_ge(S("norm_lo"), 8 * q + k + 1)

            def gate_up(name, o, norm):
                at = SLAB_AT[name]

                def pair(i, u):
                    pe.wait_ge(S("ff_product"), i * 2 + (o + u + 1))
                    for m in range(2):
                        n = 2 * u + m
                        product(bank[n], i * 4 + (at + n), (at + n) % RING, h_hi, h_lo).then_inc(S("slab_done"), 1)

                first_two(at, after_norm(norm), lambda n: pe.wait_ge(S("ff_product"), o + 1), norm)
                pair(0, 1)
                with pe.Fori(1, KF // 2) as i:
                    pair(i, 0)
                    pair(i, 1)

            def down(name, o, done, done_at, norm):
                at = SLAB_AT[name]
                for m in range(KD):
                    if m >= 4:
                        pe.wait_ge(S(done), done_at + m - 3)
                    elif name == "down3":
                        pe.wait_ge(S("taps"), 2 * KF + m + 1)
                    else:
                        pe.wait_ge(S("ff_product"), o + KF + m // 2 + 1)
                    for s, (k0, k1) in enumerate(DOWN_CUT):
                        n = at + 3 * m + s
                        wait_k = (lambda k: pe.wait_ge(S("act_lo"), o + 3 + k)) if m == 0 else None
                        product(bank[m % 4], n, n % RING, act_hi, act_lo, ks=range(k0, k1), start=s == 0, stop=s == 2,
                                wait_k=wait_k).then_inc(S("slab_done"), 1)
                if norm in LATE:
                    return
                norm_stats(norm)
                if norm == "mixpre":
                    gained_stats()
                    pe.wait_ge(S("both_rs"), 1)
                    spread(bank[6], both_rs, 1).then_inc(S("both_spread"), 1)
                    pe.wait_ge(S("norm_rs"), NORMS.index(norm) + 1)
                    spread(bank[5], n_rs, 1).then_inc(S("norm_spread"), 1)
                else:
                    norm_spread(norm)

            pe.wait_ge(S("tables_in"), 32)
            gate_up("gu1", 0, "ffn1")
            down("down1", 0, "x_new", 0, "mix")

            raw_n, spread_n = [0], [0]

            def head_stat(name, bk, col, mask, width, start):
                pe.wait_ge(S("hd_square"), raw_n[0] + 1)
                if raw_n[0] == 0:
                    pe.wait_ge(S("norm_std"), 2)
                stat(bank[bk][:, col:col + NT * width], tmp[:, raw_n[0] % 2, :], const(mask)[:, 0:width], start, width)\
                    .then_inc(S("hd_stat"), 1)
                raw_n[0] += 1

            def head_spread(cols, heads):
                r = spread_n[0]
                if r >= 2:
                    pe.wait_ge(S("hd_applied"), r - 1 if r < 12 else r)
                if r == 0:
                    pe.wait_ge(S("rs_copied"), 2)
                spread(bank[spread_bank(r)], cols, heads).then_inc(S("hd_spread"), 1)
                spread_n[0] += 1

            at = SLAB_AT["in1"]
            stats_in1 = [("cq0", 7, 0, "ones", 1, True), ("cq1", 7, 0, "ones", 1, False), ("ckv0", 7, 4, "ones", 1, False),
                         ("kr0", 7, 8, "quarter", 1, False)] + \
                        [(IN1_RAW[4 + j], 5, 8 * j, "head2", 2, j == 0) for j in range(8)]
            pe.wait_ge(S("block1_in"), 16)
            for m in range(16):
                if m == 0:
                    first_two(at, after_norm("mix"), lambda n: pe.wait_ge(S("x_new"), 5 + n), "mix")
                elif 2 <= m < 12:
                    if m >= 4:
                        pe.wait_ge(S("in1_raw"), m - 3)
                    product(bank[m % 4], at + m, (at + m) % RING, h_hi, h_lo).then_inc(S("slab_done"), 1)
                elif m >= 12:
                    pe.wait_ge(S("w_split"), at + m + 1)
                    for k in (2 * (m - 12), 2 * (m - 12) + 1):
                        for t in range(NT):
                            if k == 0:
                                pe.wait_ge(S("in1_raw"), 9 + t)
                            last = turned_passes(bank[t], h_hi, h_lo, k, t, (at + m) % RING, k % 2, k == 0, k == KD - 1)
                        for j in {2: (0,), 3: (1,), 4: (2,), 5: (3,), 6: (4, 5)}.get(k, ()):
                            if j == 0:
                                pe.wait_ge(S("hd_rs"), 2)
                            head_spread(hd_rs["main"][:, 8 * j:8 * j + 8], 2)
                    last.then_inc(S("slab_done"), 1)
                if 1 <= m <= 12:
                    head_stat(*stats_in1[m - 1])
                if m == 6:
                    pe.wait_ge(S("hd_rs"), 1)
                    head_spread(hd_rs["lat"][:, 0:4], 1)
                    head_spread(hd_rs["lat"][:, 4:8], 1)
                if m == 7:
                    head_spread(hd_rs["lat"][:, 8:12], 1)
            for t in range(14):
                if t < 6:
                    n = SLAB_AT["uq"] + t // 3
                    ks, first, a_hi, a_lo = range(2), 2 * (t % 3), cq_hi, cq_lo
                else:
                    n = SLAB_AT["ukv"]
                    ks, first, a_hi, a_lo = range(1), t - 6, ckv_hi, ckv_lo
                r = n % RING
                if t in (0, 3, 6):
                    pe.wait_ge(S("w_split"), n + 1)
                if t == 0:
                    pe.wait_ge(S("cq_split"), 2)
                if t == 6:
                    pe.wait_ge(S("cq_split"), 3)
                pe.wait_ge(S("in1_raw"), 16 + t - 3)
                for k in ks:
                    w = slice(P * (first + k), P * (first + k) + P)
                    if t < 10:
                        last = passes(bank[t % 4], w_hi[:, r, w], w_lo[:, r, w], a_hi[:, k, :], a_lo[:, k, :],
                                      k == 0, k == len(ks) - 1)
                    else:
                        last = turned_passes(bank[t % 4], a_hi, a_lo, 0, t - 10, r, 1, True, True)
                last.then_inc(S("slab_done" if t in (2, 5, 13) else "latent_mm"), 1)
                if t < 2:
                    head_spread(hd_rs["main"][:, 48 + 8 * t:56 + 8 * t], 2)
                if 2 <= t <= 11:
                    i = t - 2
                    if i < 4:
                        spec = (i * 8, "head2", 2)
                    elif i < 6:
                        spec = (32 + 16 * (i - 4), "head4", 4)
                    else:
                        spec = (64 + 8 * (i - 6), "head2", 2)
                    head_stat(LATENT_RAW[i], 7, *spec, i == 0)

            def late_norm(j):
                if j < 10:
                    if j == 0:
                        pe.wait_ge(S("hd_rs"), 3)
                    at, heads = (8 * j, 2) if j < 4 else (32 + 16 * (j - 4), 4) if j < 6 else (64 + 8 * (j - 6), 2)
                    head_spread(hd_rs["up"][:, at:at + NT * heads], heads)
                    return
                m = (qr[:, 0, :], qr[:, 1, :], kr[:, 0, :])[j - 10]
                pe.wait_ge(S("hd_applied"), 21)
                if j > 10:
                    pe.wait_ge(S("roped"), j - 10)
                mm(bank[7], const("swap"), m, start=True, stop=True).then_inc(S("swapped"), 1)

            def scores(s):
                h, q = divmod(s, NT)
                e, j, out = h % 2, (h % 8) // 2, bank[s % 3]
                L, e64 = P * (q + 1), slice(CH * e, CH * e + CH)
                if s == 0:
                    pe.wait_ge(S("hd_applied"), 11)
                    pe.wait_ge(S("in1_raw"), 30)
                if h == 8 and q == 0:
                    pe.wait_ge(S("roped"), 3)
                if s >= 3:
                    pe.wait_ge(S("probs"), s - 2)
                qs = slice(P * q, P * q + P)
                if h < 8:
                    mm(out[:, 0:L], qa[e64, j, qs], ka[e64, j, 0:L], start=True, stop=True).then_inc(S("scores"), 1)
                    return
                e32 = slice(32 * (h % 4), 32 * (h % 4) + 32)
                mm(out[:, 0:L], qn[e64, j, qs], kn[e64, j, 0:L], start=True, stop=False, skip_group_check=True)
                mm(out[:, 0:L], qr[e32, (h - 8) // 4, qs], kr[e32, 0, 0:L], start=False, stop=False,
                   skip_group_check=True, tile_position=(32 * (h % 4), 0))
                e1 = slice(32 * (h % 4), 32 * (h % 4) + 1)
                mm(out[:, L - CH:L], const("maskq")[e1, :], const("maskk")[e1, :], start=False, stop=True,
                   skip_group_check=True, tile_position=(32 * (h % 4), 0)).then_inc(S("scores"), 1)

            def turn(s):
                pe.wait_ge(S("probs_normed"), s + 1)
                if s >= 2:
                    pe.wait_ge(S("probT"), s - 1)
                for kt in range(s % NT + 1):
                    last = nc.tensor.transpose(bank[3 + s % 2][:, P * kt:P * kt + P], prob[:, s % 3, P * kt:P * kt + P], ident)
                last.then_inc(S("turned"), 1)

            def values(h):
                pe.wait_ge(S("probT"), NT * h + NT)
                if h % 2 == 0 and h >= 4:
                    pe.wait_ge(S("o_lo"), h // 2 - 1)
                v = va if h < 8 else vb
                for kt in range(NT):
                    last = mm(bank[5 + (h // 2) % 2][CH * (h % 2):CH * (h % 2) + CH, P * kt:T],
                              v[:, kt, CH * (h % 8):CH * (h % 8) + CH], probT[:, NT * (h % 2) + kt, P * kt:T],
                              start=kt == 0, stop=kt == NT - 1, skip_group_check=True)
                last.then_inc(S("values"), 1)

            scores(0)
            for s in range(16 * NT + 2):
                if s + 1 < 16 * NT:
                    scores(s + 1)
                if s >= 2:
                    turn(s - 2)
                    if s % 2 and s <= 27:
                        late_norm((s - 3) // 2)
                    if (s - 2) % NT == 0 and s > 2:
                        values((s - 2) // NT - 1)
            values(15)

            def short(name, done, done_at, wait_k):
                at = SLAB_AT[name]
                for m in range(KD):
                    if m >= 4:
                        pe.wait_ge(S(done), done_at + m - 3)
                    product(bank[m % 4], at + m, (at + m) % RING, h_hi, h_lo, wait_k=wait_k if m == 0 else None)\
                        .then_inc(S("slab_done"), 1)

            pe.wait_ge(S("probT"), 16 * NT)
            short("out1", "x_new", 8, lambda k: pe.wait_ge(S("o_lo"), k + 1))

            gate_up("gu2", KF, "ffn2")
            down("down2", KF, "x_new", 16, "mixpre")

            at = SLAB_AT["in2"]

            def project(m):
                if m >= 4:
                    pe.wait_ge(S("in2_raw"), m - 3 if m <= 18 else 16 + (m - 19) // 2)
                product(bank[m % 4], at + m, (at + m) % RING, h_hi, h_lo).then_inc(S("slab_done"), 1)

            last_use = {}

            def free_banks(name, g, half):
                _, b, _, parts = RK_PLAN[half, name, g]
                for bk in range(b, b + parts):
                    if bk in last_use:
                        before, value = last_use[bk]
                        pe.wait_ge(S("rk_" + before), value)
                    last_use[bk] = (name, 2 * half + g + 1)
                return b, parts

            def made_in(pairs, name, g, half):
                b, _ = free_banks(name, g, half)
                for i, (lhs, rhs) in enumerate(pairs):
                    for c in range(NC):
                        for e in range(2):
                            if rhs is None and e == 0:
                                last = nc.tensor.transpose(bank[b][0:CH, CH * c:CH * c + CH], chunk(lhs, 0, g, c), ident[0:CH, 0:CH])
                                continue
                            r = const("eye64")[CH * e:CH * e + CH, :] if rhs is None else chunk(rhs, e, g, c)
                            last = mm(bank[b][CH * e:CH * e + CH, CH * c:CH * c + CH], chunk(lhs, e, g, c), r,
                                      start=i == 0 and c == 0, stop=i == len(pairs) - 1, skip_group_check=True)
                return last.then_inc(S("rk_mm"), 1)

            def made_two(lhs, m, first, apart, name, g, half):
                b, _ = free_banks(name, g, half)
                for c in range(NC):
                    for e in range(2):
                        out = bank[b + c // 4][CH * e:CH * e + CH, P * (c % 4):P * (c % 4) + P]
                        last = mm(out.rearrange("p (n t) -> p n t", n=2), chunk(lhs, e, g, c),
                                  two_chunks(m, first, apart, e, g, c), start=c % 4 == 0, stop=True, skip_group_check=True)
                return last.then_inc(S("rk_mm"), 1)

            def ready(name, g, half):
                pe.wait_ge(S("rk_" + name), 2 * half + g + 1)

            def lora_products(n0, n1):
                for n in range(n0, n1):
                    G, i, b = LORA[n]
                    fs = slice(P * G, P * G + P)
                    if n == 0:
                        pe.wait_ge(S("lora_in"), 48)
                        pe.wait_ge(S("lora_act"), 3)
                    if n >= 2:
                        pe.wait_ge(S("lora_out"), n - 1)
                    out = bank[b]
                    if n == 0:
                        pe.wait_ge(S("x_final"), 8)
                    if i < 2:
                        r = slice(CH * i, CH * i + CH)
                        mm(out[:, :], lora[r, 0, fs], lora_act[r, 0, :], start=True, stop=True).then_inc(S("lora_mm"), 1)
                    else:
                        mm(out[:, :], lora[:, 1, fs], lora_act[:, 1, :], start=True, stop=False)
                        mm(out[:, :], g2b[0:32, fs], lora_act2[0:32, :], start=False, stop=True).then_inc(S("lora_mm"), 1)

            def key_norms(half):
                for g in range(2):
                    pe.wait_ge(S("rk_ksq"), 2 * half + g + 1)
                    if half:
                        pe.wait_ge(S("lora_out"), 10)
                    mm(bank[6 + g][:, :], const("block"), tmp[:, g, :], start=True, stop=True).then_inc(S("rk_kst"), 1)

            def bonus_sum(half, g):
                pe.wait_ge(S("rk_bz"), 2 * half + g + 1)
                if half == 0:
                    pe.wait_ge(S("lora_out"), 6)
                else:
                    pe.wait_ge(S("rk_out"), 2)
                mm(bank[4 + 2 * half + g], const("block"), mR[:, g, :], start=True, stop=True).then_inc(S("rk_bsum"), 1)

            def values_turned(half):
                for g in range(2):
                    pe.wait_ge(S("in2_shifted"), 9 + 6 * half)
                    made_in([(of_half(rk_v, half), None)], "tv", g, half)

            def finish(half):
                for g in range(2):
                    ready("y", g, half)
                    made_plain("d", const("center"), mP, g, half)
                for g in range(2):
                    pe.wait_ge(S("rk_dsq"), 2 * half + g + 1)
                    pe.wait_ge(S("lora_out"), 12)
                    mm(bank[6 + g][:, :], const("block"), tmp[:, 2 + g, :], start=True, stop=True).then_inc(S("rk_dst"), 1)

            def recurrence(half):
                r_, k_, v_ = (of_half(m, half) for m in (rk_r, rk_k, rk_v))
                mW, mS = k_, v_
                for g in range(2):
                    ready("factors", g, half)
                    made_in([(k_, None)], "tk", g, half)
                    made_in([(rk_a, None)], "tb", g, half)
                    made_in([(rk_w, None)], "tq", g, half)
                if half:
                    bonus_sum(1, 0)
                    bonus_sum(1, 1)
                for g in range(2):
                    made_two(rk_a, in_arena, 10 + 2 * half, 12 - 2 * half, "p0", g, half)
                    made_two(k_, in_arena, 10 + 2 * half, 12 - 2 * half, "mt", g, half)
                for g in range(2):
                    made_in([(rk_w, rk_a)], "q0", g, half)
                for g in range(2):
                    ready("p0", g, half)
                    ready("q0", g, half)
                    made_in([(mP, mQ)], "q1", g, half)
                    made_in([(mQ, mP)], "p1", g, half)
                for g in range(2):
                    ready("mt", g, half)
                    made_in([(mMT, tokV)], "x", g, half)
                for g in range(2):
                    ready("r0", g, half)
                    ready("q1", g, half)
                    ready("p1", g, half)
                    made_two(mQ, in_arena, 28, 4, "r1", g, half)
                for g in range(2):
                    made_in([(mP, mQ)], "q2", g, half)
                for g in range(2):
                    ready("r1", g, half)
                    ready("q2", g, half)
                    ready("p2", g, half)
                    made_in([(mQ, mR)], "r2", g, half)
                    made_in([(mP, mQ)], "q3", g, half)
                for g in range(2):
                    ready("r2", g, half)
                    ready("q3", g, half)
                    made_in([(mQ, mR)], "r3", g, half)
                if half == 0:
                    pe.wait_ge(S("rk_kn"), 2)
                    lora_products(6, 10)
                    key_norms(1)
                for lvl, off in ((1, mO1), (2, mO2)):
                    for g in range(2):
                        ready("r3" if lvl == 1 else "r4", g, half)
                        made_in([(mR, None)], f"rt{lvl}", g, half)
                        made_in([(off, mR)], f"y{lvl}", g, half)
                    for g in range(2):
                        ready(f"rt{lvl}", g, half)
                        ready(f"y{lvl}", g, half)
                        made_in([(mP, mQ)], "r4" if lvl == 1 else "r5", g, half)
                    if half:
                        (conv_mean if lvl == 1 else conv_stats)()
                for g in range(2):
                    ready("r5", g, half)
                    ready("tq", g, half)
                    ready("x", g, half)
                    made_two(mR, in_h, 12, 2, "z", g, half)
                for g in range(2):
                    ready("z", g, half)
                    made_two(mW, in_h, 8, 2, "rho", g, half)
                for g in range(2):
                    made_in([(tokK, tokV), (tokB, mZ)], "hd", g, half)
                if half:
                    conv_spread()
                else:
                    pe.wait_ge(S("rk_kn"), 4)
                for c in range(1, NC - 1):
                    for g in range(2):
                        if c == 1:
                            ready("hd", g, half)
                            ready("g", g, half)
                            if half:
                                pe.wait_ge(S("conv_t"), 4)
                        else:
                            pe.wait_ge(S(f"rk_state{g}"), (NC - 2) * half + c - 1)
                        src = mHD if c == 1 else mS
                        for e in range(2):
                            last = mm(bank[6 + g][CH * e:CH * e + CH, CH * c:CH * c + CH], chunk(mG, e, g, c),
                                      chunk(src, e, g, 0 if c == 1 else c), start=True, stop=True, skip_group_check=True)
                        last.then_inc(S(f"rk_step{g}"), 1)
                for g in range(2):
                    pe.wait_ge(S(f"rk_state{g}"), (NC - 2) * (half + 1))
                    ready("rho", g, half)
                    made_y(g, half, r_, mS)

            def made_y(g, half, r_, mS):
                b, _ = free_banks("y", g, half)
                out = bank[b]
                for c in range(NC):
                    for e in range(2):
                        o = out[CH * e:CH * e + CH, CH * c:CH * c + CH]
                        mm(o, chunk(tokV, e, g, c), chunk(mMR, e, g, c), start=c == 0, stop=False, skip_group_check=True)
                        if c:
                            s = mHD if c == 1 else mS
                            mm(o, chunk(s, e, g, 0 if c == 1 else c), chunk(r_, e, g, c), start=False, stop=False,
                               skip_group_check=True)
                        last = mm(o, chunk(mZ, e, g, c), chunk(mAR, e, g, c), start=False, stop=True, skip_group_check=True)
                last.then_inc(S("rk_mm"), 1)

            def made_plain(name, lhs, rhs, g, half):
                b, _ = free_banks(name, g, half)
                out = bank[b]
                mm(out[:, :], lhs, rhs[:, g, :], start=True, stop=True).then_inc(S("rk_mm"), 1)

            def conv_mean():
                pe.wait_ge(S("rk_bonus"), 4)
                for j in range(4):
                    pe.wait_ge(S("conv"), 4 * (CONV_K - 1) + j + 1)
                    last = mm(bank[6][:, :], const("mean512"), conv_out[:, j, :], start=j == 0, stop=j == 3)
                last.then_inc(S("conv_mean"), 1)

            def conv_stats():
                for j in range(4):
                    pe.wait_ge(S("conv_square"), j + 1)
                    stat(bank[7], tmp[:, j, :], const("ones"), j == 0, 1).then_inc(S("conv_stat"), 1)

            def conv_spread():
                pe.wait_ge(S("conv_rs"), 1)
                pe.wait_ge(S("conv_d"), 4)
                spread(bank[6], n_rs, 1).then_inc(S("conv_spread"), 1)

            first_two(at, after_norm("mixpre"), lambda n: pe.wait_ge(S("x_new"), 21 + n))
            for m in range(2, 23):
                project(m)
                if m == 9:
                    lora_products(0, 6)
                if m == 11:
                    key_norms(0)
                if m in (12, 13):
                    bonus_sum(0, m - 12)
            pe.wait_ge(S("in2_raw"), 19)
            pe.wait_ge(S("rk_bonus"), 2)
            values_turned(0)
            recurrence(0)
            lora_products(10, 12)
            values_turned(1)
            finish(0)
            recurrence(1)
            finish(1)

            at = SLAB_AT["out2"]
            pe.wait_ge(S("rk_d"), 4)
            for m in range(NT):
                product(bank[m], at + m, (at + m) % RING, h_hi, h_lo, ks=range(4), stop=False,
                        wait_k=(lambda k: pe.wait_ge(S("mix_split"), k + 1)) if m == 0 else None)
            for m in range(NT):
                product(bank[m], at + m, (at + m) % RING, h_hi, h_lo, ks=range(4, 8), start=False, at_slab=4,
                        wait_k=(lambda k: pe.wait_ge(S("mix_split"), k + 1)) if m == 0 else None)\
                    .then_inc(S("slab_done"), 1)
            for m in range(4, KD):
                pe.wait_ge(S("mid_a"), m - 3)
                product(bank[m % 4], at + m, (at + m) % RING, h_hi, h_lo).then_inc(S("slab_done"), 1)
            norm_stats("mixpost")
            norm_spread("mixpost")

            norm_stats("ffnpre")
            norm_spread("ffnpre")
            at = SLAB_AT["up"]

            def up_pair(i, u):
                for m in range(2):
                    n = 2 * u + m
                    pe.wait_ge(S("taps"), i * 4 + (n + 1))
                    product(bank[n], i * 4 + (at + n), (at + n) % RING, h_hi, h_lo).then_inc(S("slab_done"), 1)

            first_two(at, after_norm("ffnpre"), lambda n: pe.wait_ge(S("taps"), n + 1))
            up_pair(0, 1)
            with pe.Fori(1, KF // 2) as i:
                up_pair(i, 0)
                up_pair(i, 1)
            down("down3", 2 * KF, "mid_h", 0, "ffnpost")

        @block.scalar
        def _(act):
            f = nc.scalar.activation

            def norm_squares(name, src, wait=None):
                if name == "ffnpre":
                    for j in range(KD):
                        wait(j)
                        if j >= 4:
                            act.wait_ge(S("pre_stat"), j - 3)
                        f(tmp[:, j % 4, :], src[:, j, :], ACT.Square).then_inc(S("pre_square"), 1)
                    act.wait_ge(S("pre_stat"), 8)
                    f(n_std, bank[7][:, 0:4], ACT.Sqrt, bias=EPS, scale=1.0 / D).then_inc(S("norm_std"), 1)
                    return
                q = SUMMED.index(name)
                for j in range(KD):
                    if wait is not None:
                        wait(j)
                    if j and name in ("ffn1", "mix"):
                        norm_hi(name, j - 1)
                    if j >= 3:
                        act.wait_ge(S("norm_acc"), 6 * q + j - 2)
                    f(tmp[:, j % 2 if j else 4, :], src[:, j, :], ACT.Square).then_inc(S("norm_square"), 1)
                    if name == "mixpre":
                        if j >= 3:
                            act.wait_ge(S("gained_acc"), j - 2)
                        f(tmp[:, 2 + j % 2 if j else 5, :], src[:, j, :], ACT.Square, scale=vec("final_norm", j))\
                            .then_inc(S("gained_square"), 1)
                if name in LATE:
                    for j in range(KD) if name == "ffn2" else (KD - 1,):
                        norm_hi(name, j)
                act.wait_ge(S("norm_stat"), 2 * q + 2)
                f(n_std, bank[7][:, 0:4], ACT.Sqrt, bias=EPS, scale=1.0 / D).then_inc(S("norm_std"), 1)
                if name == "mixpre":
                    act.wait_ge(S("both_ms"), 1)
                    f(both_std, both_ms, ACT.Sqrt, bias=EPS, scale=1.0 / D).then_inc(S("both_std"), 1)

            def norm_hi(name, only=None):
                for j in range(KD) if only is None else (only,):
                    act.wait_ge(S("norm_t"), 8 * SCALED_AT[name] + j + 1)
                    if name in LATE:
                        f(h_hi[:, j, :], tmp[:, 2 + j % 2, :], ACT.Copy).then_inc(S("norm_hi"), 1)
                        continue
                    if name in shf:
                        f(h_hi[:, j, :], tmp[:, 4 + j % 2, :], ACT.Identity, bias=shf[name][:, j:j + 1]).then_inc(S("norm_hi"), 1)
                    else:
                        f(h_hi[:, j, :], tmp[:, 4 + j % 2, :], ACT.Copy).then_inc(S("norm_hi"), 1)

            def gate_up(name, o):
                at = SLAB_AT[name]
                with act.Fori(0, KF // 2) as i:
                    for u in range(2):
                        act.wait_ge(S("gate_scaled"), i * 2 + (o + u + 1))
                        f(tmp[:, 2 + u, :], tmp[:, 2 + u, :], ACT.Silu).then_inc(S("silu"), 1)

            norm_squares("ffn1", xT, lambda j: act.wait_ge(S(f"x_in{j // 4}"), 16) if j % 4 == 0 else None)
            gate_up("gu1", 0)
            norm_squares("mix", xT, lambda j: act.wait_ge(S("x_new"), j + 1))
            act.wait_ge(S("slab_done"), SLAB_AT["in1"])
            for h in range(2):
                act.dma_start(relb[:, h, :], relb_in[h]).then_inc(S(f"relb_in{h}"), 16)
            for a in range(2):
                act.dma_start(adaw[:, a, :], ada_in[a]).then_inc(S(f"ada_in{a}"), 16)
            act.wait_ge(S("norm_lo"), 16)
            act.dma_start(silc, ada_in[48]).then_inc(S("c_in"), 16)

            def next_modulation(a):
                if a + 2 < 48:
                    act.wait_ge(S("ada_sum"), a + 1)
                    act.dma_start(adaw[:, a % 2, :], ada_in[a + 2]).then_inc(S(f"ada_in{a % 2}"), 16)

            raw = {"cq0": cq[:, 0, :], "cq1": cq[:, 1, :], "ckv0": ckv[:, 0, :], "kr0": kr[:, 0, :]}
            for j in range(4):
                raw |= {f"qa{j}": qa[:, j, :], f"ka{j}": ka[:, j, :], f"qn{j}": qn[:, j, :], f"kn{j}": kn[:, j, :]}
            raw |= {"qr0": qr[:, 0, :], "qr1": qr[:, 1, :]}
            for i, name in enumerate(IN1_RAW + LATENT_RAW):
                act.wait_ge(S("in1_raw"), i + 1 if i < 12 else i + 5)
                if i >= 2:
                    act.wait_ge(S("hd_stat"), i - 1)
                f(tmp[:, i % 2, :], raw[name], ACT.Square).then_inc(S("hd_square"), 1)
                if i == 1:
                    act.wait_ge(S("c_in"), 16)
                    f(silc, silc, ACT.Silu).then_inc(S("silu_c"), 1)
                if 3 <= i < 12:
                    next_modulation(i - 3)
                if i == 3:
                    act.wait_ge(S("hd_stat"), 4)
                    f(hd_rs["lat"][:, 0:4], bank[7][:, 0:4], ACT.Sqrt, bias=EPS, scale=1.0 / 256).then_inc(S("hd_std"), 1)
                    f(hd_rs["lat"][:, 4:8], bank[7][:, 4:8], ACT.Sqrt, bias=EPS, scale=1.0 / 128).then_inc(S("hd_std"), 1)
                    f(hd_rs["lat"][:, 8:12], bank[7][:, 8:12], ACT.Sqrt, bias=EPS, scale=1.0 / 32).then_inc(S("hd_std"), 1)
                if i == 11:
                    act.wait_ge(S("hd_stat"), 12)
                    f(hd_rs["main"], bank[5][:, 0:64], ACT.Sqrt, bias=EPS, scale=1.0 / 64).then_inc(S("hd_std"), 1)
                    for a in range(9, 13):
                        next_modulation(a)
                if 18 <= i < 21:
                    next_modulation(i - 5)
                if i == 21:
                    act.wait_ge(S("hd_stat"), 22)
                    up = hd_rs["up"]
                    f(up[:, 0:32], bank[7][:, 0:32], ACT.Sqrt, bias=EPS, scale=1.0 / 64).then_inc(S("hd_std"), 1)
                    f(up[:, 32:64], bank[7][:, 32:64], ACT.Sqrt, bias=EPS, scale=1.0 / 32).then_inc(S("hd_std"), 1)
                    f(up[:, 64:96], bank[7][:, 64:96], ACT.Sqrt, bias=EPS, scale=1.0 / 64).then_inc(S("hd_std"), 1)
                    act.dma_start(rope, rope_in).then_inc(S("rope_in"), 16)

            def softmax(s):
                h, q = divmod(s, NT)
                L = P * (q + 1)
                act.wait_ge(S("row_nmax"), s + 1)
                if s >= 3:
                    act.wait_ge(S("turned"), s - 2)
                if s >= 4:
                    act.wait_ge(S("probs_normed"), s - 3)
                src = prob[:, s % 3, 0:L] if h < 8 else bank[s % 3][:, 0:L]
                f(prob[:, s % 3, 0:L], src, ACT.Exp, bias=row_nmax[:, s % 4:s % 4 + 1],
                  accum_out=row_sum[:, s % 4:s % 4 + 1]).then_inc(S("probs"), 1)

            def keep_turned(s):
                h, q = divmod(s, NT)
                act.wait_ge(S("turned"), s + 1)
                if q == 0 and h >= 2:
                    act.wait_ge(S("values"), h - 1)
                n = NT * (h % 2)
                f(probT[:, n:n + q + 1, P * q:P * q + P],
                  bank[3 + s % 2][:, 0:P * (q + 1)].rearrange("p (k c) -> p k c", c=P), ACT.Copy).then_inc(S("probT"), 1)

            def out_hi(p):
                act.wait_ge(S("values"), 2 * p + 2)
                f(h_hi[:, p, :], bank[5 + p % 2][:, :], ACT.Copy).then_inc(S("o_hi"), 1)

            for s in range(16 * NT + 2):
                if s < 16 * NT:
                    softmax(s)
                if s >= 2:
                    keep_turned(s - 2)
                    h, q = divmod(s - 2, NT)
                    if q == 3 and h < 6:
                        act.wait_ge(S("row_nmax"), NT * (h + 1))
                        act.dma_start(relb[:, h % 2, :], relb_in[h + 2]).then_inc(S(f"relb_in{h % 2}"), 16)
                    if q % 2:
                        next_modulation(16 + 2 * h + q // 2)
                    if q == 2 and h >= 2 and h % 2 == 0:
                        out_hi(h // 2 - 1)
            out_hi(7)
            norm_squares("ffn2", xT, lambda j: act.wait_ge(S("x_new"), 8 + j + 1))

            act.wait_ge(S("slab_done"), SLAB_AT["gu2"])
            act.dma_start(block2_t[:, :], block2_in).then_inc(S("block2_in"), 16)
            act.dma_start(g2b[0:32, :], g2b_in).then_inc(S("lora_in"), 16)
            gate_up("gu2", KF)
            norm_squares("mixpre", xT, lambda j: act.wait_ge(S("x_new"), 16 + j + 1))
            for i in range(2):
                act.dma_start(lora[:, i, :], lora_in[:, i, :]).then_inc(S("lora_in"), 16)
            norm_hi("mixpre")

            def raw_in(m):
                act.wait_ge(S("slab_done"), SLAB_AT["in2"] + m + 1)
                if m >= 2:
                    act.wait_ge(S("in2_shifted"), m - 1)
                else:
                    act.wait_ge(S("shift_zero"), 1)
                f(shift[:, m % 2, 4:516], bank[m % 4][:, :], ACT.Copy).then_inc(S("in2_raw"), 1)

            def move(name, dst, g, half, scale=1.0):
                act.wait_ge(S("rk_mm"), RK_PLAN[half, name, g][0])
                f(rows(dst, g), made_at(half, name, g), ACT.Copy, scale=scale).then_inc(S("rk_" + name), 1)

            def inverse_root(first, eps, scale, ln, done):
                for g in range(2):
                    f(bank[6 + g][:, :], bank[6 + g][:, :], ACT.Ln, bias=eps, scale=scale).then_inc(S(ln), 1)
                for g in range(2):
                    act.wait_ge(S(ln), first + g + 1)
                    f(bank[6 + g][:, :], bank[6 + g][:, :], ACT.Exp, scale=-0.5).then_inc(S(done), 1)

            def lora_outs(n0, n1):
                for n in range(n0, n1):
                    G, i, b = LORA[n]
                    act.wait_ge(S("lora_mm"), n + 1)
                    if i < 2:
                        dst, bias = (rk_w, rk_a)[i][:, G % 2, :], vec(("w0", "a0")[i], G)
                        f(dst, bank[b], ACT.Sigmoid, bias=bias).then_inc(S("lora_out"), 1)
                    else:
                        f(gate[G], bank[b], ACT.Copy).then_inc(S("lora_out"), 1)

            def key_squares(half):
                for g in range(2):
                    act.wait_ge(S("rk_kk"), 2 * half + g + 1)
                    f(tmp[:, g, :], key_at[half][:, g, :], ACT.Square).then_inc(S("rk_ksq"), 1)

            def key_rs(half):
                act.wait_ge(S("rk_kmax"), 2 * half + 2)
                inverse_root(2 * half, 0.0, 1.0, "rk_kln", "rk_krs")

            def decays(half):
                for g in range(2):
                    act.wait_ge(S("rk_cum"), 2 * half + g + 1)
                    upto, inverse, before = decay_at[half]
                    f(upto[:, g, :], mO1[:, g, :], ACT.Exp, scale=-DECAY).then_inc(S("rk_exp"), 1)
                    f(inverse[:, g, :], mO1[:, g, :], ACT.Exp, scale=DECAY).then_inc(S("rk_exp"), 1)
                    f(before[:, g, :], mO2[:, g, :], ACT.Exp, scale=-DECAY).then_inc(S("rk_exp"), 1)

            def recurrence(half):
                mW = of_half(rk_k, half)
                for g in range(2):
                    move("tk", tokK, g, half)
                    move("tb", tokB, g, half, scale=-1.0)
                    move("tq", tokQ, g, half)
                for g in range(2):
                    act.wait_ge(S("rk_mm"), RK_PLAN[half, "p1", g][0])
                    act.wait_ge(S("rk_r0"), 2 * half + g + 1)
                    move("q1", mQ, g, half)
                    move("p1", mP, g, half)
                for g in range(2):
                    move("x", mX, g, half)
                for g in range(2):
                    move("q2", mQ, g, half)
                for g in range(2):
                    act.wait_ge(S("rk_mm"), RK_PLAN[half, "q3", g][0])
                    move("q3", mQ, g, half)
                if half == 0:
                    lora_outs(6, 10)
                    key_squares(1)
                for lvl in (1, 2):
                    for g in range(2):
                        act.wait_ge(S("rk_" + ("r3" if lvl == 1 else "r4")), 2 * half + g + 1)
                        move(f"rt{lvl}", mP, g, half)
                        move(f"y{lvl}", mQ, g, half)
                    if half == 0 and lvl == 1:
                        key_rs(1)
                if half:
                    for j in range(4):
                        act.wait_ge(S("conv_d"), j + 1)
                        f(tmp[:, j, :], conv_out[:, j, :], ACT.Square).then_inc(S("conv_square"), 1)
                    act.wait_ge(S("conv_stat"), 4)
                    f(n_std, bank[7][:, 0:4], ACT.Sqrt, bias=1e-5, scale=1.0 / 512).then_inc(S("conv_std"), 1)
                for g in range(2):
                    move("w", mW, g, half)
                    move("z", mZ, g, half)
                if half:
                    for j in range(4):
                        act.wait_ge(S("conv_t"), j + 1)
                        f(conv_out[:, j, :], conv_out[:, j, :], ACT.Silu, bias=vec("conv_ln_b", j)).then_inc(S("conv_silu"), 1)
                for g in range(2):
                    move("y", mP, g, half)

            def values_turned(half):
                for g in range(2):
                    move("tv", tokV, g, half)

            def centred(half):
                for g in range(2):
                    move("d", mQ, g, half)
                    act.wait_ge(S("rk_d"), 2 * half + g + 1)
                    f(tmp[:, 2 + g, :], mQ[:, g, :], ACT.Square).then_inc(S("rk_dsq"), 1)

            def centred_rs(half):
                act.wait_ge(S("rk_dst"), 2 * half + 2)
                inverse_root(2 * half, 64e-5, 1.0 / 64, "rk_dln", "rk_drs")

            for m in range(15):
                raw_in(m)
                if m == 3:
                    act.wait_ge(S("in2_shifted"), 3)
                    f(lora_act[0:CH, 0, :], lora_act[0:CH, 0, :], ACT.Tanh).then_inc(S("lora_act"), 1)
                    f(lora_act[:, 1, :], lora_act[:, 1, :], ACT.Sigmoid).then_inc(S("lora_act"), 1)
                    f(lora_act2[0:32, :], lora_act2[0:32, :], ACT.Sigmoid).then_inc(S("lora_act"), 1)
                if m == 9:
                    lora_outs(0, 6)
                if m == 11:
                    key_squares(0)
                    key_rs(0)
            decays(0)
            for j in range(4):
                act.wait_ge(S("slab_done"), SLAB_AT["in2"] + 15 + 2 * j + 2)
                if j >= 1:
                    act.wait_ge(S("in2_raw"), 15 + j)
                f(conv_gate[:, 0, :], bank[(15 + 2 * j + 1) % 4][:, :], ACT.Sigmoid).then_inc(S("conv_gate"), 1)
            values_turned(0)
            recurrence(0)
            lora_outs(10, 12)
            values_turned(1)
            decays(1)
            centred(0)
            centred_rs(0)
            recurrence(1)
            centred(1)
            centred_rs(1)
            norm_squares("mixpost", mid_a, lambda j: act.wait_ge(S("mid_a"), j + 1))

            norm_squares("ffnpre", xT, lambda j: act.wait_ge(S("norm_lo"), 8 * NORMS.index("mixpost") + j + 1))
            norm_hi("ffnpre")
            with act.Fori(0, KF // 2) as i:
                for u in range(2):
                    act.wait_ge(S("up_product"), i * 2 + (u + 1))
                    for m in range(2):
                        n = 2 * u + m
                        act.wait_ge(S("slab_done"), i * 4 + (SLAB_AT["up"] + n + 1))
                        w2 = vec_t[:, bass.ds(i * 12 + (VEC_AT["ffn_dw_w"] + 3 * n + 2), 1)]
                        b = vec_t[:, bass.ds(i * 4 + (VEC_AT["ffn_dw_b"] + n), 1)]
                        f(tmp[:, n, :], bank[n][:, :], ACT.Identity, bias=b, scale=w2).then_inc(S("tap2"), 1)
                    act.wait_ge(S("taps"), i * 4 + (4 + 2 * u + 1))
                    f(tmp[:, 2 * u, :], tmp[:, 2 * u, :], ACT.Silu).then_inc(S("up_silu"), 1)
            norm_squares("ffnpost", mid_h, lambda j: act.wait_ge(S("mid_h"), j + 1))

        @block.vector
        def _(dve):
            v = nc.vector
            step = [0]

            def link(ins):
                step[0] += 1
                ins.then_inc(S("vector_step"), 1)
                dve.wait_ge(S("vector_step"), step[0])

            def sum_squares(name, j):
                if not 1 <= j <= 6:
                    return
                q = SUMMED.index(name)
                dve.wait_ge(S("norm_square"), 8 * q + j + 1)
                if 6 * q + j > 1:
                    dve.wait_ge(S("norm_acc"), 6 * q + j - 1)
                v.tensor_tensor(tmp[:, 4, :], tmp[:, 4, :], tmp[:, j % 2, :], ALU.add).then_inc(S("norm_acc"), 1)
                if name == "mixpre":
                    dve.wait_ge(S("gained_square"), j + 1)
                    if j > 1:
                        dve.wait_ge(S("gained_acc"), j - 1)
                    v.tensor_tensor(tmp[:, 5, :], tmp[:, 5, :], tmp[:, 2 + j % 2, :], ALU.add).then_inc(S("gained_acc"), 1)

            def norm_rs(name):
                q = NORMS.index(name)
                dve.wait_ge(S("norm_std"), q + 1)
                v.reciprocal(n_rs, n_std).then_inc(S("norm_rs"), 1)
                if name == "mixpre":
                    dve.wait_ge(S("norm_rs"), q + 1)
                    link(v.tensor_tensor(both_ms, n_rs, n_rs, ALU.mult))
                    dve.wait_ge(S("gained_stat"), 2)
                    v.tensor_tensor(both_ms, both_ms, bank[4][:, 0:4], ALU.mult).then_inc(S("both_ms"), 1)
                    dve.wait_ge(S("both_std"), 1)
                    link(v.reciprocal(both_rs2, both_std))
                    v.tensor_tensor(both_rs, both_rs2, n_rs, ALU.mult).then_inc(S("both_rs"), 1)
                    dve.wait_ge(S("both_spread"), 1)
                    return
                dve.wait_ge(S("norm_spread"), q + 1)

            def gained(name, gain, j):
                at = 8 * NORMS.index(name)
                if j >= 2:
                    dve.wait_ge(S("norm_lo"), at + j - 1)
                if name != "ffn1":
                    dve.wait_ge(S("x_new"), 16 if name == "ffn2" else j + 1)
                v.tensor_scalar(tmp[:, 2 + j % 2, :], xT[:, j, :], gain[:, j:j + 1], None, ALU.mult).then_inc(S("norm_t"), 1)

            def late_rs(name, dst):
                norm_rs(name)
                v.tensor_copy(dst, bank[6]).then_inc(S("rs_copied"), 1)
                dve.wait_ge(S("rs_copied"), LATE.index(name) + 1)

            def gained_lo(name, j):
                if j < 0:
                    return
                dve.wait_ge(S("norm_hi"), 8 * HI_AT[name] + j + 1)
                v.tensor_tensor(h_lo[:, j, :], tmp[:, 2 + j % 2, :], h_hi[:, j, :], ALU.subtract).then_inc(S("norm_lo"), 1)

            def norm_split(name, gain):
                norm_rs(name)

                def lo(j):
                    dve.wait_ge(S("norm_hi"), 8 * HI_AT[name] + j + 1)
                    t = tmp[:, 4 + j % 2, :]
                    if name in shf:
                        v.scalar_tensor_tensor(out=h_lo[:, j, :], in0=t, scalar=shf[name][:, j:j + 1], in1=h_hi[:, j, :],
                                               op0=ALU.add, op1=ALU.subtract).then_inc(S("norm_lo"), 1)
                    else:
                        v.tensor_tensor(h_lo[:, j, :], t, h_hi[:, j, :], ALU.subtract).then_inc(S("norm_lo"), 1)

                for j in range(KD):
                    if j >= 2:
                        lo(j - 2)
                        dve.wait_ge(S("norm_lo"), 8 * NORMS.index(name) + j - 1)
                    v.scalar_tensor_tensor(out=tmp[:, 4 + j % 2, :], in0=xT[:, j, :], scalar=gain[:, j:j + 1], in1=bank[6][:, :],
                                           op0=ALU.mult, op1=ALU.mult).then_inc(S("norm_t"), 1)
                lo(KD - 2)
                lo(KD - 1)

            def norm_add(name, src):
                norm_rs(name)
                for j in range(KD):
                    v.scalar_tensor_tensor(out=src[:, j, :], in0=src[:, j, :], scalar=gp[name][:, j:j + 1], in1=bank[6][:, :],
                                           op0=ALU.mult, op1=ALU.mult).then_inc(S("norm_t"), 1)
                    dve.wait_ge(S("norm_t"), 8 * SCALED_AT[name] + j + 1)
                    v.tensor_tensor(xT[:, j, :], xT[:, j, :], src[:, j, :], ALU.add).then_inc(S("norm_lo"), 1)

            def hidden(i, u, o, product):
                t = tmp[:, 4 + u, :]
                at = i * 2 + u
                dve.wait_ge(S(product), i * 2 + ((o if product == "ff_product" else 0) + u + 3))
                hi = acth_t[:, bass.ds(at * T, T)]
                v.tensor_copy(hi, t).then_inc(S("act_hi"), 1)
                dve.wait_ge(S("act_hi"), i * 2 + (o + u + 1))
                v.tensor_tensor(actl_t[:, bass.ds(at * T, T)], t, hi, ALU.subtract).then_inc(S("act_lo"), 1)

            def gate_up(name, o):
                at = SLAB_AT[name]
                with dve.Fori(0, KF // 2) as i:
                    for u in range(2):
                        dve.wait_ge(S("slab_done"), i * 4 + (at + 2 * u + 2))
                        dve.wait_ge(S("ff_product"), i * 2 + (o + u + 1))
                        v.tensor_tensor(tmp[:, 2 + u, :], bank[2 * u], tmp[:, 0, :], ALU.mult).then_inc(S("gate_scaled"), 1)
                        dve.wait_ge(S("act_lo"), i * 2 + (o + u + 1))
                        v.tensor_tensor(tmp[:, 4 + u, :], bank[2 * u + 1], tmp[:, 0, :], ALU.mult).then_inc(S("up_scaled"), 1)
                        dve.wait_ge(S("up_scaled"), i * 2 + (o + u + 1))
                        dve.wait_ge(S("silu"), i * 2 + (o + u + 1))
                        v.tensor_tensor(tmp[:, 4 + u, :], tmp[:, 2 + u, :], tmp[:, 4 + u, :], ALU.mult)\
                            .then_inc(S("ff_product"), 1)
                        hidden(i, u, o, "ff_product")

            def add_half(o, at, n_slabs, scale, norm):
                for m in range(KD):
                    sum_squares(norm, m - 1)
                    dve.wait_ge(S("slab_done"), at + n_slabs * (m + 1))
                    v.scalar_tensor_tensor(out=xT[:, m, :], in0=bank[m % 4][:, :], scalar=scale, in1=xT[:, m, :],
                                           op0=ALU.mult, op1=ALU.add).then_inc(S("x_new"), 1)
                    if norm == "mix":
                        gained(norm, vec("mix_norm", 0, 8), m)
                        gained_lo(norm, m - 1)

            for name, n in (("ff_product", 2), ("act_lo", 2), ("taps", 4), ("up_product", 2)):
                for _ in range(n):
                    v.memset(small_t[:, 255:256], 0.0).then_inc(S(name), 1)
                    dve.wait_ge(S(name), _ + 1)

            dve.wait_ge(S("tables_in"), 32)
            for j in range(KD):
                if j % 4 == 0:
                    dve.wait_ge(S(f"x_in{j // 4}"), 16)
                gained("ffn1", vec("ffn1_norm", 0, 8), j)
                sum_squares("ffn1", j)
                gained_lo("ffn1", j - 1)
            gained_lo("ffn1", KD - 1)
            late_rs("ffn1", tmp[:, 0, :])
            gate_up("gu1", 0)
            add_half(0, SLAB_AT["down1"], 3, 0.5, "mix")
            gained_lo("mix", KD - 1)
            rs_copy = vb[:, 0, :]
            late_rs("mix", rs_copy)

            modulated = [0]

            def modulation(a):
                modulated[0] = a + 1
                dve.wait_ge(S(f"ada_in{a % 2}"), 16 * (a // 2 + 1))
                if a == 0:
                    dve.wait_ge(S("silu_c"), 1)
                else:
                    dve.wait_ge(S("ada_sum"), a)
                v.tensor_tensor_reduce(out=mod_product, in0=adaw[:, a % 2, :], in1=silc, scale=1.0, scalar=0.0,
                                       op0=ALU.mult, op1=ALU.add, accum_out=mod[:, a:a + 1]).then_inc(S("ada_sum"), 1)

            applied = [0]

            def apply(dst, gain, scale=None):
                r = applied[0]
                dve.wait_ge(S("hd_spread"), r + 1)
                ins = v.scalar_tensor_tensor(out=dst, in0=dst, scalar=gain, in1=bank[spread_bank(r)],
                                             op0=ALU.mult, op1=ALU.mult)
                applied[0] += 1
                return ins

            def split_latent(src, hi, lo):
                link(v.tensor_copy(hi, src))
                v.tensor_tensor(lo, src, hi, ALU.subtract).then_inc(S("cq_split"), 1)

            dest = [cq[:, 0, :], cq[:, 1, :], ckv[:, 0, :], kr[:, 0, :]] + [qa[:, j, :] for j in range(4)] + \
                   [ka[:, j, :] for j in range(4)] + [va[:, t, :] for t in range(NT)]
            link(v.tensor_scalar(gain_q[:, 0:1], vec("a_q_norm"), 64.0 ** -0.5, None, ALU.mult))
            link(v.tensor_scalar(gain_q[:, 1:2], vec("b_q_nope_norm"), 96.0 ** -0.5, None, ALU.mult))
            link(v.tensor_scalar(gain_q[:, 2:3], vec("b_q_rope_norm"), 96.0 ** -0.5, None, ALU.mult))
            for m in range(16):
                if m == 12:
                    dve.wait_ge(S("hd_std"), 4)
                    v.reciprocal(hd_rs["main"], hd_rs["main"]).then_inc(S("hd_rs"), 1)
                    for j in range(4):
                        apply(qa[:, j, :], gain_q[:, 0:1]).then_inc(S("hd_applied"), 1)
                        modulation(9 + j)
                    for j in range(2):
                        apply(ka[:, j, :], vec("a_k_norm")).then_inc(S("hd_applied"), 1)
                dve.wait_ge(S("slab_done"), SLAB_AT["in1"] + (m + 1 if m < 12 else 16))
                if m < 12:
                    v.tensor_tensor(dest[m], bank[m % 4], rs_copy, ALU.mult).then_inc(S("in1_raw"), 1)
                else:
                    v.tensor_scalar(dest[m], bank[m % 4], n_rs[:, m - 12:m - 11], None, ALU.mult).then_inc(S("in1_raw"), 1)
                if 3 <= m < 12:
                    modulation(m - 3)
                if m == 5:
                    dve.wait_ge(S("hd_std"), 3)
                    v.reciprocal(hd_rs["lat"], hd_rs["lat"]).then_inc(S("hd_rs"), 1)
                if m == 6:
                    dve.wait_ge(S("hd_spread"), 1)
                    link(v.scalar_tensor_tensor(out=cq[:, 0, :], in0=cq[:, 0, :], scalar=vec("b_q_lat_norm", 0),
                                                in1=bank[6][:, :], op0=ALU.mult, op1=ALU.mult))
                    apply(cq[:, 1, :], vec("b_q_lat_norm", 1)).then_inc(S("hd_applied"), 1)
                    dve.wait_ge(S("hd_applied"), 1)
                    for k in range(2):
                        split_latent(cq[:, k, :], cq_hi[:, k, :], cq_lo[:, k, :])
                    apply(ckv[:, 0, :], vec("b_kv_lat_norm")).then_inc(S("hd_applied"), 1)
                    dve.wait_ge(S("hd_applied"), 2)
                    split_latent(ckv[:, 0, :], ckv_hi[:, 0, :], ckv_lo[:, 0, :])
                if m == 8:
                    apply(kr[:, 0, :], vec("b_k_rope_norm")).then_inc(S("hd_applied"), 1)
            raw2 = [qn[:, j, :] for j in range(4)] + [qr[:, j, :] for j in range(2)] + [kn[:, j, :] for j in range(4)] + \
                   [vb[:, t, :] for t in range(NT)]
            latent_mm = 0
            for t in range(14):
                if t in (2, 5, 13):
                    dve.wait_ge(S("slab_done"), SLAB_AT["uq"] + (2, 5, 13).index(t) + 1)
                else:
                    latent_mm += 1
                    dve.wait_ge(S("latent_mm"), latent_mm)
                v.tensor_copy(raw2[t], bank[t % 4][:, :]).then_inc(S("in1_raw"), 1)
                if 1 <= t < 3:
                    apply(ka[:, t + 1, :], vec("a_k_norm")).then_inc(S("hd_applied"), 1)
                if 5 <= t < 8:
                    modulation(t + 8)
            dve.wait_ge(S("hd_std"), 7)
            v.reciprocal(hd_rs["up"], hd_rs["up"]).then_inc(S("hd_rs"), 1)

            def late_norm(j):
                if j < 10:
                    if j < 4:
                        dst, gain = qn[:, j, :], gain_q[:, 1:2]
                    elif j < 6:
                        dst, gain = qr[:, j - 4, :], gain_q[:, 2:3]
                    else:
                        dst, gain = kn[:, j - 6, :], vec("b_k_nope_norm")
                    apply(dst, gain).then_inc(S("hd_applied"), 1)
                    return
                k = j - 10
                m = (qr[:, 0, :], qr[:, 1, :], kr[:, 0, :])[k]
                if k == 0:
                    dve.wait_ge(S("rope_in"), 16)
                dve.wait_ge(S("swapped"), k + 1)
                link(v.tensor_tensor(m, m, rope[:, 0, :], ALU.mult))
                dve.wait_ge(S("ada_sum"), modulated[0])
                link(v.tensor_tensor(tmp[:, 4, :], bank[7], rope[:, 1, :], ALU.mult))
                v.tensor_tensor(m, m, tmp[:, 4, :], ALU.add).then_inc(S("roped"), 1)
                dve.wait_ge(S("roped"), k + 1)

            def score_max(s):
                h, q = divmod(s, NT)
                L, c = P * (q + 1), s % 4
                dve.wait_ge(S("scores"), s + 1)
                if s >= 4:
                    dve.wait_ge(S("probs"), s - 3)
                if h < 8:
                    if q == 0:
                        dve.wait_ge(S(f"relb_in{h % 2}"), 16 * (h // 2 + 1))
                    if s >= 3:
                        dve.wait_ge(S("turned"), s - 2)
                    link(v.tensor_tensor_reduce(out=prob[:, s % 3, 0:L], in0=bank[s % 3][:, 0:L],
                                                in1=relb[:, h % 2, T - L:T], scale=1.0, scalar=LOWEST,
                                                op0=ALU.add, op1=ALU.max, accum_out=row_max[:, c:c + 1]))
                    v.tensor_scalar(row_nmax[:, c:c + 1], row_max[:, c:c + 1], -1.0, None, ALU.mult).then_inc(S("row_nmax"), 1)
                else:
                    v.tensor_reduce(row_nmax[:, c:c + 1], bank[s % 3][:, 0:L], AXX, ALU.max, negate=True)\
                        .then_inc(S("row_nmax"), 1)

            def normalise(s):
                L, c = P * (s % NT + 1), s % 4
                dve.wait_ge(S("probs"), s + 1)
                link(v.reciprocal(row_sum[:, c:c + 1], row_sum[:, c:c + 1]))
                v.tensor_scalar(prob[:, s % 3, 0:L], prob[:, s % 3, 0:L], row_sum[:, c:c + 1], None, ALU.mult)\
                    .then_inc(S("probs_normed"), 1)

            def out_lo(p):
                dve.wait_ge(S("o_hi"), p + 1)
                v.tensor_tensor(h_lo[:, p, :], bank[5 + p % 2][:, :], h_hi[:, p, :], ALU.subtract).then_inc(S("o_lo"), 1)

            for s in range(16 * NT + 3):
                if s < 16 * NT:
                    score_max(s)
                if 1 <= s <= 16 * NT:
                    normalise(s - 1)
                    if s % 2 == 0:
                        modulation(16 + s // 2 - 1)
                if s % 2 and 3 <= s <= 27:
                    late_norm((s - 3) // 2)
                if s >= 3:
                    h, q = divmod(s - 3, NT)
                    if q == 2 and h >= 2 and h % 2 == 0:
                        out_lo(h // 2 - 1)
            out_lo(7)
            dve.wait_ge(S("ada_sum"), 48)
            link(v.tensor_tensor(mod, mod, vec("ada_b", 0, 48), ALU.add))
            v.scalar_tensor_tensor(out=gs["mixpre"], in0=mod[:, 8:16], scalar=1.0, in1=vec("mix_pre_g", 0, 8),
                                   op0=ALU.add, op1=ALU.mult).then_inc(S("gain_made"), 1)
            dve.wait_ge(S("gain_made"), 1)
            v.tensor_tensor(gs["mixpre"], gs["mixpre"], vec("final_norm", 0, 8), ALU.mult)
            v.scalar_tensor_tensor(out=gs["ffnpre"], in0=mod[:, 32:40], scalar=1.0, in1=vec("ffn_pre_g", 0, 8),
                                   op0=ALU.add, op1=ALU.mult)
            v.tensor_tensor(gp["mixpost"], mod[:, 16:24], vec("mix_post_g", 0, 8), ALU.mult)
            v.tensor_tensor(gp["ffnpost"], mod[:, 40:48], vec("ffn_post_g", 0, 8), ALU.mult).then_inc(S("mod_ready"), 1)
            add_half(8, SLAB_AT["out1"], 1, 1.0, "ffn2")

            for j in range(KD):
                gained("ffn2", vec("ffn2_norm", 0, 8), j)
                gained_lo("ffn2", j - 1)
            gained_lo("ffn2", KD - 1)
            late_rs("ffn2", tmp[:, 0, :])
            gate_up("gu2", KF)
            add_half(16, SLAB_AT["down2"], 3, 0.5, "mixpre")
            dve.wait_ge(S("block2_in"), 16)
            norm_split("mixpre", gs["mixpre"])
            v.memset(tmp_t[:, 2 * T:2 * T + 4], 0.0)
            v.memset(tmp_t[:, 2 * T + 516:2 * T + 520], 0.0).then_inc(S("shift_zero"), 1)
            link(v.tensor_scalar(omka, vec("k_a", 0, 4), -1.0, 1.0, ALU.mult, ALU.add))

            def shifted(m, dst, rows_=slice(0, P)):
                raw = shift[:, m % 2, :]
                dve.wait_ge(S("in2_raw"), m + 1)
                link(v.tensor_tensor(dst, raw[rows_, 3:515], raw[rows_, 4:516], ALU.subtract))
                v.scalar_tensor_tensor(out=dst, in0=dst, scalar=vec("mu", m)[rows_, :], in1=raw[rows_, 4:516],
                                       op0=ALU.mult, op1=ALU.add).then_inc(S("in2_shifted"), 1)

            def move(name, half, g, ins):
                dve.wait_ge(S("rk_mm"), RK_PLAN[half, name, g][0])
                ins(made_at(half, name, g)).then_inc(S("rk_" + name), 1)

            def masked(dst, src, mask, g):
                return v.tensor_tensor(rows(dst, g), src, every_chunk(const(mask)), ALU.mult)

            def shifted_half(half, i):
                shifted(3 + 6 * half + i, (rk_r, rk_k, rk_v)[i // 2][:, 2 * half + i % 2, :])

            def keys(half, g):
                dve.wait_ge(S("in2_shifted"), 9 + 6 * half)
                v.tensor_scalar(key_at[half][:, g, :], rk_k[:, 2 * half + g, :], vec("k_k", 2 * half + g), None, ALU.mult)\
                    .then_inc(S("rk_kk"), 1)

            def prepare(half, g):
                G = 2 * half + g
                r_, k_, t = rk_r[:, G, :], rk_k[:, G, :], prepare_at[half][:, g, :]
                dve.wait_ge(S("lora_out"), LORA_AT[G, 0])
                link(v.tensor_tensor_scan(mO1[:, g, :], const("keep"), rk_w[:, g, :], 0.0, ALU.mult, ALU.add))
                v.tensor_tensor(mO2[:, g, :], mO1[:, g, :], rk_w[:, g, :], ALU.subtract).then_inc(S("rk_cum"), 1)
                dve.wait_ge(S("lora_out"), LORA_AT[G, 1])
                link(v.tensor_scalar(t, rk_a[:, g, :], vec("k_a", G), omka[:, G:G + 1], ALU.mult, ALU.add))
                link(v.tensor_tensor(k_, k_, t, ALU.mult))
                v.scalar_tensor_tensor(out=mR[:, g, :], in0=r_, scalar=vec("r_k", G), in1=k_,
                                       op0=ALU.mult, op1=ALU.mult).then_inc(S("rk_bz"), 1)

            def key_floor(half):
                for g in range(2):
                    dve.wait_ge(S("rk_kst"), 2 * half + g + 1)
                    v.tensor_scalar(bank[6 + g][:, :], bank[6 + g][:, :], 1e-24, None, ALU.max).then_inc(S("rk_kmax"), 1)

            def key_scale(half, g):
                dve.wait_ge(S("rk_krs"), 2 * half + g + 1)
                v.tensor_tensor(key_at[half][:, g, :], key_at[half][:, g, :], bank[6 + g][:, :], ALU.mult).then_inc(S("rk_kn"), 1)

            def bonus(half, g):
                G = 2 * half + g
                dve.wait_ge(S("rk_bsum"), G + 1)
                v.tensor_tensor(rk_b[:, g, :], rk_v[:, G, :], bank[4 + 2 * half + g], ALU.mult).then_inc(S("rk_bonus"), 1)

            taps = [(k, j) for k in range(CONV_K) for j in range(4)]

            def convolve(n):
                for k, j in taps[:n]:
                    w, src = vec("conv_w", CONV_K * j + k), conv_in[:, j, 2 + k:2 + k + T]
                    if k == 0:
                        dve.wait_ge(S("in2_raw"), 15 + j + 1)
                        v.tensor_scalar(conv_out[:, j, :], src, w, vec("conv_b", j), ALU.mult, ALU.add).then_inc(S("conv"), 1)
                        continue
                    dve.wait_ge(S("conv"), 4 * (k - 1) + j + 1)
                    v.scalar_tensor_tensor(out=conv_out[:, j, :], in0=src, scalar=w, in1=conv_out[:, j, :],
                                           op0=ALU.mult, op1=ALU.add).then_inc(S("conv"), 1)
                del taps[:n]

            def factors(half):
                n0 = 2 * half
                r_, k_, kn_ = of_half(rk_r, half), of_half(rk_k, half), key_at[half]
                upto, inverse, before = decay_at[half]
                for g in range(2):
                    dve.wait_ge(S("rk_exp"), 3 * (n0 + g) + 3)
                    dve.wait_ge(S("rk_kn"), n0 + g + 1)
                    link(v.tensor_tensor(rk_a[:, g, :], rk_a[:, g, :], kn_[:, g, :], ALU.mult))
                    v.tensor_tensor(rk_a[:, g, :], rk_a[:, g, :], inverse[:, g, :], ALU.mult)
                    v.tensor_tensor(k_[:, g, :], k_[:, g, :], inverse[:, g, :], ALU.mult)
                    v.tensor_tensor(r_[:, g, :], r_[:, g, :], upto[:, g, :], ALU.mult)
                    v.tensor_copy(d_end[:, 8 * g:8 * g + 8], rows(upto, g)[:, :, CH - 1])
                    v.tensor_tensor(rk_w[:, g, :], kn_[:, g, :], before[:, g, :], ALU.mult).then_inc(S("rk_factors"), 1)

            def recurrence(half):
                n0 = 2 * half
                r_, mS = of_half(rk_r, half), of_half(rk_v, half)
                for g in range(2):
                    move("ar", half, g, lambda b: masked(mAR, b, "niu", g))
                    move("p0", half, g, lambda b: masked(mP, b, "np0", g))
                    dve.wait_ge(S("rk_p0"), n0 + g + 1)
                    v.tensor_tensor(rows(mR, g), rows(mP, g), every_chunk(const("eye64")), ALU.add).then_inc(S("rk_r0"), 1)
                    move("mr", half, g, lambda b: masked(mMR, b, "iu", g))
                    move("mt", half, g, lambda b: masked(mMT, b, "su", g))
                for g in range(2):
                    dve.wait_ge(S("rk_mm"), RK_PLAN[half, "q0", g][0])
                    b = made_at(half, "q0", g)
                    masked(mO1, b, "off32", g)
                    masked(mO2, b, "off64", g)
                    masked(mQ, b, "nq0", g).then_inc(S("rk_q0"), 1)
                convolve(10)

                def add_r(name, g, op=ALU.add):
                    move(name, half, g, lambda b: v.tensor_tensor(rows(mR, g), rows(mR, g), b, op))

                for g in range(2):
                    dve.wait_ge(S("rk_r0"), n0 + g + 1)
                    add_r("r1", g)
                    dve.wait_ge(S("rk_mm"), RK_PLAN[half, "q2", g][0])
                    move("p2", half, g, lambda b: v.tensor_copy(rows(mP, g), b))
                    convolve(4)
                for g in range(2):
                    dve.wait_ge(S("rk_r1"), n0 + g + 1)
                    add_r("r2", g)
                    if half == 0:
                        dve.wait_ge(S("rk_mm"), RK_PLAN[0, "x", 1][0])
                        keys(1, g)
                    convolve(5)
                for g in range(2):
                    dve.wait_ge(S("rk_r2"), n0 + g + 1)
                    add_r("r3", g)
                    convolve(len(taps) if half and g else 7)
                if half == 0:
                    key_floor(1)
                for lvl in (1, 2):
                    for g in range(2):
                        dve.wait_ge(S("rk_r3" if lvl == 1 else "rk_r4"), n0 + g + 1)
                        add_r("r4" if lvl == 1 else "r5", g, ALU.subtract)
                        if half == 0:
                            convolve(8 if lvl == 1 else 5)
                    if half and lvl == 1:
                        dve.wait_ge(S("conv_mean"), 1)
                        for j in range(4):
                            v.tensor_tensor(conv_out[:, j, :], conv_out[:, j, :], bank[6][:, :], ALU.subtract)\
                                .then_inc(S("conv_d"), 1)
                if half == 0:
                    key_scale(1, 0)
                    key_scale(1, 1)
                if half:
                    dve.wait_ge(S("conv_std"), 1)
                    v.reciprocal(n_rs, n_std).then_inc(S("conv_rs"), 1)
                for g in range(2):
                    move("g", half, g, lambda b: v.tensor_tensor(rows(mG, g), b, every_chunk(const("eye64")), ALU.add))
                    move("rho", half, g, lambda b: v.tensor_tensor(rows(r_, g), rows(r_, g), b, ALU.add))
                for g in range(2):
                    de = d_end[:, 8 * g:8 * g + 8].unsqueeze(2).to_broadcast([P, NC, CH])
                    move("hd", half, g, lambda b: v.tensor_tensor(rows(mHD, g), b, de, ALU.mult))
                if half:
                    dve.wait_ge(S("conv_spread"), 1)
                    for j in range(4):
                        v.scalar_tensor_tensor(out=conv_out[:, j, :], in0=conv_out[:, j, :], scalar=vec("conv_ln_g", j),
                                               in1=bank[6][:, :], op0=ALU.mult, op1=ALU.mult).then_inc(S("conv_t"), 1)
                for c in range(1, NC - 1):
                    for g in range(2):
                        dve.wait_ge(S(f"rk_step{g}"), (NC - 2) * half + c)
                        dve.wait_ge(S("rk_hd"), n0 + g + 1)
                        v.scalar_tensor_tensor(out=mS[:, g, CH * (c + 1):CH * (c + 2)], in0=bank[6 + g][:, CH * c:CH * c + CH],
                                               scalar=d_end[:, 8 * g + c:8 * g + c + 1], in1=mHD[:, g, CH * c:CH * c + CH],
                                               op0=ALU.mult, op1=ALU.add).then_inc(S(f"rk_state{g}"), 1)

            def out(half):
                r_ = of_half(rk_r, half)
                for g in range(2):
                    G = 2 * half + g
                    dve.wait_ge(S("rk_drs"), G + 1)
                    link(v.scalar_tensor_tensor(out=mP[:, g, :], in0=mQ[:, g, :], scalar=vec("lnx_g", G), in1=bank[6 + g][:, :],
                                                op0=ALU.mult, op1=ALU.mult))
                    link(v.scalar_tensor_tensor(out=mP[:, g, :], in0=mP[:, g, :], scalar=vec("lnx_b", G), in1=rk_b[:, g, :],
                                                op0=ALU.add, op1=ALU.add))
                    v.tensor_tensor(r_[:, g, :], mP[:, g, :], gate[G], ALU.mult).then_inc(S("rk_out"), 1)

            def final_norm(j):
                if j == 0:
                    dve.wait_ge(S("norm_spread"), NORMS.index("mixpre") + 1)
                v.scalar_tensor_tensor(out=xT[:, j, :], in0=xT[:, j, :], scalar=vec("final_norm", j), in1=bank[5],
                                       op0=ALU.mult, op1=ALU.mult).then_inc(S("x_final"), 1)

            final_norm(0)
            final_norm(1)
            shifted(0, lora_act[:, 0, :])
            shifted(1, lora_act[:, 1, :])
            shifted(2, lora_act2[0:32, :], slice(0, 32))
            for j in range(4):
                v.memset(conv_in[:, j, 0:32], 0.0).then_inc(S("conv_zero"), 1)
            for m in range(3, 15):
                shifted_half((m - 3) // 6, (m - 3) % 6)
                if m < 9:
                    final_norm(m - 1)
                if m in (9, 10):
                    keys(0, m - 9)
                    prepare(0, m - 9)
                if m == 11:
                    key_floor(0)
                if m in (13, 14):
                    key_scale(0, m - 13)
                    bonus(0, m - 13)
            for j in range(4):
                dve.wait_ge(S("conv_gate"), j + 1)
                v.tensor_tensor(conv_in[:, j, 32:], conv_gate[:, 0, :], bank[(15 + 2 * j) % 4][:, :], ALU.mult)\
                    .then_inc(S("in2_raw"), 1)
                if j == 0:
                    factors(0)
            dve.wait_ge(S("conv_zero"), 4)
            def mix_split(j):
                src = conv_out[:, j, :] if j < 4 else rk_r[:, j - 4, :]
                link(v.tensor_copy(h_hi[:, j, :], src))
                v.tensor_tensor(h_lo[:, j, :], src, h_hi[:, j, :], ALU.subtract).then_inc(S("mix_split"), 1)

            recurrence(0)
            dve.wait_ge(S("rk_mm"), RK_PLAN[0, "y", 1][0])
            for g in range(2):
                prepare(1, g)
            factors(1)
            out(0)
            for g in range(2):
                bonus(1, g)
            recurrence(1)
            dve.wait_ge(S("rk_mm"), RK_PLAN[1, "y", 1][0])
            for j in range(4):
                dve.wait_ge(S("conv_silu"), j + 1)
                mix_split(j)
            out(1)
            dve.wait_ge(S("rk_out"), 4)
            for j in range(4, 8):
                mix_split(j)
            for m in range(KD):
                dve.wait_ge(S("slab_done"), SLAB_AT["out2"] + m + 1)
                sum_squares("mixpost", m - 1)
                v.tensor_copy(mid_a[:, m, :], bank[m % 4][:, :]).then_inc(S("mid_a"), 1)
            dve.wait_ge(S("x_final"), 8)
            norm_add("mixpost", mid_a)

            norm_split("ffnpre", gs["ffnpre"])
            with dve.Fori(0, KF // 2) as i:
                for u in range(2):
                    for m in range(2):
                        n = 2 * u + m
                        w = [vec_t[:, bass.ds(i * 12 + (VEC_AT["ffn_dw_w"] + 3 * n + k), 1)] for k in range(2)]
                        dve.wait_ge(S("tap2"), i * 4 + (n + 1))
                        v.scalar_tensor_tensor(out=tmp[:, n, 1:T], in0=bank[n][:, 0:T - 1], scalar=w[1], in1=tmp[:, n, 1:T],
                                               op0=ALU.mult, op1=ALU.add).then_inc(S("tap1"), 1)
                        dve.wait_ge(S("tap1"), i * 4 + (n + 1))
                        v.scalar_tensor_tensor(out=tmp[:, n, 2:T], in0=bank[n][:, 0:T - 2], scalar=w[0], in1=tmp[:, n, 2:T],
                                               op0=ALU.mult, op1=ALU.add).then_inc(S("taps"), 1)
                    dve.wait_ge(S("up_silu"), i * 2 + (u + 1))
                    dve.wait_ge(S("taps"), i * 4 + (4 + 2 * u + 2))
                    dve.wait_ge(S("act_lo"), i * 2 + (2 * KF + u + 1))
                    v.tensor_tensor(tmp[:, 4 + u, :], tmp[:, 2 * u, :], tmp[:, 2 * u + 1, :], ALU.mult).then_inc(S("up_product"), 1)
                    hidden(i, u, 2 * KF, "up_product")
            for m in range(KD):
                dve.wait_ge(S("slab_done"), SLAB_AT["down3"] + 3 * (m + 1))
                sum_squares("ffnpost", m - 1)
                v.tensor_copy(mid_h[:, m, :], bank[m % 4][:, :]).then_inc(S("mid_h"), 1)
            norm_add("ffnpost", mid_h)


def _columns(v, n):
    return np.ascontiguousarray(np.asarray(v).reshape(n, P).T)


def _slabs(w, order=None):
    k, m = w.shape[0] // P, w.shape[1] // P
    return w.reshape(k, P, m, P).transpose(2, 1, 0, 3).reshape(m, P, k * P)


def _layout(inp):
    g = {k: np.asarray(v) for k, v in inp.items()}
    w = {k: v[0] for k, v in g.items() if k != "x" and k != "c_2"}

    def padded(a):
        out = np.zeros((a.shape[0], P, SLAB), np.float32)
        out[:, :, :a.shape[2]] = a
        return out

    def gate_up(a, b):
        return np.stack([_slabs(a), _slabs(b)], 1).reshape(2 * KF, P, SLAB)

    def down(a):
        s = _slabs(a)
        return np.concatenate([padded(s[:, :, P * k0:P * k1])[:, None] for k0, k1 in DOWN_CUT], 1).reshape(24, P, SLAB)

    win = w["w_in"]
    kr = win[:, 1920:1952]
    in1 = np.concatenate([win[:, 1536:1920], kr, kr, kr, kr, win[:, 0:1536]], 1)
    values = in1[:, 1536:].reshape(4, 2, P, T).transpose(0, 2, 1, 3).reshape(4, P, SLAB)
    uq = w["b_w_uq"].reshape(256, 8, 96)
    uq = np.concatenate([uq[:, :, :64].reshape(256, 512), uq[:, :, 64:].reshape(256, 256)], 1)
    uq = padded(_slabs(uq).reshape(2, 3, P, 2 * P).transpose(0, 2, 1, 3).reshape(2, P, 6 * P))
    ukv = w["b_w_ukv"].reshape(P, 8, 128)
    ukv = np.concatenate([ukv[:, :, :64].reshape(P, 512), ukv[:, :, 64:].reshape(P, 512)], 1)[None]
    w2 = w["w_in_2"]
    rw, zero = w2[:, 1024:], np.zeros((D, 96), np.float32)
    cols = [rw[:, 1536:1664], rw[:, 1664:1792], np.concatenate([rw[:, 1792:1824], zero], 1)]
    mu = w["rwkv_mu_2"]
    mus = [mu[1536:1664], mu[1664:1792], np.concatenate([mu[1792:1824], zero[0]])]
    for half in range(2):
        for i in range(3):
            a = 512 * i + 256 * half
            cols.append(rw[:, a:a + 256])
            mus.append(mu[a:a + 256])
    for j in range(4):
        cols += [w2[:, P * j:P * j + P], w2[:, 512 + P * j:512 + P * j + P]]
    slabs = np.concatenate([
        gate_up(w["ffn1_w_gate"], w["ffn1_w_up"]), down(w["ffn1_w_down"]), _slabs(in1[:, :1536]), values, uq, ukv, _slabs(w["w_out"]),
        gate_up(w["ffn2_w_gate"], w["ffn2_w_up"]), down(w["ffn2_w_down"]), _slabs(np.concatenate(cols, 1)),
        _slabs(w["w_out_2"]), gate_up(w["w_up_2"][:, :DFF], w["w_up_2"][:, DFF:]), down(w["w_down_2"]),
        np.zeros((N_LOADS - N_SLABS, P, SLAB), np.float32)])
    pair = lambda v, n: _columns(np.tile(v, n), 1)
    dw = w["ffn_dw_w_2"].reshape(3, 2, KF, P).transpose(3, 2, 1, 0).reshape(P, 6 * KF)
    db = w["ffn_dw_b_2"].reshape(2, KF, P).transpose(2, 1, 0).reshape(P, 2 * KF)
    v = {"ffn1_norm": _columns(w["ffn1_norm"], 8), "mix_norm": _columns(w["mix_norm"], 8),
         "a_q_norm": pair(w["a_q_norm"], 2), "a_k_norm": pair(w["a_k_norm"], 2),
         "b_q_lat_norm": _columns(w["b_q_lat_norm"], 2), "b_kv_lat_norm": _columns(w["b_kv_lat_norm"], 1),
         "b_q_nope_norm": pair(w["b_q_nope_norm"], 2), "b_q_rope_norm": pair(w["b_q_rope_norm"], 4),
         "b_k_nope_norm": pair(w["b_k_nope_norm"], 2), "b_k_rope_norm": pair(w["b_k_rope_norm"], 4),
         "ffn2_norm": _columns(w["ffn2_norm"], 8), "final_norm": _columns(w["final_norm"], 8),
         "ada_b": _columns(w["ada_b_2"], 48),
         "mix_pre_g": _columns(w["mix_pre_g_2"], 8), "mix_post_g": _columns(w["mix_post_g_2"], 8),
         "conv_w": w["conv_dw_w_2"].reshape(CONV_K, 4, P).transpose(2, 1, 0).reshape(P, 4 * CONV_K),
         "mu": _columns(np.concatenate(mus), 15), "ffn_dw_w": dw, "ffn_dw_b": db,
         "r_k": _columns(w["r_k_2"].reshape(-1), 4),
         "ffn_pre_g": _columns(w["ffn_pre_g_2"], 8), "ffn_post_g": _columns(w["ffn_post_g_2"], 8)}
    for k, name in (("conv_b", "conv_dw_b_2"), ("conv_ln_g", "conv_ln_g_2"), ("conv_ln_b", "conv_ln_b_2"), ("w0", "w0_2"),
                    ("a0", "a0_2"), ("k_k", "k_k_2"), ("k_a", "k_a_2"), ("lnx_g", "lnx_g_2"), ("lnx_b", "lnx_b_2")):
        v[k] = _columns(w[name], 4)
    p, c = np.arange(P)[:, None], np.arange(T)[None, :]
    rel = np.clip(384 + p - c, -128, 128) + 128
    relb = w["a_rel_bias"][:, rel]
    relb = np.where(((c >= 448) & (p < CH))[None], np.float32(-1e30), relb)
    both, block1, block2, rope = constants()
    lora = np.stack([np.concatenate([w["w2_2"], w["a2_2"]], 0), w["g2_2"][:P]], 1)
    arrays = {
        "x": g["x"][0].T.reshape(KD, P, T).transpose(1, 0, 2), "slabs": slabs,
        "ada": np.concatenate([w["ada_w_2"].T.reshape(48, P, SLAB), np.broadcast_to(g["c_2"][0], (1, P, SLAB))]), "vec": np.concatenate([v[k] for k, _ in VEC_COLS], 1),
        "both": both, "block1": block1, "block2": block2, "rope": rope, "relb": relb, "lora": lora,
        "g2b": w["g2_2"][P:]}
    return {k: np.ascontiguousarray(a) for k, a in arrays.items()}


def kernel(**inputs):
    import concourse.bacc as bacc
    from concourse.bass_utils import run_bass_kernel_spmd

    nc = bacc.Bacc("TRN2", target_bir_lowering=False, num_devices=1)
    arrays = {f"in_{k}": a for k, a in _layout(inputs).items()}
    args = [nc.dram_tensor(k, a.shape, mybir.dt.from_np(a.dtype), kind="ExternalInput").ap() for k, a in arrays.items()]
    y = nc.dram_tensor("out_y", (P, KD, T), F32, kind="ExternalOutput").ap()
    build(nc, *args, y)
    r = run_bass_kernel_spmd(nc, [arrays], core_ids=[0])
    got = r.results[0]["out_y"]
    return np.ascontiguousarray(got.transpose(1, 0, 2).reshape(D, T).T)[None]
```
